# Optimizing a Trainium2 kernel written in Bass

```python
import math
import jax, jax.numpy as jnp
from jax import lax
import numpy as np

D_MODEL = 1024
BATCH = 1
SEQ = 1024
DEPTH = 1

MEM_LEN = 256
D_MIX = D_MODEL
D_SSD = D_MIX // 2
SSD_HEAD_DIM = 64
SSD_HEADS = D_SSD // SSD_HEAD_DIM
SSD_GROUPS = 2
SSD_STATE = 128
CONV_WIDTH = 4
CHUNK = 128
D_XBC = D_SSD + 2 * SSD_GROUPS * SSD_STATE
D_DIFF = D_MIX - D_SSD
DIFF_HEAD_DIM = 64
DIFF_HEADS = D_DIFF // (2 * DIFF_HEAD_DIM)
Q_BLOCK = 128
ROPE_THETA = 10000.0
D_IN = D_SSD + D_XBC + SSD_HEADS + 3 * D_DIFF
MEM_HEADS = 4
MEM_HEAD_DIM = D_MODEL // MEM_HEADS
D_FF = 4 * D_MODEL
NORM_EPS = 1e-6

kernel_name = "hybrid_ssd_diffattn_memxattn_sqrelu"

def rms_norm(x, g, eps=NORM_EPS):
    xf = x.astype(jnp.float32)
    y = xf * lax.rsqrt(jnp.mean(xf * xf, axis=-1, keepdims=True) + eps)
    return (y * g.astype(jnp.float32)).astype(x.dtype)

def rope_tables(positions, dim):
    inv = ROPE_THETA ** (-jnp.arange(0, dim, 2, dtype=jnp.float32) / dim)
    ang = positions.astype(jnp.float32)[..., None] * inv
    ang = jnp.concatenate([ang, ang], axis=-1)
    return jnp.cos(ang), jnp.sin(ang)

def apply_rope(x, cos, sin):
    extra = x.ndim - 3
    shp = cos.shape[:2] + (1,) * extra + cos.shape[-1:]
    cos, sin = cos.reshape(shp), sin.reshape(shp)
    x1, x2 = jnp.split(x, 2, axis=-1)
    rot = jnp.concatenate([-x2, x1], axis=-1)
    return (x * cos + rot * sin).astype(x.dtype)

def ssd_chunked_scan(xs, dt, a, bm, cm):
    Bsz, L, H, P = xs.shape
    G, N = SSD_GROUPS, SSD_STATE
    R = H // G
    nc = L // CHUNK
    f32 = jnp.float32
    xdt = (xs.astype(f32) * dt[..., None]).reshape(Bsz, nc, CHUNK, G, R, P)
    da = (dt * a).reshape(Bsz, nc, CHUNK, G, R)
    bc = bm.astype(f32).reshape(Bsz, nc, CHUNK, G, N)
    cc = cm.astype(f32).reshape(Bsz, nc, CHUNK, G, N)
    cum = jnp.cumsum(da, axis=2)
    causal = jnp.tril(jnp.ones((CHUNK, CHUNK), dtype=bool))
    seg = cum[:, :, :, None] - cum[:, :, None, :]
    decay = jnp.exp(jnp.where(causal[None, None, :, :, None, None], seg, -jnp.inf))
    cb = jnp.einsum('bclgn,bcsgn->bclsg', cc, bc)
    y_diag = jnp.einsum('bclsg,bclsgr,bcsgrp->bclgrp', cb, decay, xdt)
    to_end = jnp.exp(cum[:, :, -1:] - cum)
    chunk_states = jnp.einsum('bclgn,bclgr,bclgrp->bcgrpn', bc, to_end, xdt)
    chunk_decay = jnp.exp(cum[:, :, -1])

    def carry_state(h, inp):
        s_c, d_c = inp
        return h * d_c[..., None, None] + s_c, h

    h0 = jnp.zeros((Bsz, G, R, P, N), f32)
    _, h_in = lax.scan(carry_state, h0,
                       (jnp.moveaxis(chunk_states, 1, 0), jnp.moveaxis(chunk_decay, 1, 0)))
    h_in = jnp.moveaxis(h_in, 0, 1)
    y_off = jnp.einsum('bclgn,bcgrpn,bclgr->bclgrp', cc, h_in, jnp.exp(cum))
    return (y_diag + y_off).reshape(Bsz, L, H, P).astype(xs.dtype)

def ssd_mixer(z, xbc, dt_raw, conv_w, conv_b, dt_bias, a_log, d_skip, norm_w):
    Bsz, L, _ = z.shape
    xbc = lax.conv_general_dilated(
        xbc, conv_w, window_strides=(1,), padding=[(CONV_WIDTH - 1, 0)],
        dimension_numbers=('NWC', 'WIO', 'NWC'), feature_group_count=D_XBC)
    xbc = jax.nn.silu(xbc + conv_b)
    xs, bm, cm = jnp.split(xbc, [D_SSD, D_SSD + SSD_GROUPS * SSD_STATE], axis=-1)
    xs = xs.reshape(Bsz, L, SSD_HEADS, SSD_HEAD_DIM)
    bm = bm.reshape(Bsz, L, SSD_GROUPS, SSD_STATE)
    cm = cm.reshape(Bsz, L, SSD_GROUPS, SSD_STATE)
    dt = jax.nn.softplus((dt_raw + dt_bias).astype(jnp.float32))
    a = -jnp.exp(a_log.astype(jnp.float32))
    y = ssd_chunked_scan(xs, dt, a, bm, cm)
    y = (y + d_skip[:, None] * xs).reshape(Bsz, L, D_SSD)
    return rms_norm(y * jax.nn.silu(z), norm_w)

def diff_attention(q, k, v, cos, sin, lam, subln_w, lambda_init):
    Bsz, L, _ = q.shape
    q = apply_rope(q.reshape(Bsz, L, DIFF_HEADS, 2, DIFF_HEAD_DIM), cos, sin)
    k = apply_rope(k.reshape(Bsz, L, DIFF_HEADS, 2, DIFF_HEAD_DIM), cos, sin)
    q = q.transpose(0, 2, 3, 1, 4)
    k = k.transpose(0, 2, 3, 1, 4)
    v = v.reshape(Bsz, L, DIFF_HEADS, 2 * DIFF_HEAD_DIM).transpose(0, 2, 1, 3)
    scale = DIFF_HEAD_DIM ** -0.5
    key_pos = jnp.arange(L)

    def block(i):
        start = i * Q_BLOCK
        qb = lax.dynamic_slice_in_dim(q, start, Q_BLOCK, axis=3)
        s = jnp.einsum('bhcqd,bhckd->bhcqk', qb, k,
                       preferred_element_type=jnp.float32) * scale
        causal = (start + jnp.arange(Q_BLOCK))[:, None] >= key_pos[None, :]
        s = jnp.where(causal, s, -jnp.inf)
        p = jax.nn.softmax(s, axis=-1)
        attn = p[:, :, 0] - lam * p[:, :, 1]
        return jnp.einsum('bhqk,bhkv->bhqv', attn.astype(v.dtype), v)

    o = lax.map(block, jnp.arange(L // Q_BLOCK))
    o = o.transpose(1, 0, 3, 2, 4).reshape(Bsz, L, DIFF_HEADS, 2 * DIFF_HEAD_DIM)
    o = rms_norm(o, subln_w) * (1.0 - lambda_init)
    return o.reshape(Bsz, L, D_DIFF)

def cross_attention(h, mem_h, wq, wk, wv, wo):
    Bsz, L, _ = h.shape
    M = mem_h.shape[1]
    q = (h @ wq).reshape(Bsz, L, MEM_HEADS, MEM_HEAD_DIM)
    k = (mem_h @ wk).reshape(Bsz, M, MEM_HEADS, MEM_HEAD_DIM)
    v = (mem_h @ wv).reshape(Bsz, M, MEM_HEADS, MEM_HEAD_DIM)
    s = jnp.einsum('bqhd,bkhd->bhqk', q, k,
                   preferred_element_type=jnp.float32) * (MEM_HEAD_DIM ** -0.5)
    p = jax.nn.softmax(s, axis=-1)
    o = jnp.einsum('bhqk,bkhd->bqhd', p.astype(v.dtype), v).reshape(Bsz, L, D_MODEL)
    return o @ wo

def setup_inputs(seed: int = 0) -> dict:
    key = jax.random.key(seed)
    ks = jax.random.split(key, 32)
    f32 = jnp.float32

    def nrm(k, shape, scale):
        return jax.random.normal(k, shape, f32) * scale

    def gain(k, dim):
        return 1.0 + nrm(k, (DEPTH, dim), 0.02)

    x = nrm(ks[0], (BATCH, SEQ, D_MODEL), 1.0)
    mem = nrm(ks[1], (BATCH, MEM_LEN, D_MODEL), 1.0)
    offset = jax.random.randint(ks[2], (BATCH, 1), 0, 1024, dtype=jnp.int32)
    positions = offset + jnp.arange(SEQ, dtype=jnp.int32)[None, :]
    dt0 = jnp.exp(jax.random.uniform(ks[3], (DEPTH, SSD_HEADS), f32,
                                     math.log(1e-3), math.log(1e-1)))
    dt_bias = dt0 + jnp.log(-jnp.expm1(-dt0))
    a_log = jnp.log(jax.random.uniform(ks[4], (DEPTH, SSD_HEADS), f32, 1.0, 16.0))
    return {
        "x": x,
        "mem": mem,
        "positions": positions,
        "norm_mix_pre": gain(ks[5], D_MODEL),
        "norm_mix_post": gain(ks[6], D_MODEL),
        "norm_mem_q": gain(ks[7], D_MODEL),
        "norm_mem_kv": gain(ks[8], D_MODEL),
        "norm_mem_post": gain(ks[9], D_MODEL),
        "norm_mlp_pre": gain(ks[10], D_MODEL),
        "norm_mlp_post": gain(ks[11], D_MODEL),
        "w_in": nrm(ks[12], (DEPTH, D_MODEL, D_IN), D_MODEL ** -0.5),
        "conv_w": nrm(ks[13], (DEPTH, CONV_WIDTH, 1, D_XBC), CONV_WIDTH ** -0.5),
        "conv_b": nrm(ks[14], (DEPTH, D_XBC), 0.02),
        "dt_bias": dt_bias,
        "a_log": a_log,
        "d_skip": 1.0 + nrm(ks[15], (DEPTH, SSD_HEADS), 0.1),
        "ssd_norm_w": gain(ks[16], D_SSD),
        "lambda_q1": nrm(ks[17], (DEPTH, DIFF_HEAD_DIM), 0.1),
        "lambda_k1": nrm(ks[18], (DEPTH, DIFF_HEAD_DIM), 0.1),
        "lambda_q2": nrm(ks[19], (DEPTH, DIFF_HEAD_DIM), 0.1),
        "lambda_k2": nrm(ks[20], (DEPTH, DIFF_HEAD_DIM), 0.1),
        "subln_w": gain(ks[21], 2 * DIFF_HEAD_DIM),
        "w_out": nrm(ks[22], (DEPTH, D_MIX, D_MODEL), D_MIX ** -0.5),
        "w_mq": nrm(ks[23], (DEPTH, D_MODEL, D_MODEL), D_MODEL ** -0.5),
        "w_mk": nrm(ks[24], (DEPTH, D_MODEL, D_MODEL), D_MODEL ** -0.5),
        "w_mv": nrm(ks[25], (DEPTH, D_MODEL, D_MODEL), D_MODEL ** -0.5),
        "w_mo": nrm(ks[26], (DEPTH, D_MODEL, D_MODEL), D_MODEL ** -0.5),
        "w_up": nrm(ks[27], (DEPTH, D_MODEL, D_FF), D_MODEL ** -0.5),
        "w_down": nrm(ks[28], (DEPTH, D_FF, D_MODEL), D_FF ** -0.5),
    }

def reference(x, mem, positions, norm_mix_pre, norm_mix_post, norm_mem_q, norm_mem_kv,
              norm_mem_post, norm_mlp_pre, norm_mlp_post, w_in, conv_w, conv_b, dt_bias,
              a_log, d_skip, ssd_norm_w, lambda_q1, lambda_k1, lambda_q2, lambda_k2,
              subln_w, w_out, w_mq, w_mk, w_mv, w_mo, w_up, w_down):
    cos, sin = rope_tables(positions, DIFF_HEAD_DIM)
    split_at = [D_SSD, D_SSD + D_XBC, D_SSD + D_XBC + SSD_HEADS,
                D_SSD + D_XBC + SSD_HEADS + D_DIFF,
                D_SSD + D_XBC + SSD_HEADS + 2 * D_DIFF]
    for l in range(DEPTH):
        lambda_init = 0.8 - 0.6 * math.exp(-0.3 * l)
        h = rms_norm(x, norm_mix_pre[l])
        z, xbc, dt_raw, q, k, v = jnp.split(h @ w_in[l], split_at, axis=-1)
        y_ssd = ssd_mixer(z, xbc, dt_raw, conv_w[l], conv_b[l], dt_bias[l], a_log[l],
                          d_skip[l], ssd_norm_w[l])
        lam = (jnp.exp(jnp.sum(lambda_q1[l].astype(jnp.float32) * lambda_k1[l]))
               - jnp.exp(jnp.sum(lambda_q2[l].astype(jnp.float32) * lambda_k2[l]))
               + lambda_init)
        y_diff = diff_attention(q, k, v, cos, sin, lam, subln_w[l], lambda_init)
        mixed = jnp.concatenate([y_ssd, y_diff], axis=-1) @ w_out[l]
        x = x + rms_norm(mixed, norm_mix_post[l])
        h = rms_norm(x, norm_mem_q[l])
        mem_h = rms_norm(mem, norm_mem_kv[l])
        c = cross_attention(h, mem_h, w_mq[l], w_mk[l], w_mv[l], w_mo[l])
        x = x + rms_norm(c, norm_mem_post[l])
        h = rms_norm(x, norm_mlp_pre[l])
        m = jnp.square(jax.nn.relu(h @ w_up[l])) @ w_down[l]
        x = x + rms_norm(m, norm_mlp_post[l])
    return x


_drawn_inputs = setup_inputs


def setup_inputs(seed=0):
    import zlib

    import numpy as np

    out = dict(_drawn_inputs(seed))
    spreads = {}
    factors = {'norm_mix_post': 3.719,
     'norm_mem_q': 4.745,
     'norm_mem_kv': 3.369,
     'norm_mem_post': 16.381,
     'norm_mlp_pre': 58.689,
     'norm_mlp_post': 80.791,
     'conv_b': 3.514,
     'd_skip': 3.306,
     'ssd_norm_w': 5.194,
     'lambda_k1': 4.727,
     'lambda_q2': 5.271,
     'lambda_k2': 7.813,
     'subln_w': 6.129}
    for name, (base, spread) in spreads.items():
        noise = np.random.default_rng([zlib.crc32(name.encode()), seed]).standard_normal(out[name].shape)
        drawn = base * np.exp(spread * noise) if base else spread * noise
        out[name] = __import__('jax').numpy.asarray(drawn.astype(out[name].dtype))
    for name, factor in factors.items():
        out[name] = (out[name] * factor).astype(out[name].dtype)
    return out
```

```python
import math
from contextlib import ExitStack

import concourse.bass as bass
import numpy as np
from concourse import mybir

F32 = mybir.dt.float32
F32R = mybir.dt.float32r
BF16 = mybir.dt.bfloat16
I32 = mybir.dt.int32
ALU = mybir.AluOpType
ACT = mybir.ActivationFunctionType
AX = mybir.AxisListType

P = 128
T = 1024
D = 1024
NT = T // P
KD = D // P
MEM = 256
MT = MEM // P
D_SSD = 512
XBC = 1024
SSD_H = 8
DH = 4
MH = 4
FF = 4096
EPS = 1e-6
LAMBDA_INIT = 0.8 - 0.6 * math.exp(-0.3 * 0)
THETA = 10000.0
HALF_DIM = 32
NEG = -1e30

UC = 256
UE = KD * UC
COL_Z, COL_XBC, COL_DT = 0, D_SSD, D_SSD + XBC
COL_Q = COL_DT + SSD_H
COL_K, COL_V = COL_Q + 512, COL_Q + 1024

TWO_PI_A = 6.28125
TWO_PI_B = 0.0019350051879882812
TWO_PI_C = 3.0199159795074593e-07
ROUND = 1.5 * 2.0 ** 23
PI_SAFE = 3.1415925

PROJ = [("dt", 1, 0), ("xbc", 4, 4), ("v", 8, 2), ("q", 8, 2), ("k", 8, 2), ("z", 8, 2),
        ("mk", 2, 4), ("mv", 2, 4), ("wo", 8, 4), ("mq", 4, 4), ("mo", 8, 4)]


def proj_tables():
    first, unit, steps, u = {}, {}, [], 0
    for name, per, n in PROJ:
        first[name], unit[name] = len(steps), u
        steps += [(name, s) for s in range(per * max(n, 1))]
        u += n
    return first, unit, steps, u


STEP0, UNIT0, STEPS, N_UNITS = proj_tables()
PER_UNIT = {name: per for name, per, _ in PROJ}

TR_IN, TR_MIX, TR_MEM, TR_Q, TR_MLP = 0, 8, 16, 18, 26

POWS = ([("in", i) for i in range(NT)] + [("y", i) for i in range(NT)] + [("o", i) for i in range(NT)]
        + [("mem", i) for i in range(MT)])
for _a, _b in (("wo", "q"), ("mo", "mlp")):
    for _t in range(NT + 1):
        POWS += [(_a, _t)] * (_t < NT) + [(_b, _t - 1)] * (_t > 0)
POWS += [("down", i) for i in range(NT)]
POW = {what: n for n, what in enumerate(POWS)}
COL = {}
for _what in POWS:
    COL[_what] = sum(DH if x[0] == "o" else 1 for x in COL)
N_COLS = len(POWS) + NT * (DH - 1)


def build(nc, t, out):
    ctx = ExitStack()
    with ctx:
        base = (nc.sbuf_base + 63) // 64 * 64
        place = {}
        size = {"OPH": 32768, "OPL": 32768, "WH": 16384, "WL": 16384, "RAW": 8192, "X": 32768,
                "Q": 16384, "K": 16384, "V": 16384, "TMP": 16384, "GA": 4096, "GB": 4096, "MISC": 8192}
        for region, n in size.items():
            place[region] = base
            base += n
        rest = [base]

        def at(name, region, offset, shape, dt=F32):
            return nc.alloc_sbuf_tensor_at(name, shape, dt, offset=place[region] + offset)

        def small(name, shape, dt=F32):
            n = 4 if dt in (F32, F32R, I32) else 2
            for s in shape[1:]:
                n *= s
            r = nc.alloc_sbuf_tensor_at(name, shape, dt, offset=rest[0])
            rest[0] += (n + 31) // 32 * 32
            return r

        def sem(name):
            return ctx.enter_context(nc.semaphore(name))

        oph = at("oph", "OPH", 0, [P, KD, T], F32R)
        opl = at("opl", "OPL", 0, [P, KD, T], F32R)
        wh = at("wh", "WH", 0, [P, 2, UE], F32R)
        wl = at("wl", "WL", 0, [P, 2, UE], F32R)
        raw = at("raw", "RAW", 0, [P, 2, UE // 2])
        mix = at("mix", "X", 0, [P, KD, T])
        resid = at("resid", "X", 0, [P, NT, D])
        x_in = at("x_in", "V", 0, [P, 2, D])
        h_in = at("h_in", "V", 8192, [P, 2, D])
        xpre = at("xpre", "Q", 0, [P, 2, T + 4])
        rope_t = at("rope_t", "K", 0, [P, 4, NT, HALF_DIM])
        xdt = at("xdt", "K", 0, [P, 512])
        xdt_end = at("xdt_end", "K", 2048, [P, 512])
        x_skip = at("x_skip", "K", 4096, [P, 512])
        b_cb = at("b_cb", "K", 6144, [P, 4, P])
        decay = at("decay", "K", 8192, [P, SSD_H, P])
        cb_decay = at("cb_decay", "K", 12288, [P, SSD_H, P])
        state = at("state", "TMP", 0, [P, 512])
        y_off = at("y_off", "TMP", 2048, [P, 512])
        roped = at("roped", "TMP", 4096, [P, 2, UC])
        rope_b = at("rope_b", "TMP", 6144, [P, UC])
        silu_z = at("silu_z", "TMP", 7168, [P, 2, UC])
        junk = at("junk", "TMP", 9216, [P, D])
        qt = at("qt", "Q", 0, [P, DH, T])
        kt = at("kt", "K", 0, [P, DH, T])
        vt = at("vt", "V", 0, [P, NT, 512])
        probs = at("probs", "OPH", 0, [P, 2, 2, T])
        probs_t = at("probs_t", "OPH", 16384, [P, 2, NT, P])
        memh = at("memh", "Q", 0, [P, KD, MEM], F32R)
        meml = at("meml", "Q", 8192, [P, KD, MEM], F32R)
        m_in = at("m_in", "K", 0, [P, 2, D])
        h_mem = at("h_mem", "K", 8192, [P, 2, D])
        kmt = at("kmt", "V", 0, [P, KD, MEM])
        vm = at("vm", "V", 8192, [P, MT, D])
        proj_out = at("proj_out", "Q", 0, [P, NT, D])
        qct = at("qct", "Q", 0, [P, KD, T])
        h_tok = at("h_tok", "TMP", 0, [P, 2, D])
        mprobs = at("mprobs", "TMP", 0, [P, 2, MH, MEM])
        mprobs_t = at("mprobs_t", "TMP", 8192, [P, 2, MH * MT, P])
        uh = at("uh", "V", 0, [P, 2, 2, T], F32R)
        ul = at("ul", "TMP", 0, [P, 2, 2, T], F32R)
        relu_u = at("relu_u", "MISC", 0, [P, 2, 512])
        sq_u = at("sq_u", "MISC", 4096, [P, 2, 512])
        junk2 = at("junk2", "MISC", 0, [P, D])
        cos_t = at("cos_t", "MISC", 0, [P, NT, HALF_DIM])
        sin_t = at("sin_t", "MISC", 1024, [P, NT, HALF_DIM])
        nsin_t = at("nsin_t", "MISC", 2048, [P, NT, HALF_DIM])
        dts = [at(f"dts{n}", "MISC", 3072 + 256 * n, [P, NT, SSD_H]) for n in range(9)]
        ssd_w = at("ssd_w", "MISC", 5376, [P, 512])
        gain_a = at("gain_a", "GA", 0, [P, D])
        gain_b = at("gain_b", "GB", 0, [P, D])

        ident = small("ident", [P, P])
        tri = small("tri", [P, P])
        ones = small("ones", [P, P])
        ident_b = small("ident_b", [P, P], BF16)
        mask_q = small("mask_q", [P, P], BF16)
        mask_s = small("mask_s", [P, 4, P], BF16)
        inv = small("inv", [P, HALF_DIM])
        pos_i = small("pos_i", [P, NT], I32)
        conv_w = small("conv_w_sb", [P, KD, 4])
        conv_b = small("conv_b_sb", [P, KD])
        wdt = at("wdt", "MISC", 7424, [P, KD, SSD_H])
        wdt_h = at("wdt_h", "MISC", 7680, [P, KD, SSD_H], F32R)
        wdt_l = at("wdt_l", "MISC", 7936, [P, KD, SSD_H], F32R)
        heads8 = small("heads8", [P, 3, SSD_H])
        lam4 = small("lam4", [P, 4, 64])
        lam = small("lam", [P, 8])
        sub_w = small("sub_w", [P, P])
        stat = small("stat", [P, N_COLS])
        rms = small("rms", [P, N_COLS])
        mhalf = small("mhalf", [P, 4])
        half_pi = small("half_pi", [P, 1])
        nmax = small("nmax", [P, 2, 2])
        sums = small("sums", [P, 4, 2])
        recs = small("recs", [P, 4, 2])
        ratio = small("ratio", [P, 2])
        mmax = small("mmax", [P, 2, MH])
        msum = small("msum", [P, 2, MH])
        mrec = small("mrec", [P, 2, MH])
        assert rest[0] <= nc.sbuf_usable_end, (rest[0], nc.sbuf_usable_end)
        ps = ctx.enter_context(nc.psum_tensor("ps", [P, 8, 512], F32))

        x_loaded = [sem(f"x_loaded{n}") for n in range(2)]
        small_loaded = sem("small_loaded")
        gain_a_loaded, gain_b_loaded = sem("gain_a_loaded"), sem("gain_b_loaded")
        raw_loaded = [sem(f"raw_loaded{n}") for n in range(2)]
        w_hi, w_lo = sem("w_hi"), sem("w_lo")
        pool_c = sem("pool_c")
        consts_ready = sem("consts_ready")
        sq_done, ms_ready, rms_ready = sem("sq_done"), sem("ms_ready"), sem("rms_ready")
        h_ready = sem("h_ready")
        tr_done, hi_done, lo_done = sem("tr_done"), sem("hi_done"), sem("lo_done")
        pj_done = sem("pj_done")
        ev = {name: sem(f"ev_{name}") for name, _, _ in PROJ}
        dv = sem("dv")
        av = sem("av")
        rope_r, rope_abs, rope_sin = sem("rope_r"), sem("rope_abs"), sem("rope_sin")
        conv_done, silu_done = sem("conv_done"), sem("silu_done")
        wdt_hi, wdt_lo = sem("wdt_hi"), sem("wdt_lo")
        dt_v, dt_s = sem("dt_v"), sem("dt_s")
        da_ready, cum_done = sem("da_ready"), sem("cum_done")
        ssd_a, ssd_b = sem("ssd_a"), sem("ssd_b")
        ssd_x, ssd_bcb, ssd_seg, ssd_exp, ssd_m = (sem(n) for n in ("ssd_x", "ssd_bcb", "ssd_seg", "ssd_exp", "ssd_m"))
        ssd_h, ssd_y = sem("ssd_h"), sem("ssd_y")
        rope_done, rt_done, rt_ev = sem("rope_done"), sem("rt_done"), sem("rt_ev")
        gate_done, lam_s = sem("gate_done"), sem("lam_s")
        s_done = [sem(f"s_done{c}") for c in range(2)]
        mx_done = [sem(f"mx_done{c}") for c in range(2)]
        ex_done = [sem(f"ex_done{c}") for c in range(2)]
        comb_done, pt_done, pt_ev, pv_done, o_ev = (sem(n) for n in ("comb_done", "pt_done", "pt_ev", "pv_done", "o_ev"))
        resid_loaded = sem("resid_loaded")
        resid_done = sem("resid_done")
        ms_done, mmx_done, mex_done, mn_done = sem("ms_done"), sem("mmx_done"), sem("mex_done"), sem("mn_done")
        mt_done, mt_ev, mo_done, mo_hi, mo_lo = (sem(n) for n in ("mt_done", "mt_ev", "mo_done", "mo_hi", "mo_lo"))
        up_done, relu_done, sqv_done, sqh_done, ul_done = (
            sem(n) for n in ("up_done", "relu_done", "sqv_done", "sqh_done", "ul_done"))
        down_done, acc_done = sem("down_done"), sem("acc_done")
        stored = sem("stored")

        w_in = t["w_in"][0]
        cols = {"xbc": (w_in, COL_XBC), "v": (w_in, COL_V), "q": (w_in, COL_Q), "k": (w_in, COL_K),
                "z": (w_in, COL_Z), "mk": (t["w_mk"][0], 0), "mv": (t["w_mv"][0], 0),
                "wo": (t["w_out"][0], 0), "mq": (t["w_mq"][0], 0), "mo": (t["w_mo"][0], 0)}
        w_up, w_down = t["w_up"][0], t["w_down"][0]
        HALVES0 = 2 * N_UNITS
        NJ = FF // UC
        N_SMALL = 16 * 14

        def pow_cols(what, w=1):
            return stat[:, COL[what]:COL[what] + w], rms[:, COL[what]:COL[what] + w]

        def unit_source(name, u, half):
            w, c0 = cols[name]
            return w[half * 512:(half + 1) * 512, c0 + u * UC:c0 + (u + 1) * UC].rearrange("(k p) c -> p k c", p=P)

        def bank_free(eng, g):
            if g >= 3:
                name, s = STEPS[g - 3]
                eng.wait_ge(ev[name], s + 1)

        def split_at(name, s):
            per = PER_UNIT[name]
            u = UNIT0[name] + s // per
            r = s % per
            halves = []
            for half, when in ((0, 0), (1, per // 2)):
                if r == when:
                    halves.append(2 * (u + 1) + half)
            return [q for q in halves if u >= 1 and q < HALVES0 + 4]

        def unit_end(u):
            if u >= N_UNITS:
                m = u - N_UNITS
                if m == 0 or (m % 2 and m < 2 * NJ - 1):
                    return up_done, 4 * ((m + 1) // 2 + 1)
                return down_done, 16 * ((m - 2) // 2 + 1)
            name = [x for x, _, n in PROJ if n and UNIT0[x] <= u][-1]
            return pj_done, STEP0[name] + (u - UNIT0[name] + 1) * PER_UNIT[name]

        block = ctx.enter_context(nc.Block())

        @block.sync
        def _(sp):
            def load_half(q, src):
                if q >= 2:
                    sp.wait_ge(w_lo, q - 1)
                sp.dma_start(raw[:, q % 2, :], src).then_inc(raw_loaded[q % 2], 16)

            def x_tile(i):
                if i >= 2:
                    sp.wait_ge(h_ready, i - 1)
                sp.dma_start(x_in[:, i % 2, :], t["x"][0][i * P:(i + 1) * P, :]).then_inc(x_loaded[i % 2], 16)

            x_tile(0)
            x_tile(1)
            q = 0
            for name, _, units in PROJ[1:]:
                for u in range(units):
                    for half in range(2):
                        if 0 < q < 4:
                            x_tile(2 * q)
                            x_tile(2 * q + 1)
                        src = unit_source(name, u, half)
                        load_half(q, src)
                        q += 1
            for half in range(2):
                load_half(q, w_up[half * 512:(half + 1) * 512, 0:UC].rearrange("(k p) c -> p k c", p=P))
                q += 1
            with sp.Fori(0, NJ - 1) as j:
                for half in range(2):
                    sp.wait_ge(w_lo, j * 4 + (HALVES0 + 2 + half - 1))
                    sp.dma_start(raw[:, half, :], w_up[half * 512:(half + 1) * 512, bass.ts(j + 1, UC)]
                                 .rearrange("(k p) c -> p k c", p=P)).then_inc(raw_loaded[half], 16)
                for half in range(2):
                    sp.wait_ge(w_lo, j * 4 + (HALVES0 + 4 + half - 1))
                    sp.dma_start(raw[:, half, :], w_down[bass.ts(j * 2 + half, P), :]).then_inc(raw_loaded[half], 16)
            q += 4 * (NJ - 1)
            for half in range(2):
                load_half(q, w_down[(2 * (NJ - 1) + half) * P:(2 * (NJ - 1) + half + 1) * P, :])
                q += 1
            for i in range(NT):
                sp.wait_ge(resid_done, 2 * NT + i + 1)
                sp.dma_start(out[0][i * P:(i + 1) * P, :], resid[:, i, :]).then_inc(stored, 16)
            sp.wait_ge(stored, 16 * NT)

        @block.gpsimd
        def _(pool):
            g = nc.gpsimd
            g.memset(ident[:], 0.0).then_inc(pool_c, 1)
            g.memset(ident_b[:], 0.0).then_inc(pool_c, 1)
            g.memset(tri[:], 1.0).then_inc(pool_c, 1)
            g.memset(mask_q[:], 0.0).then_inc(pool_c, 1)
            g.memset(mask_s[:], 0.0).then_inc(pool_c, 1)
            g.memset(ones[:], 1.0).then_inc(consts_ready, 1)
            g.memset(mhalf[:], -0.5).then_inc(pool_c, 1)
            pool.wait_ge(pool_c, 6)
            for m in (ident, ident_b):
                g.affine_select(out=m[:], in_=m[:], compare_op=ALU.not_equal, fill=1.0, base=0,
                                pattern=[[-1, P]], channel_multiplier=1).then_inc(consts_ready, 1)
            g.affine_select(out=tri[:], in_=tri[:], compare_op=ALU.is_ge, fill=0.0, base=0,
                            pattern=[[1, P]], channel_multiplier=-1).then_inc(consts_ready, 1)
            g.affine_select(out=mask_q[:], in_=mask_q[:], compare_op=ALU.is_ge, fill=NEG, base=0,
                            pattern=[[-1, P]], channel_multiplier=1).then_inc(consts_ready, 1)
            g.affine_select(out=mask_s[:], in_=mask_s[:], compare_op=ALU.is_ge, fill=NEG, base=0,
                            pattern=[[0, 4], [1, P]], channel_multiplier=-1).then_inc(consts_ready, 1)

            def pow_step(what):
                w = 4 if what[0] == "o" else 1
                pool.wait_ge(ms_ready, POW[what] + 1)
                src, dst = pow_cols(what, w)
                g.tensor_tensor(dst, src, mhalf[:, 0:w], ALU.pow).then_inc(rms_ready, 1)

            for what in POWS[:1]:
                pow_step(what)
            for i in range(HALF_DIM):
                g.memset(inv[:, i:i + 1], float(np.float32(THETA) ** np.float32(-i / HALF_DIM))).then_inc(consts_ready, 1)
            g.memset(half_pi[:], math.pi / 2).then_inc(consts_ready, 1)
            for b in range(2):
                g.memset(xpre[:, b, 0:3], 0.0).then_inc(consts_ready, 1)
            for what in POWS[1:]:
                pow_step(what)

        ALL_CONSTS = 6 + HALF_DIM + 3

        @block.scalar
        def _(act):
            s = nc.scalar
            n_av = [0]

            def after(ins):
                n_av[0] += 1
                ins.then_inc(av, 1)
                act.wait_ge(av, n_av[0])

            def slot_free(u):
                if u >= 2:
                    sem_of, n = unit_end(u - 2)
                    act.wait_ge(sem_of, n)

            def split_hi(q):
                act.wait_ge(raw_loaded[q % 2], 16 * (q // 2 + 1))
                slot_free(q // 2)
                s.activation(wh[:, (q // 2) % 2, (q % 2) * 1024:(q % 2 + 1) * 1024], raw[:, q % 2, :],
                             ACT.Copy).then_inc(w_hi, 1)

            def square(what, src, dst, scale=1.0):
                n = sum(1 for x in POWS[:POW[what]] if x[0] != "o")
                if n:
                    act.wait_ge(sq_done, n)
                s.activation(dst, src, ACT.Square, scale=scale, accum_out=stat[:, COL[what]:COL[what] + 1]).then_inc(sq_done, 1)

            def tr_hi(n, dst):
                for b in range(2):
                    act.wait_ge(tr_done, 2 * n + b + 1)
                    s.activation(dst[:, 4 * b:4 * b + 4], ps[:, 4 + 2 * (n % 2) + b, :].rearrange("p (k c) -> p k c", k=4),
                                 ACT.Copy).then_inc(hi_done, 1)

            rows = lambda a: a.partition_broadcast(P)
            act.dma_start(gain_b[:], rows(t["norm_mix_pre"][0:1, :])).then_inc(gain_b_loaded, 16)
            act.dma_start(pos_i[:], t["positions"][0].rearrange("(i p) -> p i", p=P),
                          allow_slow_non_contiguous=True).then_inc(small_loaded, 16)
            act.dma_start(wdt[:], w_in[:, COL_DT:COL_DT + SSD_H].rearrange("(k p) c -> p k c", p=P),
                          allow_slow_non_contiguous=True).then_inc(small_loaded, 16)
            for w in range(4):
                act.dma_start(conv_w[:, :, w], t["conv_w"][0, w, 0].rearrange("(m p) -> p m", p=P),
                          allow_slow_non_contiguous=True).then_inc(small_loaded, 16)
            act.dma_start(conv_b[:], t["conv_b"][0].rearrange("(m p) -> p m", p=P),
                          allow_slow_non_contiguous=True).then_inc(small_loaded, 16)
            for n, name in enumerate(("dt_bias", "a_log", "d_skip")):
                act.dma_start(heads8[:, n, :], rows(t[name][0:1, :])).then_inc(small_loaded, 16)
            for n, name in enumerate(("lambda_q1", "lambda_q2", "lambda_k1", "lambda_k2")):
                act.dma_start(lam4[:, n, :], rows(t[name][0:1, :])).then_inc(small_loaded, 16)
            act.dma_start(ssd_w[:], rows(t["ssd_norm_w"][0:1, :])).then_inc(gain_a_loaded, 16)
            act.dma_start(sub_w[:], rows(t["subln_w"][0:1, :])).then_inc(gain_a_loaded, 16)

            for i in range(NT + 2):
                if i < NT:
                    act.wait_ge(x_loaded[i % 2], 16 * (i // 2 + 1))
                    square(("in", i), x_in[:, i % 2, :], junk[:])
                if i >= 2:
                    tr_hi(TR_IN + i - 2, oph[:, :, (i - 2) * P:(i - 1) * P])
                if i in (3, 5, 7, 9):
                    split_hi((i - 3) // 2)
            act.wait_ge(small_loaded, N_SMALL)
            s.activation(wdt_h[:], wdt[:], ACT.Copy).then_inc(wdt_hi, 1)

            act.wait_ge(rope_r, 1)
            act.wait_ge(consts_ready, ALL_CONSTS)
            s.activation(sin_t[:], rope_t[:, 0], ACT.Sin).then_inc(rope_sin, 1)
            s.activation(nsin_t[:], rope_t[:, 0], ACT.Sin, scale=-1.0).then_inc(rope_sin, 1)
            after(s.activation(rope_t[:, 1], rope_t[:, 0], ACT.Abs))
            s.activation(cos_t[:], rope_t[:, 1], ACT.Sin, scale=-1.0, bias=half_pi[:]).then_inc(rope_sin, 1)

            def silu(m):
                act.wait_ge(conv_done, m + 1)
                s.activation(mix[:, m, :], mix[:, m, :], ACT.Silu).then_inc(silu_done, 1)

            for st in range(16):
                m, half = st // 2, st % 2
                g = STEP0["xbc"] + st
                act.wait_ge(pj_done, g + 1)
                if m >= 2:
                    act.wait_ge(conv_done, m - 1)
                s.activation(xpre[:, m % 2, 3 + half * 512:3 + (half + 1) * 512], ps[:, g % 3, :],
                             ACT.Copy).then_inc(ev["xbc"], 1)
                for q in split_at("xbc", st):
                    split_hi(q)
                if half and m >= 1:
                    silu(m - 1)
            silu(7)

            act.wait_ge(dt_v, 1)
            after(s.activation(dts[1][:], dts[0][:], ACT.Abs))
            s.activation(dts[2][:], dts[1][:], ACT.Exp, scale=-1.0).then_inc(dt_s, 1)
            act.wait_ge(dt_v, 2)
            s.activation(dts[4][:], dts[3][:], ACT.Ln).then_inc(dt_s, 1)
            s.activation(heads8[:, 1, :], heads8[:, 1, :], ACT.Exp).then_inc(dt_s, 1)
            act.wait_ge(lam_s, 1)
            s.activation(lam[:, 2:4], lam[:, 0:2], ACT.Exp).then_inc(dt_s, 1)
            act.wait_ge(dt_v, 3)
            s.activation(dts[4][:], dts[5][:], ACT.Exp).then_inc(dt_s, 1)
            s.activation(dts[7][:], dts[6][:], ACT.Exp).then_inc(dt_s, 1)
            s.activation(dts[8][:], dts[2][:], ACT.Exp).then_inc(dt_s, 1)

            def ssd_act(c):
                act.wait_ge(ssd_a, c + 1)
                if c:
                    act.wait_ge(ssd_m, c)
                    act.wait_ge(ssd_b, c)
                s.activation(b_cb[:], ps[:, 5, :].rearrange("p (k c) -> p k c", k=4), ACT.Copy).then_inc(ssd_bcb, 1)
                act.wait_ge(ssd_seg, c + 1)
                s.activation(decay[:], decay[:], ACT.Exp).then_inc(ssd_exp, 1)

            def rope_evac(st, name):
                dst, base_n = (qt, 0) if name == "q" else (kt, 16)
                u, i = st // NT, st % NT
                act.wait_ge(rt_done, base_n + st + 1)
                if name == "k" and st == 0:
                    act.wait_ge(ssd_y, NT)
                    act.wait_ge(ssd_b, NT)
                s.activation(dst[:, 2 * u:2 * u + 2, i * P:(i + 1) * P],
                             ps[:, 3, 0:UC].rearrange("p (k c) -> p k c", k=2), ACT.Copy,
                             scale=0.125 if name == "q" else 1.0).then_inc(rt_ev, 1)

            for n in range(66):
                name, st = STEPS[STEP0["v"] + n] if n < 64 else (None, 0)
                g = STEP0["v"] + n
                if name == "v":
                    u, i = st // NT, st % NT
                    act.wait_ge(pj_done, g + 1)
                    s.activation(vt[:, i, u * UC:(u + 1) * UC], ps[:, g % 3, 0:UC], ACT.Copy).then_inc(ev["v"], 1)
                if name == "z":
                    act.wait_ge(pj_done, g + 1)
                    if st >= 2:
                        act.wait_ge(gate_done, st - 1)
                    s.activation(silu_z[:, st % 2, :], ps[:, g % 3, 0:UC], ACT.Silu).then_inc(ev["z"], 1)
                if name:
                    for q in split_at(name, st):
                        split_hi(q)
                if n < 32 and n % 4 == 1:
                    ssd_act(n // 4)
                if 16 <= n - 2 < 48:
                    rope_evac((n - 18) % 16, "q" if n - 2 < 32 else "k")
            for i in range(NT):
                act.wait_ge(gate_done, NT + i + 1)
                square(("y", i), mix[:, 0:4, i * P:(i + 1) * P], junk[:, 0:512].rearrange("p (k c) -> p k c", k=4))

            steps = [(i, h) for i in range(NT) for h in range(DH)]
            NS = len(steps)

            def attn_exp(n, c):
                keys = (steps[n][0] + 1) * P
                act.wait_ge(mx_done[c], n + 1)
                if n >= 2:
                    act.wait_ge(comb_done, n - 1) if c else act.wait_ge(pt_done, n - 1)
                src = ps[:, 2 * c:2 * c + 2, :].rearrange("p b k -> p (b k)")
                s.activation(probs[:, n % 2, c, 0:keys], src[:, 0:keys], ACT.Exp, bias=nmax[:, n % 2, c:c + 1],
                             accum_out=sums[:, n % 4, c:c + 1]).then_inc(ex_done[c], 1)

            act.wait_ge(pj_done, STEP0["z"] + 16)
            for n in range(NS + 3):
                if n < NS:
                    attn_exp(n, 0)
                    attn_exp(n, 1)
                if n >= 1 and n - 1 < NS:
                    k = n - 1
                    i = steps[k][0]
                    act.wait_ge(pt_done, k + 1)
                    if k >= 2:
                        act.wait_ge(pv_done, k - 1)
                    src = ps[:, 4:6, :].rearrange("p b k -> p (b k)")
                    s.activation(probs_t[:, k % 2, 0:i + 1, :].rearrange("p b k -> p (b k)"), src[:, 0:(i + 1) * P],
                                 ACT.Copy).then_inc(pt_ev, 1)
                if n >= 2 and n - 2 < NS:
                    k = n - 2
                    i, h = steps[k]
                    act.wait_ge(pv_done, k + 1)
                    o = ps[:, 6 + k % 2, 0:P]
                    s.activation(mix[:, 4 + h, i * P:(i + 1) * P], o, ACT.Copy, scale=recs[:, k % 4, 0:1])
                    if k >= 4:
                        act.wait_ge(o_ev, k - 3)
                    elif k == 0:
                        act.wait_ge(sq_done, 2 * NT)
                    s.activation(junk[:, (k % 4) * P:(k % 4 + 1) * P], o, ACT.Square, scale=recs[:, k % 4, 0:1],
                                 accum_out=stat[:, COL[("o", i)] + h:COL[("o", i)] + h + 1]).then_inc(o_ev, 1)

            for i in range(NT):
                tr_hi(TR_MIX + i, oph[:, :, i * P:(i + 1) * P])
            act.wait_ge(tr_done, 2 * (TR_MIX + NT))
            for i in range(NT):
                act.dma_start(resid[:, i, :], t["x"][0][i * P:(i + 1) * P, :]).then_inc(resid_loaded, 16)
            for i in range(MT):
                act.dma_start(m_in[:, i, :], t["mem"][0][i * P:(i + 1) * P, :]).then_inc(x_loaded[i], 16)
            act.wait_ge(h_ready, TR_MIX)
            act.dma_start(gain_b[:], rows(t["norm_mem_kv"][0:1, :])).then_inc(gain_b_loaded, 16)
            act.dma_start(gain_a[:], rows(t["norm_mix_post"][0:1, :])).then_inc(gain_a_loaded, 16)
            for i in range(MT):
                act.wait_ge(x_loaded[i], 16 * 5)
                act.wait_ge(o_ev, NS)
                square(("mem", i), m_in[:, i, :], junk[:])
            for i in range(MT):
                tr_hi(TR_MEM + i, memh[:, :, i * P:(i + 1) * P])
            act.wait_ge(h_ready, TR_MEM + MT)
            act.dma_start(gain_b[:], rows(t["norm_mem_q"][0:1, :])).then_inc(gain_b_loaded, 16)

            for st in range(8):
                g = STEP0["mk"] + st
                act.wait_ge(pj_done, g + 1)
                s.activation(kmt[:, st, :], ps[:, g % 3, 0:MEM], ACT.Copy).then_inc(ev["mk"], 1)
                for q in split_at("mk", st):
                    split_hi(q)
            for st in range(8):
                u, i = st // MT, st % MT
                g = STEP0["mv"] + st
                act.wait_ge(pj_done, g + 1)
                s.activation(vm[:, i, u * UC:(u + 1) * UC], ps[:, g % 3, 0:UC], ACT.Copy).then_inc(ev["mv"], 1)
                for q in split_at("mv", st):
                    split_hi(q)

            def post_block(name, nxt, tr0, ready):
                for k in range(NT + 4):
                    if k < NT:
                        ready(k)
                        square((name, k), proj_out[:, k, :], junk[:])
                    if 1 <= k <= NT:
                        act.wait_ge(resid_done, (0 if name == "wo" else NT) + k)
                        square((nxt, k - 1), resid[:, k - 1, :], junk[:])
                    if k >= 4:
                        tr_hi(tr0 + k - 4, oph[:, :, (k - 4) * P:(k - 3) * P])

            def out_proj(name, nxt, tr0):
                def evac(st):
                    u, i = st // NT, st % NT
                    g = STEP0[name] + st
                    act.wait_ge(pj_done, g + 1)
                    s.activation(proj_out[:, i, u * UC:(u + 1) * UC], ps[:, g % 3, 0:UC], ACT.Copy).then_inc(ev[name], 1)
                    for q in split_at(name, st):
                        split_hi(q)

                for st in range(3 * NT):
                    evac(st)

                def ready(k):
                    evac(3 * NT + k)
                    act.wait_ge(ev[name], 3 * NT + k + 1)

                post_block(name, nxt, tr0, ready)

            out_proj("wo", "q", TR_Q)
            act.wait_ge(h_ready, TR_Q + NT)
            act.dma_start(gain_a[:], rows(t["norm_mem_post"][0:1, :])).then_inc(gain_a_loaded, 16)
            act.dma_start(gain_b[:], rows(t["norm_mlp_pre"][0:1, :])).then_inc(gain_b_loaded, 16)

            for st in range(16):
                f, half = st // 2, st % 2
                g = STEP0["mq"] + st
                act.wait_ge(pj_done, g + 1)
                s.activation(qct[:, f, half * 512:(half + 1) * 512], ps[:, g % 3, :], ACT.Copy,
                             scale=0.0625).then_inc(ev["mq"], 1)
                for q in split_at("mq", st):
                    split_hi(q)

            for n in range(NT + 2):
                if n < NT:
                    act.wait_ge(mmx_done, n + 1)
                    if n >= 2:
                        act.wait_ge(mt_done, n - 1)
                    src = ps[:, 2 * (n % 2):2 * (n % 2) + 2, :].rearrange("p b (h m) -> p (b h) m", h=2)
                    for h in range(MH):
                        ins = s.activation(mprobs[:, n % 2, h, :], src[:, h, :], ACT.Exp, bias=mmax[:, n % 2, h:h + 1],
                                           accum_out=msum[:, n % 2, h:h + 1])
                    ins.then_inc(mex_done, 1)
                if 1 <= n <= NT:
                    k = n - 1
                    act.wait_ge(mt_done, k + 1)
                    if k >= 2:
                        act.wait_ge(mo_done, k - 1)
                    s.activation(mprobs_t[:, k % 2], ps[:, 4:6, :].rearrange("p b (h m) -> p (b h) m", h=4),
                                 ACT.Copy).then_inc(mt_ev, 1)
                if n >= 2:
                    k = n - 2
                    act.wait_ge(mo_done, k + 1)
                    s.activation(oph[:, :, k * P:(k + 1) * P], ps[:, 6:8, :].rearrange("p b (h m) -> p (b h) m", h=4),
                                 ACT.Copy).then_inc(mo_hi, 1)

            out_proj("mo", "mlp", TR_MLP)
            act.wait_ge(h_ready, TR_MLP + NT)
            act.dma_start(gain_a[:], rows(t["norm_mlp_post"][0:1, :])).then_inc(gain_a_loaded, 16)

            def relu_sq(done, sq_free, st, par):
                f, half = st // 2, st % 2
                act.wait_ge(up_done, done)
                if sq_free is not None:
                    act.wait_ge(sqv_done, sq_free)
                s.activation(relu_u[:, st % 2, :], ps[:, st, :], ACT.Relu).then_inc(relu_done, 1)
                act.wait_ge(relu_done, done)
                s.activation(uh[:, par, f, half * 512:(half + 1) * 512], relu_u[:, st % 2, :],
                             ACT.Square).then_inc(sqh_done, 1)

            for half in range(2):
                split_hi(2 * (N_UNITS + 1) + half)
            for st in range(4):
                relu_sq(st + 1, st - 1 if st >= 2 else None, st, 0)
            with act.Fori(0, (NJ - 2) // 2) as jj:
                for r in range(2):
                    act.wait_ge(up_done, jj * 8 + (4 * r + 5))
                    for half in range(2):
                        act.wait_ge(raw_loaded[half], jj * 64 + 16 * (N_UNITS + 2 * r + 3))
                        s.activation(wh[:, 0, half * 1024:(half + 1) * 1024], raw[:, half, :], ACT.Copy).then_inc(w_hi, 1)
                    for st in range(4):
                        relu_sq(jj * 8 + (4 * r + st + 5), jj * 8 + (4 * r + st + 3), st, (r + 1) % 2)
                    for half in range(2):
                        act.wait_ge(raw_loaded[half], jj * 64 + 16 * (N_UNITS + 2 * r + 4))
                        s.activation(wh[:, 1, half * 1024:(half + 1) * 1024], raw[:, half, :], ACT.Copy).then_inc(w_hi, 1)
            for half in range(2):
                split_hi(2 * (N_UNITS + 2 * NJ - 2) + half)
            for st in range(4):
                relu_sq(4 * (NJ - 1) + st + 1, 4 * (NJ - 1) + st - 1, st, 1)
            for half in range(2):
                split_hi(2 * (N_UNITS + 2 * NJ - 1) + half)
            act.wait_ge(sqv_done, 4 * NJ)
            for i in range(NT):
                act.wait_ge(acc_done, 4 + 16 * (NJ - 1) + 2 * i + 2)
                square(("down", i), proj_out[:, i, :], junk2[:])

        @block.vector
        def _(dve):
            v = nc.vector
            n_dv = [0]

            def after(ins):
                n_dv[0] += 1
                ins.then_inc(dv, 1)
                dve.wait_ge(dv, n_dv[0])

            def split_lo(q):
                dve.wait_ge(w_hi, q + 1)
                part = (slice(None), (q // 2) % 2, slice((q % 2) * 1024, (q % 2 + 1) * 1024))
                v.tensor_tensor(wl[part], raw[:, q % 2, :], wh[part].bitcast(F32), ALU.subtract).then_inc(w_lo, 1)

            def mean(what, n, w=1):
                c = stat[:, COL[what]:COL[what] + w]
                v.tensor_scalar(c, c, 1.0 / n, EPS, ALU.mult, ALU.add).then_inc(ms_ready, 1)

            def squares(what):
                dve.wait_ge(sq_done, sum(1 for x in POWS[:POW[what] + 1] if x[0] != "o"))

            def tr_lo(n, dst_h, dst_l):
                for b in range(2):
                    dve.wait_ge(hi_done, 2 * n + b + 1)
                    v.tensor_tensor(dst_l[:, 4 * b:4 * b + 4],
                                    ps[:, 4 + 2 * (n % 2) + b, :].rearrange("p (k c) -> p k c", k=4),
                                    dst_h[:, 4 * b:4 * b + 4].bitcast(F32), ALU.subtract).then_inc(lo_done, 1)

            def normalise(what, n, src, gain, dst):
                dve.wait_ge(rms_ready, POW[what] + 1)
                v.scalar_tensor_tensor(dst, src, rms[:, COL[what]:COL[what] + 1], gain, ALU.mult, ALU.mult).then_inc(h_ready, 1)

            dve.wait_ge(gain_b_loaded, 16)
            for i in range(NT + 3):
                if i < NT:
                    squares(("in", i))
                    mean(("in", i), D)
                if 1 <= i <= NT:
                    if i - 1 >= 2:
                        dve.wait_ge(tr_done, 2 * (i - 2))
                    normalise(("in", i - 1), i - 1, x_in[:, (i - 1) % 2, :], gain_b[:], h_in[:, (i - 1) % 2, :])
                if i >= 3:
                    k = i - 3
                    tr_lo(k, oph[:, :, k * P:(k + 1) * P], opl[:, :, k * P:(k + 1) * P])
                if i in (3, 5, 7, 9):
                    split_lo((i - 3) // 2)
            dve.wait_ge(wdt_hi, 1)
            v.tensor_tensor(wdt_l[:], wdt[:], wdt_h[:].bitcast(F32), ALU.subtract).then_inc(wdt_lo, 1)

            dve.wait_ge(consts_ready, ALL_CONSTS)
            ang, turns = rope_t[:, 0], rope_t[:, 2]
            posf = rope_t[:, 3, 0, 0:NT]
            after(v.tensor_copy(posf, pos_i[:]))
            after(v.tensor_tensor(ang, posf.unsqueeze(2).to_broadcast([P, NT, HALF_DIM]),
                                  inv[:].unsqueeze(1).to_broadcast([P, NT, HALF_DIM]), ALU.mult))
            after(v.tensor_scalar(turns, ang, 1.0 / (2 * math.pi), None, ALU.mult))
            after(v.tensor_scalar(turns, turns, ROUND, None, ALU.add))
            after(v.tensor_scalar(turns, turns, -ROUND, None, ALU.add))
            for part in (TWO_PI_A, TWO_PI_B, TWO_PI_C):
                after(v.scalar_tensor_tensor(ang, turns, -part, ang, ALU.mult, ALU.add))
            v.tensor_scalar(ang, ang, PI_SAFE, -PI_SAFE, ALU.min, ALU.max).then_inc(rope_r, 1)

            after(v.tensor_tensor(lam4[:, 0:2, :], lam4[:, 0:2, :], lam4[:, 2:4, :], ALU.mult))
            v.tensor_reduce(lam[:, 0:2], lam4[:, 0:2, :], AX.X, ALU.add).then_inc(lam_s, 1)
            dve.wait_ge(gain_a_loaded, 32)
            v.tensor_scalar(sub_w[:], sub_w[:], 1.0 - LAMBDA_INIT, None, ALU.mult)

            dve.wait_ge(pj_done, STEP0["dt"] + 1)
            v.tensor_tensor(dts[0][:], ps[:, 0, 0:64].rearrange("p (c h) -> p c h", h=SSD_H),
                            heads8[:, 0, :].unsqueeze(1).to_broadcast([P, NT, SSD_H]), ALU.add).then_inc(ev["dt"], 1)
            dve.wait_ge(ev["dt"], 1)
            v.tensor_scalar(dts[3][:], dts[0][:], 0.0, None, ALU.max).then_inc(dt_v, 1)

            def conv(m):
                dve.wait_ge(ev["xbc"], 2 * m + 2)
                x = xpre[:, m % 2, :]
                after(v.tensor_scalar(mix[:, m, :], x[:, 3:3 + T], conv_w[:, m, 3:4], conv_b[:, m:m + 1], ALU.mult, ALU.add))
                for w in (2, 1):
                    after(v.scalar_tensor_tensor(mix[:, m, :], x[:, w:w + T], conv_w[:, m, w:w + 1], mix[:, m, :],
                                                 ALU.mult, ALU.add))
                v.scalar_tensor_tensor(mix[:, m, :], x[:, 0:T], conv_w[:, m, 0:1], mix[:, m, :],
                                       ALU.mult, ALU.add).then_inc(conv_done, 1)

            for st in range(16):
                if st % 2 and st >= 2:
                    conv((st - 2) // 2)
                for q in split_at("xbc", st):
                    split_lo(q)
            conv(7)

            dve.wait_ge(dt_s, 1)
            after(v.tensor_scalar(dts[5][:], dts[3][:], 0.0, None, ALU.add))
            after(v.tensor_scalar(dts[3][:], dts[2][:], 1.0, None, ALU.add))
            v.tensor_scalar(dts[6][:], dts[3][:], -1.0, None, ALU.add).then_inc(dt_v, 1)
            dve.wait_ge(dt_v, 2)
            after(v.tensor_scalar(dts[7][:], dts[6][:], 1e-30, None, ALU.max))
            after(v.reciprocal(dts[7][:], dts[7][:]))
            after(v.tensor_tensor(dts[7][:], dts[7][:], dts[2][:], ALU.mult))
            dve.wait_ge(dt_s, 3)
            after(v.tensor_tensor(dts[7][:], dts[7][:], dts[4][:], ALU.mult))
            after(v.scalar_tensor_tensor(dts[8][:], dts[6][:], 0.0, dts[2][:], ALU.is_equal, ALU.mult))
            after(v.tensor_tensor(dts[7][:], dts[7][:], dts[8][:], ALU.add))
            after(v.tensor_tensor(dts[0][:], dts[7][:], dts[5][:], ALU.add))
            v.scalar_tensor_tensor(dts[1][:], dts[0][:], -1.0,
                                   heads8[:, 1, :].unsqueeze(1).to_broadcast([P, NT, SSD_H]),
                                   ALU.mult, ALU.mult).then_inc(da_ready, 1)
            dve.wait_ge(cum_done, 1)
            cum, end = dts[5], dts[6]
            v.tensor_copy(cum[:], ps[:, 4, 0:64].rearrange("p (c h) -> p c h", h=SSD_H)).then_inc(dv, 1)
            v.tensor_copy(end[:], ps[:, 4, 64:128].rearrange("p (c h) -> p c h", h=SSD_H)).then_inc(dv, 1)
            n_dv[0] += 2
            dve.wait_ge(dv, n_dv[0])
            v.tensor_tensor(dts[2][:], end[:], cum[:], ALU.subtract).then_inc(dt_v, 1)
            dve.wait_ge(dt_s, 7)
            after(v.tensor_tensor(lam[:, 4:5], lam[:, 3:4], lam[:, 2:3], ALU.subtract))
            after(v.tensor_scalar(lam[:, 4:5], lam[:, 4:5], -LAMBDA_INIT, None, ALU.add))
            dt, e_cum, e_end, dt_end = dts[0], dts[4], dts[7], dts[2]
            after(v.tensor_tensor(dt_end[:], dt[:], dts[8][:], ALU.mult))

            def heads(a):
                return a.rearrange("p (h c) -> p h c", h=SSD_H)

            def spread(a, c):
                return a[:, c, :].unsqueeze(2).to_broadcast([P, SSD_H, 64])

            def ssd_first(c):
                dve.wait_ge(ssd_a, c + 1)
                if c:
                    dve.wait_ge(ssd_b, c)
                xs = heads(ps[:, 4, :])
                v.tensor_tensor(heads(xdt[:]), xs, spread(dt, c), ALU.mult).then_inc(ssd_x, 1)
                v.tensor_tensor(heads(xdt_end[:]), xs, spread(dt_end, c), ALU.mult).then_inc(ssd_x, 1)
                v.tensor_tensor(heads(x_skip[:]), xs, heads8[:, 2, :].unsqueeze(2).to_broadcast([P, SSD_H, 64]),
                                ALU.mult).then_inc(ssd_x, 1)
                both = ps[:, 6:8, :].rearrange("p b (h l) -> p (b h) l", h=4)
                v.tensor_tensor(decay[:], both, cum[:, c, :].unsqueeze(2).to_broadcast([P, SSD_H, P]),
                                ALU.subtract).then_inc(dv, 1)
                n_dv[0] += 1
                dve.wait_ge(dv, n_dv[0])
                v.tensor_scalar(decay[:], decay[:], 0.0, None, ALU.min).then_inc(ssd_seg, 1)

            def ssd_mid(c):
                dve.wait_ge(ssd_exp, c + 1)
                dve.wait_ge(ssd_bcb, c + 1)
                for gr in range(2):
                    ins = v.tensor_tensor(cb_decay[:, 4 * gr:4 * gr + 4, :], decay[:, 4 * gr:4 * gr + 4, :],
                                          b_cb[:, 2 + gr, :].unsqueeze(1).to_broadcast([P, 4, P]), ALU.mult)
                ins.then_inc(ssd_m, 1)

            def ssd_last(c):
                dve.wait_ge(ssd_b, c + 1)
                if c:
                    after(v.tensor_tensor(heads(y_off[:]), heads(ps[:, 7, :]), spread(e_cum, c), ALU.mult))
                    after(v.tensor_tensor(x_skip[:], x_skip[:], y_off[:], ALU.add))
                    after(v.tensor_tensor(heads(state[:]), heads(state[:]), spread(e_end, c), ALU.mult))
                    v.tensor_tensor(state[:], state[:], ps[:, 6, :], ALU.add).then_inc(ssd_h, 1)
                else:
                    v.tensor_copy(state[:], ps[:, 6, :]).then_inc(ssd_h, 1)
                dve.wait_ge(ssd_x, 3 * c + 3)
                v.tensor_tensor(mix[:, 0:4, c * P:(c + 1) * P], ps[:, 4, :].rearrange("p (k c) -> p k c", k=4),
                                x_skip[:].rearrange("p (k c) -> p k c", k=4), ALU.add).then_inc(ssd_y, 1)

            def rope(st, name, g):
                i = st % NT
                n = st + (16 if name == "k" else 0)
                dve.wait_ge(pj_done, g + 1)
                if n == 0:
                    dve.wait_ge(rope_sin, 3)
                if n >= 2:
                    dve.wait_ge(rt_done, n - 1)
                src = ps[:, g % 3, 0:UC].rearrange("p (a h c) -> p a h c", a=4, h=2)
                dst = roped[:, n % 2, :].rearrange("p (a h c) -> p a h c", a=4, h=2)
                tmp = rope_b[:].rearrange("p (a h c) -> p a h c", a=4, h=2)
                spread_t = lambda tab: tab[:, i, :].unsqueeze(1).to_broadcast([P, 4, HALF_DIM])
                for h in range(2):
                    v.tensor_tensor(dst[:, :, h, :], src[:, :, h, :], spread_t(cos_t), ALU.mult)
                if n:
                    dve.wait_ge(rope_done, n)
                v.tensor_tensor(tmp[:, :, 0, :], src[:, :, 1, :], spread_t(nsin_t), ALU.mult)
                v.tensor_tensor(tmp[:, :, 1, :], src[:, :, 0, :], spread_t(sin_t), ALU.mult).then_inc(ev[name], 1)
                dve.wait_ge(ev[name], st + 1)
                v.tensor_tensor(roped[:, n % 2, :], roped[:, n % 2, :], rope_b[:], ALU.add).then_inc(rope_done, 1)

            for n in range(64):
                name, st = STEPS[STEP0["v"] + n]
                if name in ("q", "k"):
                    rope(st, name, STEP0["v"] + n)
                if name == "z":
                    u, i = st // NT, st % NT
                    dve.wait_ge(ev["z"], st + 1)
                    if st == 0:
                        dve.wait_ge(ssd_y, NT)
                    y = mix[:, 2 * u:2 * u + 2, i * P:(i + 1) * P]
                    v.tensor_tensor(y, y, silu_z[:, st % 2, :].rearrange("p (k c) -> p k c", k=2), ALU.mult).then_inc(gate_done, 1)
                for q in split_at(name, st):
                    split_lo(q)
                if n < 32 and n % 4 == 1:
                    ssd_first(n // 4)
                    ssd_mid(n // 4)
                if n < 32 and n % 4 == 3:
                    ssd_last(n // 4)

            for i in range(NT):
                squares(("y", i))
                mean(("y", i), D_SSD)
            for i in range(NT):
                dve.wait_ge(rms_ready, POW[("y", i)] + 1)
                y = mix[:, 0:4, i * P:(i + 1) * P]
                v.scalar_tensor_tensor(y, y, rms[:, COL[("y", i)]:COL[("y", i)] + 1], ssd_w[:].rearrange("p (k c) -> p k c", k=4),
                                       ALU.mult, ALU.mult)

            steps = [(i, h) for i in range(NT) for h in range(DH)]
            NS = len(steps)

            def attn_max(n, c):
                keys = (steps[n][0] + 1) * P
                dve.wait_ge(s_done[c], n + 1)
                if n >= 2:
                    dve.wait_ge(ex_done[c], n - 1)
                src = ps[:, 2 * c:2 * c + 2, :].rearrange("p b k -> p (b k)")
                v.tensor_reduce(nmax[:, n % 2, c:c + 1], src[:, 0:keys], AX.X, ALU.max, negate=True).then_inc(mx_done[c], 1)

            def attn_comb(n):
                keys = (steps[n][0] + 1) * P
                dve.wait_ge(ex_done[0], n + 1)
                dve.wait_ge(ex_done[1], n + 1)
                if n >= 4:
                    dve.wait_ge(o_ev, n - 3)
                after(v.reciprocal(recs[:, n % 4, :], sums[:, n % 4, :]))
                after(v.scalar_tensor_tensor(ratio[:, n % 2:n % 2 + 1], sums[:, n % 4, 0:1], recs[:, n % 4, 1:2],
                                             lam[:, 4:5], ALU.mult, ALU.mult))
                v.scalar_tensor_tensor(probs[:, n % 2, 0, 0:keys], probs[:, n % 2, 1, 0:keys], ratio[:, n % 2:n % 2 + 1],
                                       probs[:, n % 2, 0, 0:keys], ALU.mult, ALU.add).then_inc(comb_done, 1)

            for n in range(NS + 1):
                if n < NS:
                    attn_max(n, 0)
                if n >= 1:
                    attn_comb(n - 1)
                if n < NS:
                    attn_max(n, 1)
            for i in range(NT):
                dve.wait_ge(o_ev, DH * (i + 1))
                mean(("o", i), P, DH)
            for i in range(NT):
                dve.wait_ge(rms_ready, POW[("o", i)] + 1)
                for h in range(DH):
                    o = mix[:, 4 + h, i * P:(i + 1) * P]
                    ins = v.scalar_tensor_tensor(o, o, rms[:, COL[("o", i)] + h:COL[("o", i)] + h + 1], sub_w[:], ALU.mult, ALU.mult)
                ins.then_inc(h_ready, 1)
                if i:
                    tr_lo(TR_MIX + i - 1, oph[:, :, (i - 1) * P:i * P], opl[:, :, (i - 1) * P:i * P])
            tr_lo(TR_MIX + 7, oph[:, :, 7 * P:T], opl[:, :, 7 * P:T])

            for i in range(MT):
                squares(("mem", i))
                mean(("mem", i), D)
            dve.wait_ge(gain_b_loaded, 32)
            for i in range(MT):
                normalise(("mem", i), TR_MEM + i, m_in[:, i, :], gain_b[:], h_mem[:, i, :])
            for i in range(MT):
                tr_lo(TR_MEM + i, memh[:, :, i * P:(i + 1) * P], meml[:, :, i * P:(i + 1) * P])
            for name in ("mk", "mv"):
                for st in range(8):
                    for q in split_at(name, st):
                        split_lo(q)

            def out_proj(name, nxt, tr0, first):
                for st in range(3 * NT):
                    for q in split_at(name, st):
                        split_lo(q)
                k0 = 0 if name == "wo" else NT
                for k in range(NT + 5):
                    if k < NT:
                        for q in split_at(name, 3 * NT + k):
                            split_lo(q)
                        squares((name, k))
                        mean((name, k), D)
                    if 1 <= k <= NT:
                        i = k - 1
                        dve.wait_ge(rms_ready, POW[(name, i)] + 1)
                        if i == 0:
                            dve.wait_ge(gain_a_loaded, 48 if name == "wo" else 64)
                            dve.wait_ge(gain_b_loaded, 48 if name == "wo" else 64)
                            dve.wait_ge(resid_loaded, 16 * NT)
                        after(v.scalar_tensor_tensor(proj_out[:, i, :], proj_out[:, i, :], rms[:, COL[(name, i)]:COL[(name, i)] + 1],
                                                     gain_a[:], ALU.mult, ALU.mult))
                        v.tensor_tensor(resid[:, i, :], resid[:, i, :], proj_out[:, i, :], ALU.add).then_inc(resid_done, 1)
                    if 2 <= k <= NT + 1:
                        i = k - 2
                        if i >= 2:
                            dve.wait_ge(tr_done, 2 * (tr0 + i - 1))
                        normalise((nxt, i), tr0 + i, resid[:, i, :], gain_b[:], h_tok[:, i % 2, :])
                    if k >= 5:
                        i = k - 5
                        tr_lo(tr0 + i, oph[:, :, i * P:(i + 1) * P], opl[:, :, i * P:(i + 1) * P])
                    if 1 <= k <= NT:
                        squares((nxt, k - 1))
                        mean((nxt, k - 1), D)

            out_proj("wo", "q", TR_Q, 0)
            for st in range(16):
                for q in split_at("mq", st):
                    split_lo(q)

            for n in range(NT + 3):
                if n < NT:
                    dve.wait_ge(ms_done, n + 1)
                    if n >= 2:
                        dve.wait_ge(mex_done, n - 1)
                    src = ps[:, 2 * (n % 2):2 * (n % 2) + 2, :].rearrange("p b (h m) -> p (b h) m", h=2)
                    v.tensor_reduce(mmax[:, n % 2, :], src, AX.X, ALU.max, negate=True).then_inc(mmx_done, 1)
                if 1 <= n <= NT:
                    k = n - 1
                    dve.wait_ge(mex_done, k + 1)
                    after(v.reciprocal(mrec[:, k % 2, :], msum[:, k % 2, :]))
                    v.tensor_tensor(mprobs[:, k % 2], mprobs[:, k % 2],
                                    mrec[:, k % 2, :].unsqueeze(2).to_broadcast([P, MH, MEM]), ALU.mult).then_inc(mn_done, 1)
                if n >= 3:
                    k = n - 3
                    dve.wait_ge(mo_hi, k + 1)
                    v.tensor_tensor(opl[:, :, k * P:(k + 1) * P], ps[:, 6:8, :].rearrange("p b (h m) -> p (b h) m", h=4),
                                    oph[:, :, k * P:(k + 1) * P].bitcast(F32), ALU.subtract).then_inc(mo_lo, 1)

            out_proj("mo", "mlp", TR_MLP, NT)

            for half in range(2):
                split_lo(2 * (N_UNITS + 1) + half)
            v.memset(proj_out[:], 0.0).then_inc(acc_done, 4)

            def square_lo(j4, par, st):
                f, half = st // 2, st % 2
                dve.wait_ge(relu_done, j4 + (st + 1))
                v.tensor_tensor(sq_u[:, st % 2, :], relu_u[:, st % 2, :], relu_u[:, st % 2, :], ALU.mult).then_inc(sqv_done, 1)
                dve.wait_ge(sqv_done, j4 + (st + 1))
                dve.wait_ge(sqh_done, j4 + (st + 1))
                part = (slice(None), par, f, slice(half * 512, (half + 1) * 512))
                v.tensor_tensor(ul[part], sq_u[:, st % 2, :], uh[part].bitcast(F32), ALU.subtract).then_inc(ul_done, 1)

            def add_down(j16, n):
                i, ch = n // 2, n % 2
                dve.wait_ge(down_done, j16 + (n + 1))
                a = proj_out[:, i, ch * 512:(ch + 1) * 512]
                v.tensor_tensor(a, a, ps[:, 4 + n % 4, :], ALU.add).then_inc(acc_done, 1)

            def split_lo_mlp(count, slot, half):
                dve.wait_ge(w_hi, count)
                part = (slice(None), slot, slice(half * 1024, (half + 1) * 1024))
                v.tensor_tensor(wl[part], raw[:, half, :], wh[part].bitcast(F32), ALU.subtract).then_inc(w_lo, 1)

            dve.wait_ge(acc_done, 4)
            for st in range(4):
                square_lo(0, 0, st)
            with dve.Fori(0, (NJ - 2) // 2) as jj:
                for r in range(2):
                    for half in range(2):
                        split_lo_mlp(jj * 8 + (2 * (N_UNITS + 2 * r + 2) + half + 1), 0, half)
                    for st in range(4):
                        square_lo(jj * 8 + 4 * (r + 1), (r + 1) % 2, st)
                    for n in range(4):
                        add_down(jj * 32 + 16 * r, n)
                    for half in range(2):
                        split_lo_mlp(jj * 8 + (2 * (N_UNITS + 2 * r + 3) + half + 1), 1, half)
                    for n in range(4, 16):
                        add_down(jj * 32 + 16 * r, n)
            split_lo(2 * (N_UNITS + 2 * NJ - 2))
            split_lo(2 * (N_UNITS + 2 * NJ - 2) + 1)
            for st in range(4):
                square_lo(4 * (NJ - 1), 1, st)
            for n in range(4):
                add_down(16 * (NJ - 2), n)
            split_lo(2 * (N_UNITS + 2 * NJ - 1))
            split_lo(2 * (N_UNITS + 2 * NJ - 1) + 1)
            for n in range(4, 16):
                add_down(16 * (NJ - 2), n)
            for n in range(16):
                add_down(16 * (NJ - 1), n)
                if n == 0:
                    dve.wait_ge(gain_a_loaded, 80)
                if n % 2 and n >= 3:
                    i = n // 2 - 1
                    squares(("down", i))
                    mean(("down", i), D)
            squares(("down", NT - 1))
            mean(("down", NT - 1), D)
            for i in range(NT):
                dve.wait_ge(rms_ready, POW[("down", i)] + 1)
                after(v.scalar_tensor_tensor(proj_out[:, i, :], proj_out[:, i, :], rms[:, COL[("down", i)]:COL[("down", i)] + 1],
                                             gain_a[:], ALU.mult, ALU.mult))
                v.tensor_tensor(resid[:, i, :], resid[:, i, :], proj_out[:, i, :], ALU.add).then_inc(resid_done, 1)

        @block.tensor
        def _(pe):
            te = nc.tensor

            def three(o, lh, ll, rh, rl, first, last):
                te.matmul(o, lh, rh, start=first, stop=False)
                te.matmul(o, lh, rl, start=False, stop=False)
                return te.matmul(o, ll, rh, start=False, stop=last)

            def wcols(w, slot, k, c0=0, n=UC):
                return w[:, slot, k * UC + c0:k * UC + c0 + n]

            def unit_ready(u):
                pe.wait_ge(w_lo, 2 * u + 2)

            def token_step(name, st, lh, ll, tile):
                per = PER_UNIT[name]
                g, u = STEP0[name] + st, UNIT0[name] + st // per
                bank_free(pe, g)
                unit_ready(u)
                for k in range(KD):
                    ins = three(ps[:, g % 3, 0:UC], lh[:, k, tile * P:(tile + 1) * P], ll[:, k, tile * P:(tile + 1) * P],
                                wcols(wh, u % 2, k), wcols(wl, u % 2, k), k == 0, k == KD - 1)
                ins.then_inc(pj_done, 1)

            def feature_step(name, st, rh, rl, f, c0, n):
                per = PER_UNIT[name]
                g, u = STEP0[name] + st, UNIT0[name] + st // per
                bank_free(pe, g)
                unit_ready(u)
                for k in range(KD):
                    ins = three(ps[:, g % 3, 0:n], wcols(wh, u % 2, k, f * P, P), wcols(wl, u % 2, k, f * P, P),
                                rh[:, k, c0:c0 + n], rl[:, k, c0:c0 + n], k == 0, k == KD - 1)
                ins.then_inc(pj_done, 1)

            def transpose_tile(n, src):
                if n >= 2:
                    pe.wait_ge(lo_done, 2 * (n - 1))
                pe.wait_ge(h_ready, n + 1)
                for b in range(2):
                    for k in range(4):
                        ins = te.transpose(ps[:, 4 + 2 * (n % 2) + b, k * P:(k + 1) * P], src(4 * b + k), ident[:])
                    ins.then_inc(tr_done, 1)

            pe.wait_ge(consts_ready, 6)
            for i in range(NT):
                transpose_tile(TR_IN + i, lambda k: h_in[:, i % 2, k * P:(k + 1) * P])

            pe.wait_ge(lo_done, 2 * NT)
            pe.wait_ge(wdt_lo, 1)
            for i in range(NT):
                for k in range(KD):
                    tok = slice(i * P, (i + 1) * P)
                    ins = three(ps[:, 0, i * SSD_H:(i + 1) * SSD_H], oph[:, k, tok], opl[:, k, tok],
                                wdt_h[:, k, :], wdt_l[:, k, :], k == 0, k == KD - 1)
            ins.then_inc(pj_done, 1)

            for st in range(16):
                feature_step("xbc", st, oph, opl, (st % 4) // 2, (st % 2) * 512, 512)

            pe.wait_ge(da_ready, 1)
            da = dts[1]
            da_all = da[:].rearrange("p c h -> p (c h)")
            te.matmul(ps[:, 4, 0:64], tri[:], da_all, start=True, stop=True)
            te.matmul(ps[:, 4, 64:128], ones[:], da_all, start=True, stop=True).then_inc(cum_done, 1)

            def ssd_products(c):
                tok = slice(c * P, (c + 1) * P)
                pe.wait_ge(silu_done, KD)
                pe.wait_ge(dt_v, 3)
                if c:
                    pe.wait_ge(ssd_y, c)
                    pe.wait_ge(ssd_h, c)
                    pe.wait_ge(ssd_bcb, c)
                for k in range(4):
                    te.transpose(ps[:, 4, k * P:(k + 1) * P], mix[:, k, tok], ident[:])
                for gr in range(2):
                    te.transpose(ps[:, 5, gr * P:(gr + 1) * P], mix[:, 4 + gr, tok], ident[:])
                for gr in range(2):
                    te.matmul(ps[:, 5, (2 + gr) * P:(3 + gr) * P], mix[:, 4 + gr, tok], mix[:, 6 + gr, tok],
                              start=True, stop=True)
                for b in range(2):
                    te.matmul(ps[:, 6 + b, :], ident_b[:], mask_s[:].rearrange("p a l -> p (a l)"), start=True, stop=False)
                    for h in range(4):
                        hh = 4 * b + h
                        ins = te.matmul(ps[:, 6 + b, h * P:(h + 1) * P], da[:, c, hh:hh + 1].to_broadcast([P, P]), tri[:],
                                        start=False, stop=h == 3)
                ins.then_inc(ssd_a, 1)

            def ssd_outputs(c):
                pe.wait_ge(ssd_m, c + 1)
                pe.wait_ge(ssd_x, 3 * c + 3)
                for h in range(SSD_H):
                    te.matmul(ps[:, 4, h * 64:(h + 1) * 64], cb_decay[:, h, :], xdt[:, h * 64:(h + 1) * 64],
                              start=True, stop=True)
                for gr in range(2):
                    ins = te.matmul(ps[:, 6, gr * 256:(gr + 1) * 256], b_cb[:, gr, :], xdt_end[:, gr * 256:(gr + 1) * 256],
                                    start=True, stop=True)
                if c:
                    pe.wait_ge(ssd_h, c)
                    for gr in range(2):
                        ins = te.matmul(ps[:, 7, gr * 256:(gr + 1) * 256], mix[:, 6 + gr, c * P:(c + 1) * P],
                                        state[:, gr * 256:(gr + 1) * 256], start=True, stop=True)
                ins.then_inc(ssd_b, 1)

            def rope_transpose(n):
                pe.wait_ge(rope_done, n + 1)
                if n:
                    pe.wait_ge(rt_ev, n)
                for b in range(2):
                    ins = te.transpose(ps[:, 3, b * P:(b + 1) * P], roped[:, n % 2, b * P:(b + 1) * P], ident[:])
                ins.then_inc(rt_done, 1)

            for n in range(66):
                if n < 64:
                    name, st = STEPS[STEP0["v"] + n]
                    token_step(name, st, oph, opl, st % NT)
                if n < 32 and n % 4 == 1:
                    ssd_products(n // 4)
                if n < 32 and n % 4 == 3:
                    ssd_outputs(n // 4)
                if 16 <= n - 2 < 48:
                    rope_transpose(n - 18)

            steps = [(i, h) for i in range(NT) for h in range(DH)]
            NS = len(steps)
            pe.wait_ge(ev["z"], 16)
            pe.wait_ge(rt_ev, 32)
            pe.wait_ge(ev["v"], 16)

            def scores(n, c):
                i, h = steps[n]
                half = slice(64 * c, 64 * c + 64)
                if n:
                    pe.wait_ge(ex_done[c], n)
                for k0 in range(0, (i + 1) * P, 512):
                    kn = min(512, (i + 1) * P - k0)
                    diag = k0 + kn == (i + 1) * P
                    ins = te.matmul(ps[:, 2 * c + k0 // 512, 0:kn], qt[half, h, i * P:(i + 1) * P], kt[half, h, k0:k0 + kn],
                                    start=True, stop=not diag)
                    if diag:
                        ins = te.matmul(ps[:, 2 * c + k0 // 512, kn - P:kn], ident_b[:], mask_q[:], start=False, stop=True)
                ins.then_inc(s_done[c], 1)

            for n in range(NS + 2):
                if n < NS:
                    scores(n, 0)
                    scores(n, 1)
                if n >= 2:
                    k = n - 2
                    i, h = steps[k]
                    pe.wait_ge(pt_ev, k + 1)
                    if k >= 2:
                        pe.wait_ge(o_ev, k - 1)
                    for b in range(i + 1):
                        ins = te.matmul(ps[:, 6 + k % 2, 0:P], probs_t[:, k % 2, b, :], vt[:, b, h * P:(h + 1) * P],
                                        start=b == 0, stop=b == i)
                    ins.then_inc(pv_done, 1)
                if 1 <= n <= NS:
                    k = n - 1
                    i = steps[k][0]
                    pe.wait_ge(comb_done, k + 1)
                    if k:
                        pe.wait_ge(pt_ev, k)
                    for b in range(i + 1):
                        ins = te.transpose(ps[:, 4 + b // 4, (b % 4) * P:(b % 4 + 1) * P],
                                           probs[:, k % 2, 0, b * P:(b + 1) * P], ident[:])
                    ins.then_inc(pt_done, 1)

            pe.wait_ge(pt_ev, NS)
            pe.wait_ge(o_ev, NS)
            for i in range(NT):
                transpose_tile(TR_MIX + i, lambda k: mix[:, k, i * P:(i + 1) * P])
            for i in range(MT):
                transpose_tile(TR_MEM + i, lambda k: h_mem[:, i, k * P:(k + 1) * P])
            pe.wait_ge(lo_done, 2 * (TR_MEM + MT))
            for st in range(8):
                feature_step("mk", st, memh, meml, st % 2, 0, MEM)
            for st in range(8):
                token_step("mv", st, memh, meml, st % MT)

            def out_proj(name, tr0, ready):
                for st in range(4 * NT):
                    ready(st)
                    token_step(name, st, oph, opl, st % NT)
                    if st >= 3 * NT + 3:
                        i = st - 3 * NT - 3
                        transpose_tile(tr0 + i, lambda k: h_tok[:, i % 2, k * P:(k + 1) * P])
                for i in range(NT - 3, NT):
                    transpose_tile(tr0 + i, lambda k: h_tok[:, i % 2, k * P:(k + 1) * P])

            out_proj("wo", TR_Q, lambda st: None)
            for st in range(16):
                if st < 2:
                    pe.wait_ge(lo_done, 2 * (TR_Q + 4 * st + 4))
                feature_step("mq", st, oph, opl, (st % 4) // 2, (st % 2) * 512, 512)

            pe.wait_ge(ev["mq"], 16)
            pe.wait_ge(ev["mv"], 8)
            for n in range(NT + 2):
                if n < NT:
                    if n >= 2:
                        pe.wait_ge(mex_done, n - 1)
                    for h in range(MH):
                        for d in range(2):
                            ins = te.matmul(ps[:, 2 * (n % 2) + h // 2, (h % 2) * MEM:(h % 2 + 1) * MEM],
                                            qct[:, 2 * h + d, n * P:(n + 1) * P], kmt[:, 2 * h + d, :],
                                            start=d == 0, stop=d == 1)
                    ins.then_inc(ms_done, 1)
                if n >= 2:
                    k = n - 2
                    pe.wait_ge(mt_ev, k + 1)
                    if k:
                        pe.wait_ge(mo_lo, k)
                    for d in range(KD):
                        for m in range(MT):
                            ins = te.matmul(ps[:, 6 + d // 4, (d % 4) * P:(d % 4 + 1) * P], vm[:, m, d * P:(d + 1) * P],
                                            mprobs_t[:, k % 2, (d // 2) * MT + m, :], start=m == 0, stop=m == MT - 1)
                    ins.then_inc(mo_done, 1)
                if 1 <= n <= NT:
                    k = n - 1
                    pe.wait_ge(mn_done, k + 1)
                    if k:
                        pe.wait_ge(mt_ev, k)
                    for h in range(MH):
                        for m in range(MT):
                            b = h * MT + m
                            ins = te.transpose(ps[:, 4 + b // 4, (b % 4) * P:(b % 4 + 1) * P],
                                               mprobs[:, k % 2, h, m * P:(m + 1) * P], ident[:])
                    ins.then_inc(mt_done, 1)

            out_proj("mo", TR_MLP, lambda st: pe.wait_ge(mo_lo, st + 1) if st < NT else None)

            pe.wait_ge(lo_done, 2 * (TR_MLP + NT))
            pe.wait_ge(ev["mo"], 4 * NT)

            def up_step(st, slot):
                f, half = st // 2, st % 2
                for k in range(KD):
                    ins = three(ps[:, st, :], wcols(wh, slot, k, f * P, P), wcols(wl, slot, k, f * P, P),
                                oph[:, k, half * 512:(half + 1) * 512], opl[:, k, half * 512:(half + 1) * 512],
                                k == 0, k == KD - 1)
                ins.then_inc(up_done, 1)

            def down_step(n, par, slot, wait):
                i, ch = n // 2, n % 2
                pe.wait_ge(acc_done, wait)
                for f in range(2):
                    tok, col = slice(i * P, (i + 1) * P), slice(f * 1024 + ch * 512, f * 1024 + (ch + 1) * 512)
                    ins = three(ps[:, 4 + n % 4, :], uh[:, par, f, tok], ul[:, par, f, tok],
                                wh[:, slot, col], wl[:, slot, col], f == 0, f == 1)
                ins.then_inc(down_done, 1)

            unit_ready(N_UNITS)
            for st in range(4):
                up_step(st, 0)
            with pe.Fori(0, (NJ - 2) // 2) as jj:
                for r in range(2):
                    pe.wait_ge(w_lo, jj * 8 + 2 * (N_UNITS + 2 * r + 2))
                    for st in range(4):
                        pe.wait_ge(relu_done, jj * 8 + (4 * r + st + 1))
                        up_step(st, 1)
                    pe.wait_ge(w_lo, jj * 8 + 2 * (N_UNITS + 2 * r + 3))
                    pe.wait_ge(ul_done, jj * 8 + (4 * r + 4))
                    for n in range(16):
                        down_step(n, r, 0, jj * 32 + (16 * r + n + 1))
            unit_ready(N_UNITS + 2 * NJ - 3)
            for st in range(4):
                pe.wait_ge(relu_done, 4 * (NJ - 2) + st + 1)
                up_step(st, 1)
            for j, slot in ((NJ - 2, 0), (NJ - 1, 1)):
                unit_ready(N_UNITS + NJ + j)
                pe.wait_ge(ul_done, 4 * (j + 1))
                for n in range(16):
                    down_step(n, j % 2, slot, 16 * j + n + 1)


_INS = ["x", "mem", "positions", "norm_mix_pre", "norm_mix_post", "norm_mem_q", "norm_mem_kv", "norm_mem_post",
        "norm_mlp_pre", "norm_mlp_post", "w_in", "conv_w", "conv_b", "dt_bias", "a_log", "d_skip", "ssd_norm_w",
        "lambda_q1", "lambda_k1", "lambda_q2", "lambda_k2", "subln_w", "w_out", "w_mq", "w_mk", "w_mv", "w_mo",
        "w_up", "w_down"]


def kernel(**inputs):
    import numpy as _np
    import concourse.bacc as _bacc
    from concourse import mybir as _mybir
    from concourse.bass_utils import run_bass_kernel_spmd as _run

    nc = _bacc.Bacc("TRN2", target_bir_lowering=False, num_devices=1, dynamic_dma_scratch_size=1024)
    arrays, tensors = {}, {}
    for name in _INS:
        a = _np.ascontiguousarray(inputs[name])
        arrays[f"in_{name}_dram"] = a
        tensors[name] = nc.dram_tensor(f"in_{name}_dram", a.shape, _mybir.dt.from_np(a.dtype),
                                       kind="ExternalInput").ap()
    out = nc.dram_tensor("out_0_dram", (1, T, D), _mybir.dt.float32, kind="ExternalOutput").ap()
    build(nc, tensors, out)
    r = _run(nc, [arrays], core_ids=[0])
    return r.results[0]["out_0_dram"]
```

```python
import math
from contextlib import ExitStack

import concourse.bass as bass
import numpy as np
from concourse import mybir

F32 = mybir.dt.float32
F32R = mybir.dt.float32r
BF16 = mybir.dt.bfloat16
I32 = mybir.dt.int32
ALU = mybir.AluOpType
ACT = mybir.ActivationFunctionType
AX = mybir.AxisListType

P = 128
T = 1024
D = 1024
NT = T // P
KD = D // P
MEM = 256
MT = MEM // P
D_SSD = 512
XBC = 1024
SSD_H = 8
DH = 4
MH = 4
FF = 4096
EPS = 1e-6
LAMBDA_INIT = 0.8 - 0.6 * math.exp(-0.3 * 0)
THETA = 10000.0
HALF_DIM = 32
NEG = -1e30

UC = 256
UE = KD * UC
COL_Z, COL_XBC, COL_DT = 0, D_SSD, D_SSD + XBC
COL_Q = COL_DT + SSD_H
COL_K, COL_V = COL_Q + 512, COL_Q + 1024

TWO_PI_A = 6.28125
TWO_PI_B = 0.0019350051879882812
TWO_PI_C = 3.0199159795074593e-07
ROUND = 1.5 * 2.0 ** 23
PI_SAFE = 3.1415925

PROJ = [("xbc", 4, 4), ("dt", 2, 0), ("v", 8, 2), ("q", 8, 2), ("k", 8, 2), ("z", 8, 2),
        ("mk", 2, 4), ("mv", 2, 4), ("wo", 8, 4), ("mq", 4, 4), ("mo", 8, 4)]


def proj_tables():
    first, unit, steps, u = {}, {}, [], 0
    for name, per, n in PROJ:
        first[name], unit[name] = len(steps), u
        steps += [(name, s) for s in range(per * max(n, 1))]
        u += n
    return first, unit, steps, u


STEP0, UNIT0, STEPS, N_UNITS = proj_tables()
PER_UNIT = {name: per for name, per, _ in PROJ}

XBC_ORDER = [(0, 0), (1, 0), (0, 1), (1, 1)] + [(m, half) for m in range(2, KD) for half in range(2)]
XBC_CONV = {2: 0, 3: 1, **{2 * m + 1: m for m in range(2, KD)}}

OUT_ORDER = ([(u, i) for u in range(2) for i in range(NT)] + [(2, 0), (2, 1), (2, 2)]
             + [x for i in range(NT - 3) for x in ((3, i), (2, i + 3))] + [(3, i) for i in range(NT - 3, NT)])
OUT_COMPLETE = [OUT_ORDER.index((3, i)) for i in range(NT)]
OUT_UNIT_END = [max(n for n, x in enumerate(OUT_ORDER) if x[0] == u) + 1 for u in range(4)]
OUT_SPLIT = {0: 2, 4: 3, 8: 4, 12: 5, 16: 6, 17: 7, OUT_UNIT_END[2]: 8, OUT_UNIT_END[2] + 1: 9}
OUT_TR = {OUT_COMPLETE[i + 2] + 2: i for i in range(4)}

SSD_FIRST = {4 + 5 * c: c for c in range(NT)}
SSD_MID = {n + 1: c for n, c in SSD_FIRST.items()}
SSD_LAST = {n + 3: c for n, c in SSD_FIRST.items()}

TR_IN, TR_MIX, TR_MEM, TR_Q, TR_MLP = 0, 8, 16, 18, 26

POWS = ([("in", i) for i in range(NT)] + [("y", i) for i in range(NT)] + [("o", i) for i in range(NT)]
        + [("mem", i) for i in range(MT)])
for _a, _b in (("wo", "q"), ("mo", "mlp")):
    for _t in range(NT + 1):
        POWS += [(_a, _t)] * (_t < NT) + [(_b, _t - 1)] * (_t > 0)
POWS += [("down", i) for i in range(NT)]
POW = {what: n for n, what in enumerate(POWS)}
COL = {}
for _what in POWS:
    COL[_what] = sum(DH if x[0] == "o" else 1 for x in COL)
N_COLS = len(POWS) + NT * (DH - 1)


def build(nc, t, out):
    ctx = ExitStack()
    with ctx:
        base = (nc.sbuf_base + 63) // 64 * 64
        place = {}
        size = {"OPH": 32768, "OPL": 32768, "WH": 16384, "WL": 16384, "RAW": 8192, "X": 32768,
                "Q": 16384, "K": 16384, "V": 16384, "TMP": 16384, "GA": 4096, "GB": 4096, "MISC": 8192}
        for region, n in size.items():
            place[region] = base
            base += n
        rest = [base]

        def at(name, region, offset, shape, dt=F32):
            return nc.alloc_sbuf_tensor_at(name, shape, dt, offset=place[region] + offset)

        def small(name, shape, dt=F32):
            n = 4 if dt in (F32, F32R, I32) else 2
            for s in shape[1:]:
                n *= s
            r = nc.alloc_sbuf_tensor_at(name, shape, dt, offset=rest[0])
            rest[0] += (n + 31) // 32 * 32
            return r

        def sem(name):
            return ctx.enter_context(nc.semaphore(name))

        oph = at("oph", "OPH", 0, [P, KD, T], F32R)
        opl = at("opl", "OPL", 0, [P, KD, T], F32R)
        wh = at("wh", "WH", 0, [P, 2, UE], F32R)
        wl = at("wl", "WL", 0, [P, 2, UE], F32R)
        raw = at("raw", "RAW", 0, [P, 2, UE // 2])
        mix = at("mix", "X", 0, [P, KD, T])
        resid = at("resid", "X", 0, [P, NT, D])
        x_in = at("x_in", "V", 0, [P, 4, D])
        h_in = at("h_in", "K", 8192, [P, 2, D])
        xpre = at("xpre", "Q", 0, [P, 2, T + 4])
        rope_t = at("rope_t", "K", 0, [P, 4, NT, HALF_DIM])
        xdt = at("xdt", "TMP", 7168, [P, 512])
        xdt_end = at("xdt_end", "TMP", 9216, [P, 512])
        x_skip = at("x_skip", "TMP", 11264, [P, 512])
        b_cb = at("b_cb", "TMP", 13312, [P, 4, P])
        decay = at("decay", "GA", 0, [P, SSD_H, P])
        cb_decay = at("cb_decay", "GB", 0, [P, SSD_H, P])
        conv_rows = at("conv_rows", "TMP", 13312, [P, P])
        pos_i = at("pos_i", "TMP", 13824, [P, P], I32)
        pos_rows = at("pos_rows", "TMP", 14336, [P, P])
        state = at("state", "TMP", 0, [P, 512])
        y_off = at("y_off", "TMP", 2048, [P, 512])
        roped = at("roped", "TMP", 4096, [P, 2, UC])
        rope_b = at("rope_b", "TMP", 6144, [P, UC])
        silu_z = at("silu_z", "TMP", 7168, [P, 2, UC])
        junk = at("junk", "TMP", 9216, [P, D])
        qt = at("qt", "Q", 0, [P, DH, T])
        kt = at("kt", "K", 0, [P, DH, T])
        vt = at("vt", "V", 0, [P, NT, 512])
        probs = at("probs", "OPH", 0, [P, 2, 2, T])
        probs_t = at("probs_t", "OPH", 16384, [P, 2, NT, P])
        memh = at("memh", "Q", 0, [P, KD, MEM], F32R)
        meml = at("meml", "Q", 8192, [P, KD, MEM], F32R)
        m_in = at("m_in", "K", 0, [P, 2, D])
        h_mem = at("h_mem", "K", 8192, [P, 2, D])
        kmt = at("kmt", "V", 0, [P, KD, MEM])
        vm = at("vm", "V", 8192, [P, MT, D])
        proj_out = at("proj_out", "Q", 0, [P, NT, D])
        qct = at("qct", "Q", 0, [P, KD, T])
        h_tok = at("h_tok", "TMP", 0, [P, 2, D])
        mprobs = at("mprobs", "TMP", 0, [P, 2, MH, MEM])
        mprobs_t = at("mprobs_t", "TMP", 8192, [P, 2, MH * MT, P])
        uh = at("uh", "V", 0, [P, 2, 2, T], F32R)
        ul = at("ul", "TMP", 0, [P, 2, 2, T], F32R)
        relu_u = at("relu_u", "MISC", 0, [P, 2, 512])
        sq_u = at("sq_u", "MISC", 4096, [P, 2, 512])
        junk2 = at("junk2", "MISC", 0, [P, D])
        cos_t = at("cos_t", "MISC", 0, [P, NT, HALF_DIM])
        sin_t = at("sin_t", "MISC", 1024, [P, NT, HALF_DIM])
        nsin_t = at("nsin_t", "MISC", 2048, [P, NT, HALF_DIM])
        dts = [at(f"dts{n}", "MISC", 3072 + 256 * n, [P, NT, SSD_H]) for n in range(9)]
        ncum = dts[3]
        ssd_w = at("ssd_w", "MISC", 5376, [P, 512])
        gain_a = at("gain_a", "GA", 0, [P, D])
        gain_b = at("gain_b", "GB", 0, [P, D])

        ident = small("ident", [P, P])
        tri = small("tri", [P, P])
        ones = small("ones", [P, P])
        ident_b = small("ident_b", [P, P], BF16)
        mask_q = small("mask_q", [P, P], BF16)
        mask_s = small("mask_s", [P, 4, P], BF16)
        inv = small("inv", [P, HALF_DIM])
        conv_wb = small("conv_wb", [P, 5, KD])
        wdt = at("wdt", "MISC", 7424, [P, KD, SSD_H])
        wdt_h = at("wdt_h", "K", 4096, [P, KD * SSD_H + P], F32R)
        wdt_l = at("wdt_l", "K", 5120, [P, KD * SSD_H + P], F32R)
        dt_rows = at("dt_rows", "K", 8192, [P, T])
        heads8 = small("heads8", [P, 3, SSD_H])
        lam4 = small("lam4", [P, 4, 64])
        lam = small("lam", [P, 8])
        sub_w = small("sub_w", [P, P])
        stat = small("stat", [P, N_COLS])
        rms = small("rms", [P, N_COLS])
        mhalf = small("mhalf", [P, 4])
        half_pi = small("half_pi", [P, 1])
        nmax = small("nmax", [P, 2, 2])
        sums = small("sums", [P, 4, 2])
        recs = small("recs", [P, 4, 2])
        ratio = small("ratio", [P, 2])
        mmax = small("mmax", [P, 2, MH])
        msum = small("msum", [P, 2, MH])
        mrec = small("mrec", [P, 2, MH])
        assert rest[0] <= nc.sbuf_usable_end, (rest[0], nc.sbuf_usable_end)
        ps = ctx.enter_context(nc.psum_tensor("ps", [P, 8, 512], F32))

        x_loaded = [sem(f"x_loaded{n}") for n in range(4)]
        rows_loaded, wdt_loaded, small_loaded = sem("rows_loaded"), sem("wdt_loaded"), sem("small_loaded")
        pos_ready, rows_tr = sem("pos_ready"), sem("rows_tr")
        gain_a_loaded, gain_b_loaded = sem("gain_a_loaded"), sem("gain_b_loaded")
        raw_loaded = [sem(f"raw_loaded{n}") for n in range(2)]
        w_hi, w_lo = sem("w_hi"), sem("w_lo")
        pool_c = sem("pool_c")
        consts_ready = sem("consts_ready")
        sq_done, ms_ready, rms_ready = sem("sq_done"), sem("ms_ready"), sem("rms_ready")
        h_ready = sem("h_ready")
        tr_done, hi_done, lo_done = sem("tr_done"), sem("hi_done"), sem("lo_done")
        pj_done = sem("pj_done")
        ev = {name: sem(f"ev_{name}") for name, _, _ in PROJ}
        dv = sem("dv")
        av = sem("av")
        rope_r, rope_abs, rope_sin = sem("rope_r"), sem("rope_abs"), sem("rope_sin")
        conv_done, silu_done = sem("conv_done"), sem("silu_done")
        wdt_hi, wdt_lo = sem("wdt_hi"), sem("wdt_lo")
        dt_tr = sem("dt_tr")
        dt_v, dt_s = sem("dt_v"), sem("dt_s")
        da_ready, cum_done = sem("da_ready"), sem("cum_done")
        ssd_a, ssd_b = sem("ssd_a"), sem("ssd_b")
        ssd_x, ssd_bcb, ssd_exp, ssd_m = (sem(n) for n in ("ssd_x", "ssd_bcb", "ssd_exp", "ssd_m"))
        ssd_h, ssd_y = sem("ssd_h"), sem("ssd_y")
        rope_done, rt_done, rt_ev = sem("rope_done"), sem("rt_done"), sem("rt_ev")
        gate_done, lam_s = sem("gate_done"), sem("lam_s")
        s_done = [sem(f"s_done{c}") for c in range(2)]
        mx_done = [sem(f"mx_done{c}") for c in range(2)]
        ex_done = [sem(f"ex_done{c}") for c in range(2)]
        comb_done, pt_done, pt_ev, pv_done, o_ev = (sem(n) for n in ("comb_done", "pt_done", "pt_ev", "pv_done", "o_ev"))
        resid_loaded = sem("resid_loaded")
        resid_done = sem("resid_done")
        ms_done, mmx_done, mex_done, mn_done = sem("ms_done"), sem("mmx_done"), sem("mex_done"), sem("mn_done")
        mt_done, mt_ev, mo_done, mo_hi, mo_lo = (sem(n) for n in ("mt_done", "mt_ev", "mo_done", "mo_hi", "mo_lo"))
        up_done, relu_done, sqv_done, sqh_done, ul_done = (
            sem(n) for n in ("up_done", "relu_done", "sqv_done", "sqh_done", "ul_done"))
        down_done, acc_done = sem("down_done"), sem("acc_done")
        stored = sem("stored")

        w_in = t["w_in"][0]
        cols = {"xbc": (w_in, COL_XBC), "v": (w_in, COL_V), "q": (w_in, COL_Q), "k": (w_in, COL_K),
                "z": (w_in, COL_Z), "mk": (t["w_mk"][0], 0), "mv": (t["w_mv"][0], 0),
                "wo": (t["w_out"][0], 0), "mq": (t["w_mq"][0], 0), "mo": (t["w_mo"][0], 0)}
        w_up, w_down = t["w_up"][0], t["w_down"][0]
        HALVES0 = 2 * N_UNITS
        NJ = FF // UC
        N_SMALL = 16 * 7

        def pow_cols(what, w=1):
            return stat[:, COL[what]:COL[what] + w], rms[:, COL[what]:COL[what] + w]

        def unit_source(name, u, half):
            w, c0 = cols[name]
            return w[half * 512:(half + 1) * 512, c0 + u * UC:c0 + (u + 1) * UC].rearrange("(k p) c -> p k c", p=P)

        def bank_free(eng, g):
            if g >= 3:
                name, s = STEPS[g - 3]
                eng.wait_ge(ev[name], s + 1)

        def split_at(name, s):
            if name in ("wo", "mo"):
                return [2 * UNIT0[name] + OUT_SPLIT[s]] if s in OUT_SPLIT else []
            per = PER_UNIT[name]
            u = UNIT0[name] + s // per
            r = s % per
            halves = []
            for half, when in ((0, 0), (1, per // 2)):
                if r == when:
                    halves.append(2 * (u + 1) + half)
            return [q for q in halves if u >= 1 and q < HALVES0 + 4]

        def unit_end(u):
            if u >= N_UNITS:
                m = u - N_UNITS
                if m == 0 or (m % 2 and m < 2 * NJ - 1):
                    return up_done, 4 * ((m + 1) // 2 + 1)
                return down_done, 16 * ((m - 2) // 2 + 1)
            name = [x for x, _, n in PROJ if n and UNIT0[x] <= u][-1]
            if name in ("wo", "mo"):
                return pj_done, STEP0[name] + OUT_UNIT_END[u - UNIT0[name]]
            return pj_done, STEP0[name] + (u - UNIT0[name] + 1) * PER_UNIT[name]

        block = ctx.enter_context(nc.Block())

        @block.sync
        def _(sp):
            def load_half(q, src):
                if q >= 2:
                    sp.wait_ge(w_lo, q - 1)
                sp.dma_start(raw[:, q % 2, :], src).then_inc(raw_loaded[q % 2], 16)

            def x_tile(i):
                if i >= 4:
                    sp.wait_ge(h_ready, i - 3)
                sp.dma_start(x_in[:, i % 4, :], t["x"][0][i * P:(i + 1) * P, :]).then_inc(x_loaded[i % 4], 16)

            for i in range(4):
                x_tile(i)
            q = 0
            for name, _, units in PROJ:
                for u in range(units):
                    for half in range(2):
                        if 0 < q < 3:
                            x_tile(2 * q + 2)
                            x_tile(2 * q + 3)
                        src = unit_source(name, u, half)
                        load_half(q, src)
                        q += 1
            for half in range(2):
                load_half(q, w_up[half * 512:(half + 1) * 512, 0:UC].rearrange("(k p) c -> p k c", p=P))
                q += 1
            with sp.Fori(0, NJ - 1) as j:
                for half in range(2):
                    sp.wait_ge(w_lo, j * 4 + (HALVES0 + 2 + half - 1))
                    sp.dma_start(raw[:, half, :], w_up[half * 512:(half + 1) * 512, bass.ts(j + 1, UC)]
                                 .rearrange("(k p) c -> p k c", p=P)).then_inc(raw_loaded[half], 16)
                for half in range(2):
                    sp.wait_ge(w_lo, j * 4 + (HALVES0 + 4 + half - 1))
                    sp.dma_start(raw[:, half, :], w_down[bass.ts(j * 2 + half, P), :]).then_inc(raw_loaded[half], 16)
            q += 4 * (NJ - 1)
            for half in range(2):
                load_half(q, w_down[(2 * (NJ - 1) + half) * P:(2 * (NJ - 1) + half + 1) * P, :])
                q += 1
            for i in range(NT):
                sp.wait_ge(resid_done, 2 * NT + i + 1)
                sp.dma_start(out[0][i * P:(i + 1) * P, :], resid[:, i, :]).then_inc(stored, 16)
            sp.wait_ge(stored, 16 * NT)

        @block.gpsimd
        def _(pool):
            g = nc.gpsimd
            g.memset(ident[:], 0.0).then_inc(pool_c, 1)
            g.memset(ident_b[:], 0.0).then_inc(pool_c, 1)
            g.memset(tri[:], 1.0).then_inc(pool_c, 1)
            g.memset(mask_q[:], 0.0).then_inc(pool_c, 1)
            g.memset(mask_s[:], 0.0).then_inc(pool_c, 1)
            g.memset(ones[:], 1.0).then_inc(consts_ready, 1)
            g.memset(mhalf[:], -0.5).then_inc(pool_c, 1)
            pool.wait_ge(pool_c, 6)
            for m in (ident, ident_b):
                g.affine_select(out=m[:], in_=m[:], compare_op=ALU.not_equal, fill=1.0, base=0,
                                pattern=[[-1, P]], channel_multiplier=1).then_inc(consts_ready, 1)
            g.affine_select(out=tri[:], in_=tri[:], compare_op=ALU.is_ge, fill=0.0, base=0,
                            pattern=[[1, P]], channel_multiplier=-1).then_inc(consts_ready, 1)
            g.affine_select(out=mask_q[:], in_=mask_q[:], compare_op=ALU.is_ge, fill=NEG, base=0,
                            pattern=[[-1, P]], channel_multiplier=1).then_inc(consts_ready, 1)
            g.affine_select(out=mask_s[:], in_=mask_s[:], compare_op=ALU.is_ge, fill=NEG, base=0,
                            pattern=[[0, 4], [1, P]], channel_multiplier=-1).then_inc(consts_ready, 1)

            def pow_step(what):
                w = 4 if what[0] == "o" else 1
                pool.wait_ge(ms_ready, POW[what] + 1)
                src, dst = pow_cols(what, w)
                g.tensor_tensor(dst, src, mhalf[:, 0:w], ALU.pow).then_inc(rms_ready, 1)

            for what in POWS[:1]:
                pow_step(what)
            for i in range(HALF_DIM):
                g.memset(inv[:, i:i + 1], float(np.float32(THETA) ** np.float32(-i / HALF_DIM))).then_inc(consts_ready, 1)
            g.memset(half_pi[:], math.pi / 2).then_inc(consts_ready, 1)
            for b in range(2):
                g.memset(xpre[:, b, 0:3], 0.0).then_inc(consts_ready, 1)
            for what in POWS[1:]:
                if what == ("down", 0):
                    pool.wait_ge(resid_done, 2 * NT)
                    g.memset(proj_out[:], 0.0).then_inc(acc_done, 4)
                pow_step(what)

        ALL_CONSTS = 6 + HALF_DIM + 3

        @block.scalar
        def _(act):
            s = nc.scalar
            n_av = [0]

            def after(ins):
                n_av[0] += 1
                ins.then_inc(av, 1)
                act.wait_ge(av, n_av[0])

            def slot_free(u):
                if u >= 2:
                    sem_of, n = unit_end(u - 2)
                    act.wait_ge(sem_of, n)

            def split_hi(q):
                act.wait_ge(raw_loaded[q % 2], 16 * (q // 2 + 1))
                slot_free(q // 2)
                s.activation(wh[:, (q // 2) % 2, (q % 2) * 1024:(q % 2 + 1) * 1024], raw[:, q % 2, :],
                             ACT.Copy).then_inc(w_hi, 1)

            def square(what, src, dst, scale=1.0):
                n = sum(1 for x in POWS[:POW[what]] if x[0] != "o")
                if n:
                    act.wait_ge(sq_done, n)
                s.activation(dst, src, ACT.Square, scale=scale, accum_out=stat[:, COL[what]:COL[what] + 1]).then_inc(sq_done, 1)

            def tr_hi(n, dst):
                for b in range(2):
                    act.wait_ge(tr_done, 2 * n + b + 1)
                    s.activation(dst[:, 4 * b:4 * b + 4], ps[:, 4 + 2 * (n % 2) + b, :].rearrange("p (k c) -> p k c", k=4),
                                 ACT.Copy).then_inc(hi_done, 1)

            rows = lambda a: a.partition_broadcast(P)
            act.dma_start(gain_b[:], rows(t["norm_mix_pre"][0:1, :])).then_inc(gain_b_loaded, 16)
            act.dma_start(pos_i[0:NT, :], t["positions"][0].rearrange("(i p) -> i p", p=P)).then_inc(rows_loaded, 16)
            act.dma_start(conv_rows[0:4 * KD, :], t["conv_w"][0, :, 0].rearrange("w (m p) -> (w m) p", p=P)
                          ).then_inc(rows_loaded, 16)
            act.dma_start(conv_rows[4 * KD:5 * KD, :], t["conv_b"][0].rearrange("(m p) -> m p", p=P)
                          ).then_inc(rows_loaded, 16)
            act.dma_start(wdt[:], w_in[:, COL_DT:COL_DT + SSD_H].rearrange("(k p) c -> p k c", p=P),
                          allow_slow_non_contiguous=True).then_inc(wdt_loaded, 16)
            for n, name in enumerate(("dt_bias", "a_log", "d_skip")):
                act.dma_start(heads8[:, n, :], rows(t[name][0:1, :])).then_inc(small_loaded, 16)
            for n, name in enumerate(("lambda_q1", "lambda_q2", "lambda_k1", "lambda_k2")):
                act.dma_start(lam4[:, n, :], rows(t[name][0:1, :])).then_inc(small_loaded, 16)
            act.dma_start(ssd_w[:], rows(t["ssd_norm_w"][0:1, :])).then_inc(gain_a_loaded, 16)
            act.dma_start(sub_w[:], rows(t["subln_w"][0:1, :])).then_inc(gain_a_loaded, 16)

            for i in range(NT + 2):
                if i < NT:
                    act.wait_ge(x_loaded[i % 4], 16 * (i // 4 + 1))
                    square(("in", i), x_in[:, i % 4, :], junk[:])
                if i >= 2:
                    tr_hi(TR_IN + i - 2, oph[:, :, (i - 2) * P:(i - 1) * P])
                if 2 <= i < 6:
                    split_hi(i - 2)
            act.wait_ge(wdt_loaded, 16)
            s.activation(wdt_h[:, 0:KD * SSD_H], wdt[:].rearrange("p k c -> p (k c)"), ACT.Copy).then_inc(wdt_hi, 1)
            s.activation(wdt_h[:, KD * SSD_H:], ones[:], ACT.Copy).then_inc(wdt_hi, 1)

            act.wait_ge(rope_r, 1)
            act.wait_ge(consts_ready, ALL_CONSTS)
            s.activation(sin_t[:], rope_t[:, 0], ACT.Sin).then_inc(rope_sin, 1)
            s.activation(nsin_t[:], rope_t[:, 0], ACT.Sin, scale=-1.0).then_inc(rope_sin, 1)
            after(s.activation(rope_t[:, 1], rope_t[:, 0], ACT.Abs))
            s.activation(cos_t[:], rope_t[:, 1], ACT.Sin, scale=-1.0, bias=half_pi[:]).then_inc(rope_sin, 1)

            def silu(m):
                act.wait_ge(conv_done, m + 1)
                s.activation(mix[:, m, :], mix[:, m, :], ACT.Silu).then_inc(silu_done, 1)

            for st in range(16):
                m, half = XBC_ORDER[st]
                g = STEP0["xbc"] + st
                act.wait_ge(pj_done, g + 1)
                if m >= 2:
                    act.wait_ge(conv_done, m - 1)
                s.activation(xpre[:, m % 2, 3 + half * 512:3 + (half + 1) * 512], ps[:, g % 3, :],
                             ACT.Copy).then_inc(ev["xbc"], 1)
                for q in split_at("xbc", st):
                    split_hi(q)
                if st >= 4 and st % 2:
                    silu(st // 2 - 2)

            for half in range(2):
                g = STEP0["dt"] + half
                act.wait_ge(pj_done, g + 1)
                s.activation(dt_rows[0:SSD_H, half * 512:(half + 1) * 512], ps[0:SSD_H, g % 3, :], ACT.Copy).then_inc(ev["dt"], 1)
            silu(6)
            silu(7)
            act.wait_ge(small_loaded, N_SMALL)
            act.wait_ge(dt_v, 1)
            after(s.activation(dts[1][:], dts[0][:], ACT.Abs))
            s.activation(dts[2][:], dts[1][:], ACT.Exp, scale=-1.0).then_inc(dt_s, 1)
            act.wait_ge(dt_v, 2)
            s.activation(dts[4][:], dts[3][:], ACT.Ln).then_inc(dt_s, 1)
            s.activation(heads8[:, 1, :], heads8[:, 1, :], ACT.Exp).then_inc(dt_s, 1)
            act.wait_ge(lam_s, 1)
            s.activation(lam[:, 2:4], lam[:, 0:2], ACT.Exp).then_inc(dt_s, 1)
            act.wait_ge(dt_v, 3)
            s.activation(dts[4][:], dts[5][:], ACT.Exp).then_inc(dt_s, 1)
            s.activation(dts[7][:], dts[6][:], ACT.Exp).then_inc(dt_s, 1)
            s.activation(dts[8][:], dts[2][:], ACT.Exp).then_inc(dt_s, 1)

            def ssd_act(c):
                act.wait_ge(ssd_a, c + 1)
                if c:
                    act.wait_ge(ssd_m, c)
                    act.wait_ge(ssd_b, c)
                s.activation(b_cb[:], ps[:, 5, :].rearrange("p (k c) -> p k c", k=4), ACT.Copy).then_inc(ssd_bcb, 1)
                both = ps[:, 6:8, :].rearrange("p b (h l) -> p (b h) l", h=4)
                for h in range(SSD_H):
                    ins = s.activation(decay[:, h, :], both[:, h, :], ACT.Exp, bias=ncum[:, c, h:h + 1])
                ins.then_inc(ssd_exp, 1)

            def rope_evac(st, name):
                dst, base_n = (qt, 0) if name == "q" else (kt, 16)
                u, i = st // NT, st % NT
                act.wait_ge(rt_done, base_n + st + 1)
                s.activation(dst[:, 2 * u:2 * u + 2, i * P:(i + 1) * P],
                             ps[:, 3, 0:UC].rearrange("p (k c) -> p k c", k=2), ACT.Copy,
                             scale=0.125 if name == "q" else 1.0).then_inc(rt_ev, 1)

            for n in range(66):
                name, st = STEPS[STEP0["v"] + n] if n < 64 else (None, 0)
                g = STEP0["v"] + n
                if name == "v":
                    u, i = st // NT, st % NT
                    act.wait_ge(pj_done, g + 1)
                    s.activation(vt[:, i, u * UC:(u + 1) * UC], ps[:, g % 3, 0:UC], ACT.Copy).then_inc(ev["v"], 1)
                if name == "z":
                    act.wait_ge(pj_done, g + 1)
                    if st >= 2:
                        act.wait_ge(gate_done, st - 1)
                    elif st == 0:
                        act.wait_ge(ssd_b, NT)
                    s.activation(silu_z[:, st % 2, :], ps[:, g % 3, 0:UC], ACT.Silu).then_inc(ev["z"], 1)
                if name:
                    for q in split_at(name, st):
                        split_hi(q)
                if n in SSD_FIRST:
                    ssd_act(SSD_FIRST[n])
                if 16 <= n - 2 < 48:
                    rope_evac((n - 18) % 16, "q" if n - 2 < 32 else "k")
            for i in range(NT):
                act.wait_ge(gate_done, NT + i + 1)
                square(("y", i), mix[:, 0:4, i * P:(i + 1) * P], junk[:, 0:512].rearrange("p (k c) -> p k c", k=4))

            steps = [(i, h) for i in range(NT) for h in range(DH)]
            NS = len(steps)

            def attn_exp(n, c):
                keys = (steps[n][0] + 1) * P
                act.wait_ge(mx_done[c], n + 1)
                if n >= 2:
                    act.wait_ge(comb_done, n - 1) if c else act.wait_ge(pt_done, n - 1)
                src = ps[:, 2 * c:2 * c + 2, :].rearrange("p b k -> p (b k)")
                s.activation(probs[:, n % 2, c, 0:keys], src[:, 0:keys], ACT.Exp, bias=nmax[:, n % 2, c:c + 1],
                             accum_out=sums[:, n % 4, c:c + 1]).then_inc(ex_done[c], 1)

            act.wait_ge(pj_done, STEP0["z"] + 16)
            for n in range(NS + 3):
                if n < NS:
                    attn_exp(n, 0)
                    attn_exp(n, 1)
                if n >= 1 and n - 1 < NS:
                    k = n - 1
                    i = steps[k][0]
                    act.wait_ge(pt_done, k + 1)
                    if k >= 2:
                        act.wait_ge(pv_done, k - 1)
                    src = ps[:, 4:6, :].rearrange("p b k -> p (b k)")
                    s.activation(probs_t[:, k % 2, 0:i + 1, :].rearrange("p b k -> p (b k)"), src[:, 0:(i + 1) * P],
                                 ACT.Copy).then_inc(pt_ev, 1)
                if n >= 2 and n - 2 < NS:
                    k = n - 2
                    i, h = steps[k]
                    act.wait_ge(pv_done, k + 1)
                    o = ps[:, 6 + k % 2, 0:P]
                    s.activation(mix[:, 4 + h, i * P:(i + 1) * P], o, ACT.Copy, scale=recs[:, k % 4, 0:1])
                    if k >= 4:
                        act.wait_ge(o_ev, k - 3)
                    elif k == 0:
                        act.wait_ge(sq_done, 2 * NT)
                    s.activation(junk[:, (k % 4) * P:(k % 4 + 1) * P], o, ACT.Square, scale=recs[:, k % 4, 0:1],
                                 accum_out=stat[:, COL[("o", i)] + h:COL[("o", i)] + h + 1]).then_inc(o_ev, 1)

            for i in range(NT):
                tr_hi(TR_MIX + i, oph[:, :, i * P:(i + 1) * P])
            act.wait_ge(tr_done, 2 * (TR_MIX + NT))
            for i in range(NT):
                act.dma_start(resid[:, i, :], t["x"][0][i * P:(i + 1) * P, :]).then_inc(resid_loaded, 16)
            for i in range(MT):
                act.dma_start(m_in[:, i, :], t["mem"][0][i * P:(i + 1) * P, :]).then_inc(x_loaded[i], 16)
            act.wait_ge(h_ready, TR_MIX)
            act.dma_start(gain_b[:], rows(t["norm_mem_kv"][0:1, :])).then_inc(gain_b_loaded, 16)
            act.dma_start(gain_a[:], rows(t["norm_mix_post"][0:1, :])).then_inc(gain_a_loaded, 16)
            for i in range(MT):
                act.wait_ge(x_loaded[i], 16 * 3)
                act.wait_ge(o_ev, NS)
                square(("mem", i), m_in[:, i, :], junk[:])
            for i in range(MT):
                tr_hi(TR_MEM + i, memh[:, :, i * P:(i + 1) * P])
            act.wait_ge(h_ready, TR_MEM + MT)
            act.dma_start(gain_b[:], rows(t["norm_mem_q"][0:1, :])).then_inc(gain_b_loaded, 16)

            for st in range(8):
                g = STEP0["mk"] + st
                act.wait_ge(pj_done, g + 1)
                s.activation(kmt[:, st, :], ps[:, g % 3, 0:MEM], ACT.Copy).then_inc(ev["mk"], 1)
                for q in split_at("mk", st):
                    split_hi(q)
            for st in range(8):
                u, i = st // MT, st % MT
                g = STEP0["mv"] + st
                act.wait_ge(pj_done, g + 1)
                s.activation(vm[:, i, u * UC:(u + 1) * UC], ps[:, g % 3, 0:UC], ACT.Copy).then_inc(ev["mv"], 1)
                for q in split_at("mv", st):
                    split_hi(q)

            def out_proj(name, nxt, tr0):
                st = 0
                for k in range(NT + 3):
                    while k < NT and st <= OUT_COMPLETE[k]:
                        u, i = OUT_ORDER[st]
                        g = STEP0[name] + st
                        act.wait_ge(pj_done, g + 1)
                        s.activation(proj_out[:, i, u * UC:(u + 1) * UC], ps[:, g % 3, 0:UC], ACT.Copy).then_inc(ev[name], 1)
                        for q in split_at(name, st):
                            split_hi(q)
                        st += 1
                    if k < NT:
                        act.wait_ge(ev[name], st)
                        square((name, k), proj_out[:, k, :], junk[:])
                    if k >= 3:
                        tr_hi(tr0 + k - 3, oph[:, :, (k - 3) * P:(k - 2) * P])
                    if 1 <= k <= NT:
                        act.wait_ge(resid_done, (0 if name == "wo" else NT) + k)
                        square((nxt, k - 1), resid[:, k - 1, :], junk[:])

            out_proj("wo", "q", TR_Q)
            act.wait_ge(h_ready, TR_Q + NT)
            act.dma_start(gain_a[:], rows(t["norm_mem_post"][0:1, :])).then_inc(gain_a_loaded, 16)
            act.dma_start(gain_b[:], rows(t["norm_mlp_pre"][0:1, :])).then_inc(gain_b_loaded, 16)

            for st in range(16):
                f, half = XBC_ORDER[st]
                g = STEP0["mq"] + st
                act.wait_ge(pj_done, g + 1)
                s.activation(qct[:, f, half * 512:(half + 1) * 512], ps[:, g % 3, :], ACT.Copy,
                             scale=0.0625).then_inc(ev["mq"], 1)
                for q in split_at("mq", st):
                    split_hi(q)

            for n in range(NT + 2):
                if n < NT:
                    act.wait_ge(mmx_done, n + 1)
                    if n >= 2:
                        act.wait_ge(mt_done, n - 1)
                    src = ps[:, 2 * (n % 2):2 * (n % 2) + 2, :].rearrange("p b (h m) -> p (b h) m", h=2)
                    for h in range(MH):
                        ins = s.activation(mprobs[:, n % 2, h, :], src[:, h, :], ACT.Exp, bias=mmax[:, n % 2, h:h + 1],
                                           accum_out=msum[:, n % 2, h:h + 1])
                    ins.then_inc(mex_done, 1)
                if 1 <= n <= NT:
                    k = n - 1
                    act.wait_ge(mt_done, k + 1)
                    if k >= 2:
                        act.wait_ge(mo_done, k - 1)
                    s.activation(mprobs_t[:, k % 2], ps[:, 4:6, :].rearrange("p b (h m) -> p (b h) m", h=4),
                                 ACT.Copy).then_inc(mt_ev, 1)
                if n >= 2:
                    k = n - 2
                    act.wait_ge(mo_done, k + 1)
                    s.activation(oph[:, :, k * P:(k + 1) * P], ps[:, 6:8, :].rearrange("p b (h m) -> p (b h) m", h=4),
                                 ACT.Copy).then_inc(mo_hi, 1)

            out_proj("mo", "mlp", TR_MLP)
            act.wait_ge(h_ready, TR_MLP + NT)
            act.dma_start(gain_a[:], rows(t["norm_mlp_post"][0:1, :])).then_inc(gain_a_loaded, 16)

            def relu_sq(done, sq_free, st, par):
                f, half = st % 2, st // 2
                act.wait_ge(up_done, done)
                if sq_free is not None:
                    act.wait_ge(sqv_done, sq_free)
                s.activation(relu_u[:, st % 2, :], ps[:, st, :], ACT.Relu).then_inc(relu_done, 1)
                act.wait_ge(relu_done, done)
                s.activation(uh[:, par, f, half * 512:(half + 1) * 512], relu_u[:, st % 2, :],
                             ACT.Square).then_inc(sqh_done, 1)

            for half in range(2):
                split_hi(2 * (N_UNITS + 1) + half)
            for st in range(4):
                relu_sq(st + 1, st - 1 if st >= 2 else None, st, 0)
            with act.Fori(0, (NJ - 2) // 2) as jj:
                for r in range(2):
                    act.wait_ge(up_done, jj * 8 + (4 * r + 5))
                    for half in range(2):
                        act.wait_ge(raw_loaded[half], jj * 64 + 16 * (N_UNITS + 2 * r + 3))
                        s.activation(wh[:, 0, half * 1024:(half + 1) * 1024], raw[:, half, :], ACT.Copy).then_inc(w_hi, 1)
                    for st in range(4):
                        relu_sq(jj * 8 + (4 * r + st + 5), jj * 8 + (4 * r + st + 3), st, (r + 1) % 2)
                    for half in range(2):
                        act.wait_ge(raw_loaded[half], jj * 64 + 16 * (N_UNITS + 2 * r + 4))
                        s.activation(wh[:, 1, half * 1024:(half + 1) * 1024], raw[:, half, :], ACT.Copy).then_inc(w_hi, 1)
            for half in range(2):
                split_hi(2 * (N_UNITS + 2 * NJ - 2) + half)
            for st in range(4):
                relu_sq(4 * (NJ - 1) + st + 1, 4 * (NJ - 1) + st - 1, st, 1)
            for half in range(2):
                split_hi(2 * (N_UNITS + 2 * NJ - 1) + half)
            act.wait_ge(sqv_done, 4 * NJ)
            for i in range(NT):
                act.wait_ge(acc_done, 4 + 16 * (NJ - 1) + 2 * i + 2)
                square(("down", i), proj_out[:, i, :], junk2[:])

        @block.vector
        def _(dve):
            v = nc.vector
            n_dv = [0]

            def after(ins):
                n_dv[0] += 1
                ins.then_inc(dv, 1)
                dve.wait_ge(dv, n_dv[0])

            def split_lo(q):
                dve.wait_ge(w_hi, q + 1)
                part = (slice(None), (q // 2) % 2, slice((q % 2) * 1024, (q % 2 + 1) * 1024))
                v.tensor_tensor(wl[part], raw[:, q % 2, :], wh[part].bitcast(F32), ALU.subtract).then_inc(w_lo, 1)

            def mean(what, n, w=1):
                c = stat[:, COL[what]:COL[what] + w]
                v.tensor_scalar(c, c, 1.0 / n, EPS, ALU.mult, ALU.add).then_inc(ms_ready, 1)

            def squares(what):
                dve.wait_ge(sq_done, sum(1 for x in POWS[:POW[what] + 1] if x[0] != "o"))

            def tr_lo(n, dst_h, dst_l):
                for b in range(2):
                    dve.wait_ge(hi_done, 2 * n + b + 1)
                    v.tensor_tensor(dst_l[:, 4 * b:4 * b + 4],
                                    ps[:, 4 + 2 * (n % 2) + b, :].rearrange("p (k c) -> p k c", k=4),
                                    dst_h[:, 4 * b:4 * b + 4].bitcast(F32), ALU.subtract).then_inc(lo_done, 1)

            def normalise(what, n, src, gain, dst):
                dve.wait_ge(rms_ready, POW[what] + 1)
                v.scalar_tensor_tensor(dst, src, rms[:, COL[what]:COL[what] + 1], gain, ALU.mult, ALU.mult).then_inc(h_ready, 1)

            dve.wait_ge(rows_loaded, 48)
            v.tensor_copy(pos_rows[0:NT, :], pos_i[0:NT, :]).then_inc(pos_ready, 1)
            for i in range(NT + 3):
                if i < NT:
                    squares(("in", i))
                    mean(("in", i), D)
                if 1 <= i <= NT:
                    if i - 1 >= 2:
                        dve.wait_ge(tr_done, 2 * (i - 2))
                    if i == 1:
                        dve.wait_ge(gain_b_loaded, 16)
                    normalise(("in", i - 1), i - 1, x_in[:, (i - 1) % 4, :], gain_b[:], h_in[:, (i - 1) % 2, :])
                if i >= 3:
                    k = i - 3
                    tr_lo(k, oph[:, :, k * P:(k + 1) * P], opl[:, :, k * P:(k + 1) * P])
                if 3 <= i < 7:
                    split_lo(i - 3)
            dve.wait_ge(wdt_hi, 2)
            v.tensor_tensor(wdt_l[:, 0:KD * SSD_H], wdt[:].rearrange("p k c -> p (k c)"),
                            wdt_h[:, 0:KD * SSD_H].bitcast(F32), ALU.subtract).then_inc(wdt_lo, 1)
            v.tensor_tensor(wdt_l[:, KD * SSD_H:], ones[:], wdt_h[:, KD * SSD_H:].bitcast(F32), ALU.subtract).then_inc(wdt_lo, 1)

            dve.wait_ge(consts_ready, ALL_CONSTS)
            ang, turns = rope_t[:, 0], rope_t[:, 2]
            dve.wait_ge(rows_tr, 1)
            v.tensor_copy(conv_wb[:], ps[:, 3, 0:5 * KD].rearrange("p (w m) -> p w m", w=5)).then_inc(rows_tr, 1)
            after(v.tensor_tensor(ang, ps[:, 3, 64:64 + NT].unsqueeze(2).to_broadcast([P, NT, HALF_DIM]),
                                  inv[:].unsqueeze(1).to_broadcast([P, NT, HALF_DIM]), ALU.mult))
            after(v.tensor_scalar(turns, ang, 1.0 / (2 * math.pi), None, ALU.mult))
            after(v.tensor_scalar(turns, turns, ROUND, None, ALU.add))
            after(v.tensor_scalar(turns, turns, -ROUND, None, ALU.add))
            for part in (TWO_PI_A, TWO_PI_B, TWO_PI_C):
                after(v.scalar_tensor_tensor(ang, turns, -part, ang, ALU.mult, ALU.add))
            v.tensor_scalar(ang, ang, PI_SAFE, -PI_SAFE, ALU.min, ALU.max).then_inc(rope_r, 1)

            dve.wait_ge(small_loaded, N_SMALL)
            after(v.tensor_tensor(lam4[:, 0:2, :], lam4[:, 0:2, :], lam4[:, 2:4, :], ALU.mult))
            v.tensor_reduce(lam[:, 0:2], lam4[:, 0:2, :], AX.X, ALU.add).then_inc(lam_s, 1)
            dve.wait_ge(gain_a_loaded, 32)
            v.tensor_scalar(sub_w[:], sub_w[:], 1.0 - LAMBDA_INIT, None, ALU.mult)

            dve.wait_ge(rows_tr, 2)

            def conv(m, st):
                dve.wait_ge(ev["xbc"], st + 1)
                x = xpre[:, m % 2, :]
                after(v.tensor_scalar(mix[:, m, :], x[:, 3:3 + T], conv_wb[:, 3, m:m + 1], conv_wb[:, 4, m:m + 1], ALU.mult, ALU.add))
                for w in (2, 1):
                    after(v.scalar_tensor_tensor(mix[:, m, :], x[:, w:w + T], conv_wb[:, w, m:m + 1], mix[:, m, :],
                                                 ALU.mult, ALU.add))
                v.scalar_tensor_tensor(mix[:, m, :], x[:, 0:T], conv_wb[:, 0, m:m + 1], mix[:, m, :],
                                       ALU.mult, ALU.add).then_inc(conv_done, 1)

            for st in range(16):
                for q in split_at("xbc", st):
                    split_lo(q)
                if st in XBC_CONV:
                    conv(XBC_CONV[st], st)

            dve.wait_ge(dt_tr, 1)
            after(v.tensor_tensor(dts[0][:], ps[:, 3, 0:64].rearrange("p (c h) -> p c h", h=SSD_H),
                                  heads8[:, 0, :].unsqueeze(1).to_broadcast([P, NT, SSD_H]), ALU.add))
            v.tensor_scalar(dts[3][:], dts[0][:], 0.0, None, ALU.max).then_inc(dt_v, 1)

            dve.wait_ge(dt_s, 1)
            after(v.tensor_scalar(dts[5][:], dts[3][:], 0.0, None, ALU.add))
            after(v.tensor_scalar(dts[3][:], dts[2][:], 1.0, None, ALU.add))
            v.tensor_scalar(dts[6][:], dts[3][:], -1.0, None, ALU.add).then_inc(dt_v, 1)
            dve.wait_ge(dt_v, 2)
            after(v.tensor_scalar(dts[7][:], dts[6][:], 1e-30, None, ALU.max))
            after(v.reciprocal(dts[7][:], dts[7][:]))
            after(v.tensor_tensor(dts[7][:], dts[7][:], dts[2][:], ALU.mult))
            dve.wait_ge(dt_s, 3)
            after(v.tensor_tensor(dts[7][:], dts[7][:], dts[4][:], ALU.mult))
            after(v.scalar_tensor_tensor(dts[8][:], dts[6][:], 0.0, dts[2][:], ALU.is_equal, ALU.mult))
            after(v.tensor_tensor(dts[7][:], dts[7][:], dts[8][:], ALU.add))
            after(v.tensor_tensor(dts[0][:], dts[7][:], dts[5][:], ALU.add))
            v.scalar_tensor_tensor(dts[1][:], dts[0][:], -1.0,
                                   heads8[:, 1, :].unsqueeze(1).to_broadcast([P, NT, SSD_H]),
                                   ALU.mult, ALU.mult).then_inc(da_ready, 1)
            dve.wait_ge(cum_done, 1)
            cum, end = dts[5], dts[6]
            v.tensor_copy(cum[:], ps[:, 4, 0:64].rearrange("p (c h) -> p c h", h=SSD_H)).then_inc(dv, 1)
            v.tensor_copy(end[:], ps[:, 4, 64:128].rearrange("p (c h) -> p c h", h=SSD_H)).then_inc(dv, 1)
            n_dv[0] += 2
            dve.wait_ge(dv, n_dv[0])
            after(v.tensor_scalar(ncum[:], cum[:], -1.0, None, ALU.mult))
            v.tensor_tensor(dts[2][:], end[:], cum[:], ALU.subtract).then_inc(dt_v, 1)
            dve.wait_ge(dt_s, 7)
            after(v.tensor_tensor(lam[:, 4:5], lam[:, 3:4], lam[:, 2:3], ALU.subtract))
            after(v.tensor_scalar(lam[:, 4:5], lam[:, 4:5], -LAMBDA_INIT, None, ALU.add))
            dt, e_cum, e_end, dt_end = dts[0], dts[4], dts[7], dts[2]
            after(v.tensor_tensor(dt_end[:], dt[:], dts[8][:], ALU.mult))

            def heads(a):
                return a.rearrange("p (h c) -> p h c", h=SSD_H)

            def spread(a, c):
                return a[:, c, :].unsqueeze(2).to_broadcast([P, SSD_H, 64])

            def ssd_first(c):
                dve.wait_ge(ssd_a, c + 1)
                if c:
                    dve.wait_ge(ssd_b, c)
                xs = heads(ps[:, 4, :])
                v.tensor_tensor(heads(xdt[:]), xs, spread(dt, c), ALU.mult).then_inc(ssd_x, 1)
                v.tensor_tensor(heads(xdt_end[:]), xs, spread(dt_end, c), ALU.mult).then_inc(ssd_x, 1)
                v.tensor_tensor(heads(x_skip[:]), xs, heads8[:, 2, :].unsqueeze(2).to_broadcast([P, SSD_H, 64]),
                                ALU.mult).then_inc(ssd_x, 1)

            def ssd_mid(c):
                dve.wait_ge(ssd_exp, c + 1)
                dve.wait_ge(ssd_bcb, c + 1)
                for gr in range(2):
                    ins = v.tensor_tensor(cb_decay[:, 4 * gr:4 * gr + 4, :], decay[:, 4 * gr:4 * gr + 4, :],
                                          b_cb[:, 2 + gr, :].unsqueeze(1).to_broadcast([P, 4, P]), ALU.mult)
                ins.then_inc(ssd_m, 1)

            def ssd_last(c):
                dve.wait_ge(ssd_b, c + 1)
                if c:
                    after(v.tensor_tensor(heads(y_off[:]), heads(ps[:, 7, :]), spread(e_cum, c), ALU.mult))
                    after(v.tensor_tensor(x_skip[:], x_skip[:], y_off[:], ALU.add))
                    after(v.tensor_tensor(heads(state[:]), heads(state[:]), spread(e_end, c), ALU.mult))
                    v.tensor_tensor(state[:], state[:], ps[:, 6, :], ALU.add).then_inc(ssd_h, 1)
                else:
                    v.tensor_copy(state[:], ps[:, 6, :]).then_inc(ssd_h, 1)
                dve.wait_ge(ssd_x, 3 * c + 3)
                v.tensor_tensor(mix[:, 0:4, c * P:(c + 1) * P], ps[:, 4, :].rearrange("p (k c) -> p k c", k=4),
                                x_skip[:].rearrange("p (k c) -> p k c", k=4), ALU.add).then_inc(ssd_y, 1)

            def rope(st, name, g):
                i = st % NT
                n = st + (16 if name == "k" else 0)
                dve.wait_ge(pj_done, g + 1)
                if n == 0:
                    dve.wait_ge(rope_sin, 3)
                if n >= 2:
                    dve.wait_ge(rt_done, n - 1)
                src = ps[:, g % 3, 0:UC].rearrange("p (a h c) -> p a h c", a=4, h=2)
                dst = roped[:, n % 2, :].rearrange("p (a h c) -> p a h c", a=4, h=2)
                tmp = rope_b[:].rearrange("p (a h c) -> p a h c", a=4, h=2)
                spread_t = lambda tab: tab[:, i, :].unsqueeze(1).to_broadcast([P, 4, HALF_DIM])
                for h in range(2):
                    v.tensor_tensor(dst[:, :, h, :], src[:, :, h, :], spread_t(cos_t), ALU.mult)
                if n:
                    dve.wait_ge(rope_done, n)
                v.tensor_tensor(tmp[:, :, 0, :], src[:, :, 1, :], spread_t(nsin_t), ALU.mult)
                v.tensor_tensor(tmp[:, :, 1, :], src[:, :, 0, :], spread_t(sin_t), ALU.mult).then_inc(ev[name], 1)
                dve.wait_ge(ev[name], st + 1)
                v.tensor_tensor(roped[:, n % 2, :], roped[:, n % 2, :], rope_b[:], ALU.add).then_inc(rope_done, 1)

            for n in range(64):
                name, st = STEPS[STEP0["v"] + n]
                if name in ("q", "k"):
                    rope(st, name, STEP0["v"] + n)
                if name == "z":
                    u, i = st // NT, st % NT
                    dve.wait_ge(ev["z"], st + 1)
                    if st == 0:
                        dve.wait_ge(ssd_y, NT)
                    y = mix[:, 2 * u:2 * u + 2, i * P:(i + 1) * P]
                    v.tensor_tensor(y, y, silu_z[:, st % 2, :].rearrange("p (k c) -> p k c", k=2), ALU.mult).then_inc(gate_done, 1)
                for q in split_at(name, st):
                    split_lo(q)
                if n in SSD_FIRST:
                    ssd_first(SSD_FIRST[n])
                if n in SSD_MID:
                    ssd_mid(SSD_MID[n])
                if n in SSD_LAST:
                    ssd_last(SSD_LAST[n])

            for i in range(NT):
                squares(("y", i))
                mean(("y", i), D_SSD)
            for i in range(NT):
                dve.wait_ge(rms_ready, POW[("y", i)] + 1)
                y = mix[:, 0:4, i * P:(i + 1) * P]
                v.scalar_tensor_tensor(y, y, rms[:, COL[("y", i)]:COL[("y", i)] + 1], ssd_w[:].rearrange("p (k c) -> p k c", k=4),
                                       ALU.mult, ALU.mult)

            steps = [(i, h) for i in range(NT) for h in range(DH)]
            NS = len(steps)

            def attn_max(n, c):
                keys = (steps[n][0] + 1) * P
                dve.wait_ge(s_done[c], n + 1)
                if n >= 2:
                    dve.wait_ge(ex_done[c], n - 1)
                src = ps[:, 2 * c:2 * c + 2, :].rearrange("p b k -> p (b k)")
                v.tensor_reduce(nmax[:, n % 2, c:c + 1], src[:, 0:keys], AX.X, ALU.max, negate=True).then_inc(mx_done[c], 1)

            def attn_comb(n):
                keys = (steps[n][0] + 1) * P
                dve.wait_ge(ex_done[0], n + 1)
                dve.wait_ge(ex_done[1], n + 1)
                if n >= 4:
                    dve.wait_ge(o_ev, n - 3)
                after(v.reciprocal(recs[:, n % 4, :], sums[:, n % 4, :]))
                after(v.scalar_tensor_tensor(ratio[:, n % 2:n % 2 + 1], sums[:, n % 4, 0:1], recs[:, n % 4, 1:2],
                                             lam[:, 4:5], ALU.mult, ALU.mult))
                v.scalar_tensor_tensor(probs[:, n % 2, 0, 0:keys], probs[:, n % 2, 1, 0:keys], ratio[:, n % 2:n % 2 + 1],
                                       probs[:, n % 2, 0, 0:keys], ALU.mult, ALU.add).then_inc(comb_done, 1)

            for n in range(NS + 1):
                if n < NS:
                    attn_max(n, 0)
                if n >= 1:
                    attn_comb(n - 1)
                if n < NS:
                    attn_max(n, 1)
            for i in range(NT):
                dve.wait_ge(o_ev, DH * (i + 1))
                mean(("o", i), P, DH)
            for i in range(NT):
                dve.wait_ge(rms_ready, POW[("o", i)] + 1)
                for h in range(DH):
                    o = mix[:, 4 + h, i * P:(i + 1) * P]
                    ins = v.scalar_tensor_tensor(o, o, rms[:, COL[("o", i)] + h:COL[("o", i)] + h + 1], sub_w[:], ALU.mult, ALU.mult)
                ins.then_inc(h_ready, 1)
                if i:
                    tr_lo(TR_MIX + i - 1, oph[:, :, (i - 1) * P:i * P], opl[:, :, (i - 1) * P:i * P])
            tr_lo(TR_MIX + 7, oph[:, :, 7 * P:T], opl[:, :, 7 * P:T])

            for i in range(MT):
                squares(("mem", i))
                mean(("mem", i), D)
            dve.wait_ge(gain_b_loaded, 32)
            for i in range(MT):
                normalise(("mem", i), TR_MEM + i, m_in[:, i, :], gain_b[:], h_mem[:, i, :])
            for i in range(MT):
                tr_lo(TR_MEM + i, memh[:, :, i * P:(i + 1) * P], meml[:, :, i * P:(i + 1) * P])
            for name in ("mk", "mv"):
                for st in range(8):
                    for q in split_at(name, st):
                        split_lo(q)

            def out_proj(name, nxt, tr0):
                st = 0
                for k in range(NT + 3):
                    while k < NT and st <= OUT_COMPLETE[k]:
                        for q in split_at(name, st):
                            split_lo(q)
                        st += 1
                    if k < NT:
                        squares((name, k))
                        mean((name, k), D)
                    if 1 <= k <= NT:
                        i = k - 1
                        dve.wait_ge(rms_ready, POW[(name, i)] + 1)
                        if i == 0:
                            dve.wait_ge(gain_a_loaded, 48 if name == "wo" else 64)
                            dve.wait_ge(gain_b_loaded, 48 if name == "wo" else 64)
                            dve.wait_ge(resid_loaded, 16 * NT)
                        after(v.scalar_tensor_tensor(proj_out[:, i, :], proj_out[:, i, :], rms[:, COL[(name, i)]:COL[(name, i)] + 1],
                                                     gain_a[:], ALU.mult, ALU.mult))
                        v.tensor_tensor(resid[:, i, :], resid[:, i, :], proj_out[:, i, :], ALU.add).then_inc(resid_done, 1)
                    if 2 <= k <= NT + 1:
                        i = k - 2
                        if i >= 2:
                            dve.wait_ge(tr_done, 2 * (tr0 + i - 1))
                        normalise((nxt, i), tr0 + i, resid[:, i, :], gain_b[:], h_tok[:, i % 2, :])
                    if 1 <= k <= NT:
                        squares((nxt, k - 1))
                        mean((nxt, k - 1), D)
                    if k >= 3:
                        i = k - 3
                        tr_lo(tr0 + i, oph[:, :, i * P:(i + 1) * P], opl[:, :, i * P:(i + 1) * P])

            out_proj("wo", "q", TR_Q)
            for st in range(16):
                for q in split_at("mq", st):
                    split_lo(q)

            for n in range(NT + 3):
                if n >= 3:
                    k = n - 3
                    dve.wait_ge(mo_hi, k + 1)
                    v.tensor_tensor(opl[:, :, k * P:(k + 1) * P], ps[:, 6:8, :].rearrange("p b (h m) -> p (b h) m", h=4),
                                    oph[:, :, k * P:(k + 1) * P].bitcast(F32), ALU.subtract).then_inc(mo_lo, 1)
                if n < NT:
                    dve.wait_ge(ms_done, n + 1)
                    if n >= 2:
                        dve.wait_ge(mex_done, n - 1)
                    src = ps[:, 2 * (n % 2):2 * (n % 2) + 2, :].rearrange("p b (h m) -> p (b h) m", h=2)
                    v.tensor_reduce(mmax[:, n % 2, :], src, AX.X, ALU.max, negate=True).then_inc(mmx_done, 1)
                if 1 <= n <= NT:
                    k = n - 1
                    dve.wait_ge(mex_done, k + 1)
                    after(v.reciprocal(mrec[:, k % 2, :], msum[:, k % 2, :]))
                    v.tensor_tensor(mprobs[:, k % 2], mprobs[:, k % 2],
                                    mrec[:, k % 2, :].unsqueeze(2).to_broadcast([P, MH, MEM]), ALU.mult).then_inc(mn_done, 1)

            out_proj("mo", "mlp", TR_MLP)

            for half in range(2):
                split_lo(2 * (N_UNITS + 1) + half)

            def square_lo(j4, par, st):
                f, half = st % 2, st // 2
                dve.wait_ge(relu_done, j4 + (st + 1))
                v.tensor_tensor(sq_u[:, st % 2, :], relu_u[:, st % 2, :], relu_u[:, st % 2, :], ALU.mult).then_inc(sqv_done, 1)
                dve.wait_ge(sqv_done, j4 + (st + 1))
                dve.wait_ge(sqh_done, j4 + (st + 1))
                part = (slice(None), par, f, slice(half * 512, (half + 1) * 512))
                v.tensor_tensor(ul[part], sq_u[:, st % 2, :], uh[part].bitcast(F32), ALU.subtract).then_inc(ul_done, 1)

            def add_down(j16, n):
                i, ch = n // 2, n % 2
                dve.wait_ge(down_done, j16 + (n + 1))
                a = proj_out[:, i, ch * 512:(ch + 1) * 512]
                v.tensor_tensor(a, a, ps[:, 4 + n % 4, :], ALU.add).then_inc(acc_done, 1)

            def split_lo_mlp(count, slot, half):
                dve.wait_ge(w_hi, count)
                part = (slice(None), slot, slice(half * 1024, (half + 1) * 1024))
                v.tensor_tensor(wl[part], raw[:, half, :], wh[part].bitcast(F32), ALU.subtract).then_inc(w_lo, 1)

            for st in range(4):
                square_lo(0, 0, st)
            dve.wait_ge(acc_done, 4)
            with dve.Fori(0, (NJ - 2) // 2) as jj:
                for r in range(2):
                    for half in range(2):
                        split_lo_mlp(jj * 8 + (2 * (N_UNITS + 2 * r + 2) + half + 1), 0, half)
                    for st in range(4):
                        square_lo(jj * 8 + 4 * (r + 1), (r + 1) % 2, st)
                    for n in range(4):
                        add_down(jj * 32 + 16 * r, n)
                    for half in range(2):
                        split_lo_mlp(jj * 8 + (2 * (N_UNITS + 2 * r + 3) + half + 1), 1, half)
                    for n in range(4, 16):
                        add_down(jj * 32 + 16 * r, n)
            split_lo(2 * (N_UNITS + 2 * NJ - 2))
            split_lo(2 * (N_UNITS + 2 * NJ - 2) + 1)
            for st in range(4):
                square_lo(4 * (NJ - 1), 1, st)
            for n in range(4):
                add_down(16 * (NJ - 2), n)
            split_lo(2 * (N_UNITS + 2 * NJ - 1))
            split_lo(2 * (N_UNITS + 2 * NJ - 1) + 1)
            for n in range(4, 16):
                add_down(16 * (NJ - 2), n)
            for n in range(16):
                add_down(16 * (NJ - 1), n)
                if n == 0:
                    dve.wait_ge(gain_a_loaded, 80)
                if n % 2 and n >= 3:
                    i = n // 2 - 1
                    squares(("down", i))
                    mean(("down", i), D)
            squares(("down", NT - 1))
            mean(("down", NT - 1), D)
            for i in range(NT):
                dve.wait_ge(rms_ready, POW[("down", i)] + 1)
                after(v.scalar_tensor_tensor(proj_out[:, i, :], proj_out[:, i, :], rms[:, COL[("down", i)]:COL[("down", i)] + 1],
                                             gain_a[:], ALU.mult, ALU.mult))
                v.tensor_tensor(resid[:, i, :], resid[:, i, :], proj_out[:, i, :], ALU.add).then_inc(resid_done, 1)

        @block.tensor
        def _(pe):
            te = nc.tensor

            def three(o, lh, ll, rh, rl, first, last):
                te.matmul(o, lh, rh, start=first, stop=False)
                te.matmul(o, lh, rl, start=False, stop=False)
                return te.matmul(o, ll, rh, start=False, stop=last)

            def wcols(w, slot, k, c0=0, n=UC):
                return w[:, slot, k * UC + c0:k * UC + c0 + n]

            def unit_ready(u):
                pe.wait_ge(w_lo, 2 * u + 2)

            def token_step(name, st, lh, ll, tile, unit=None):
                g, u = STEP0[name] + st, UNIT0[name] + (st // PER_UNIT[name] if unit is None else unit)
                bank_free(pe, g)
                unit_ready(u)
                for k in range(KD):
                    ins = three(ps[:, g % 3, 0:UC], lh[:, k, tile * P:(tile + 1) * P], ll[:, k, tile * P:(tile + 1) * P],
                                wcols(wh, u % 2, k), wcols(wl, u % 2, k), k == 0, k == KD - 1)
                ins.then_inc(pj_done, 1)

            def feature_step(name, st, rh, rl, f, c0, n):
                per = PER_UNIT[name]
                g, u = STEP0[name] + st, UNIT0[name] + st // per
                bank_free(pe, g)
                unit_ready(u)
                for k in range(KD):
                    ins = three(ps[:, g % 3, 0:n], wcols(wh, u % 2, k, f * P, P), wcols(wl, u % 2, k, f * P, P),
                                rh[:, k, c0:c0 + n], rl[:, k, c0:c0 + n], k == 0, k == KD - 1)
                ins.then_inc(pj_done, 1)

            def transpose_tile(n, src):
                if n >= 2:
                    pe.wait_ge(lo_done, 2 * (n - 1))
                pe.wait_ge(h_ready, n + 1)
                for b in range(2):
                    for k in range(4):
                        ins = te.transpose(ps[:, 4 + 2 * (n % 2) + b, k * P:(k + 1) * P], src(4 * b + k), ident[:])
                    ins.then_inc(tr_done, 1)

            pe.wait_ge(consts_ready, 6)
            pe.wait_ge(rows_loaded, 48)
            pe.wait_ge(pos_ready, 1)
            te.transpose(ps[:, 3, 0:5 * KD], conv_rows[0:5 * KD, :], ident[0:5 * KD, 0:5 * KD])
            te.transpose(ps[:, 3, 64:64 + NT], pos_rows[0:NT, :], ident[0:NT, 0:NT]).then_inc(rows_tr, 1)

            def in_tile(i):
                transpose_tile(TR_IN + i, lambda k: h_in[:, i % 2, k * P:(k + 1) * P])

            for i in range(4):
                in_tile(i)
            for st in range(16):
                f, half = XBC_ORDER[st]
                if st in (0, 2):
                    pe.wait_ge(lo_done, 4 * st + 8)
                feature_step("xbc", st, oph, opl, f % 2, half * 512, 512)
                if st < 2:
                    in_tile(2 * st + 4)
                    in_tile(2 * st + 5)

            pe.wait_ge(wdt_lo, 2)
            for half in range(2):
                g = STEP0["dt"] + half
                bank_free(pe, g)
                for k in range(KD):
                    tok = slice(half * 512, (half + 1) * 512)
                    cols8 = slice(k * SSD_H, k * SSD_H + P)
                    ins = three(ps[:, g % 3, :], wdt_h[:, cols8], wdt_l[:, cols8], oph[:, k, tok], opl[:, k, tok],
                                k == 0, k == KD - 1)
                ins.then_inc(pj_done, 1)

            def dt_transpose():
                pe.wait_ge(ev["dt"], 2)
                for i in range(NT):
                    ins = te.transpose(ps[:, 3, i * SSD_H:(i + 1) * SSD_H], dt_rows[0:SSD_H, i * P:(i + 1) * P],
                                       ident[0:SSD_H, 0:SSD_H])
                ins.then_inc(dt_tr, 1)

            da = dts[1]

            def sums_of_da():
                pe.wait_ge(da_ready, 1)
                da_all = da[:].rearrange("p c h -> p (c h)")
                te.matmul(ps[:, 4, 0:64], tri[:], da_all, start=True, stop=True)
                te.matmul(ps[:, 4, 64:128], ones[:], da_all, start=True, stop=True).then_inc(cum_done, 1)

            def ssd_products(c):
                tok = slice(c * P, (c + 1) * P)
                pe.wait_ge(silu_done, KD)
                pe.wait_ge(dt_v, 3)
                if c:
                    pe.wait_ge(ssd_y, c)
                    pe.wait_ge(ssd_h, c)
                    pe.wait_ge(ssd_bcb, c)
                for k in range(4):
                    te.transpose(ps[:, 4, k * P:(k + 1) * P], mix[:, k, tok], ident[:])
                for gr in range(2):
                    te.transpose(ps[:, 5, gr * P:(gr + 1) * P], mix[:, 4 + gr, tok], ident[:])
                for gr in range(2):
                    te.matmul(ps[:, 5, (2 + gr) * P:(3 + gr) * P], mix[:, 4 + gr, tok], mix[:, 6 + gr, tok],
                              start=True, stop=True)
                for b in range(2):
                    te.matmul(ps[:, 6 + b, :], ident_b[:], mask_s[:].rearrange("p a l -> p (a l)"), start=True, stop=False)
                    for h in range(4):
                        hh = 4 * b + h
                        ins = te.matmul(ps[:, 6 + b, h * P:(h + 1) * P], da[:, c, hh:hh + 1].to_broadcast([P, P]), tri[:],
                                        start=False, stop=h == 3)
                ins.then_inc(ssd_a, 1)

            def ssd_outputs(c):
                pe.wait_ge(ssd_m, c + 1)
                pe.wait_ge(ssd_x, 3 * c + 3)
                for h in range(SSD_H):
                    te.matmul(ps[:, 4, h * 64:(h + 1) * 64], cb_decay[:, h, :], xdt[:, h * 64:(h + 1) * 64],
                              start=True, stop=True)
                for gr in range(2):
                    ins = te.matmul(ps[:, 6, gr * 256:(gr + 1) * 256], b_cb[:, gr, :], xdt_end[:, gr * 256:(gr + 1) * 256],
                                    start=True, stop=True)
                if c:
                    pe.wait_ge(ssd_h, c)
                    for gr in range(2):
                        ins = te.matmul(ps[:, 7, gr * 256:(gr + 1) * 256], mix[:, 6 + gr, c * P:(c + 1) * P],
                                        state[:, gr * 256:(gr + 1) * 256], start=True, stop=True)
                ins.then_inc(ssd_b, 1)

            def rope_transpose(n):
                pe.wait_ge(rope_done, n + 1)
                if n:
                    pe.wait_ge(rt_ev, n)
                for b in range(2):
                    ins = te.transpose(ps[:, 3, b * P:(b + 1) * P], roped[:, n % 2, b * P:(b + 1) * P], ident[:])
                ins.then_inc(rt_done, 1)

            for n in range(66):
                if n < 64:
                    name, st = STEPS[STEP0["v"] + n]
                    token_step(name, st, oph, opl, st % NT)
                if n == 0:
                    dt_transpose()
                if n == 2:
                    sums_of_da()
                if n in SSD_FIRST:
                    ssd_products(SSD_FIRST[n])
                if n in SSD_LAST:
                    ssd_outputs(SSD_LAST[n])
                if 16 <= n - 2 < 48:
                    rope_transpose(n - 18)

            steps = [(i, h) for i in range(NT) for h in range(DH)]
            NS = len(steps)
            pe.wait_ge(ev["z"], 16)
            pe.wait_ge(rt_ev, 32)
            pe.wait_ge(ev["v"], 16)

            def scores(n, c):
                i, h = steps[n]
                half = slice(64 * c, 64 * c + 64)
                if n:
                    pe.wait_ge(ex_done[c], n)
                for k0 in range(0, (i + 1) * P, 512):
                    kn = min(512, (i + 1) * P - k0)
                    diag = k0 + kn == (i + 1) * P
                    ins = te.matmul(ps[:, 2 * c + k0 // 512, 0:kn], qt[half, h, i * P:(i + 1) * P], kt[half, h, k0:k0 + kn],
                                    start=True, stop=not diag)
                    if diag:
                        ins = te.matmul(ps[:, 2 * c + k0 // 512, kn - P:kn], ident_b[:], mask_q[:], start=False, stop=True)
                ins.then_inc(s_done[c], 1)

            for n in range(NS + 2):
                if n < NS:
                    scores(n, 0)
                    scores(n, 1)
                if n >= 2:
                    k = n - 2
                    i, h = steps[k]
                    pe.wait_ge(pt_ev, k + 1)
                    if k >= 2:
                        pe.wait_ge(o_ev, k - 1)
                    for b in range(i + 1):
                        ins = te.matmul(ps[:, 6 + k % 2, 0:P], probs_t[:, k % 2, b, :], vt[:, b, h * P:(h + 1) * P],
                                        start=b == 0, stop=b == i)
                    ins.then_inc(pv_done, 1)
                if 1 <= n <= NS:
                    k = n - 1
                    i = steps[k][0]
                    pe.wait_ge(comb_done, k + 1)
                    if k:
                        pe.wait_ge(pt_ev, k)
                    for b in range(i + 1):
                        ins = te.transpose(ps[:, 4 + b // 4, (b % 4) * P:(b % 4 + 1) * P],
                                           probs[:, k % 2, 0, b * P:(b + 1) * P], ident[:])
                    ins.then_inc(pt_done, 1)

            pe.wait_ge(pt_ev, NS)
            pe.wait_ge(o_ev, NS)
            for i in range(NT):
                transpose_tile(TR_MIX + i, lambda k: mix[:, k, i * P:(i + 1) * P])
            for i in range(MT):
                transpose_tile(TR_MEM + i, lambda k: h_mem[:, i, k * P:(k + 1) * P])
            pe.wait_ge(lo_done, 2 * (TR_MEM + MT))
            for st in range(8):
                feature_step("mk", st, memh, meml, st % 2, 0, MEM)
            for st in range(8):
                token_step("mv", st, memh, meml, st % MT)

            def norm_tile(tr0, i):
                transpose_tile(tr0 + i, lambda k: h_tok[:, i % 2, k * P:(k + 1) * P])

            def out_proj(name, tr0, ready):
                for st, (u, i) in enumerate(OUT_ORDER):
                    ready(st)
                    token_step(name, st, oph, opl, i, u)
                    if st in OUT_TR:
                        norm_tile(tr0, OUT_TR[st])

            out_proj("wo", TR_Q, lambda st: None)
            for st in range(16):
                f, half = XBC_ORDER[st]
                if st in (0, 2):
                    pe.wait_ge(lo_done, 2 * (TR_Q + 2 * st + 4))
                feature_step("mq", st, oph, opl, f % 2, half * 512, 512)
                if st < 2:
                    norm_tile(TR_Q, 2 * st + 4)
                    norm_tile(TR_Q, 2 * st + 5)

            pe.wait_ge(ev["mq"], 16)
            pe.wait_ge(ev["mv"], 8)
            for n in range(NT + 2):
                if n < NT:
                    if n >= 2:
                        pe.wait_ge(mex_done, n - 1)
                    for h in range(MH):
                        for d in range(2):
                            ins = te.matmul(ps[:, 2 * (n % 2) + h // 2, (h % 2) * MEM:(h % 2 + 1) * MEM],
                                            qct[:, 2 * h + d, n * P:(n + 1) * P], kmt[:, 2 * h + d, :],
                                            start=d == 0, stop=d == 1)
                    ins.then_inc(ms_done, 1)
                if n >= 2:
                    k = n - 2
                    pe.wait_ge(mt_ev, k + 1)
                    if k:
                        pe.wait_ge(mo_lo, k)
                    for d in range(KD):
                        for m in range(MT):
                            ins = te.matmul(ps[:, 6 + d // 4, (d % 4) * P:(d % 4 + 1) * P], vm[:, m, d * P:(d + 1) * P],
                                            mprobs_t[:, k % 2, (d // 2) * MT + m, :], start=m == 0, stop=m == MT - 1)
                    ins.then_inc(mo_done, 1)
                if 1 <= n <= NT:
                    k = n - 1
                    pe.wait_ge(mn_done, k + 1)
                    if k:
                        pe.wait_ge(mt_ev, k)
                    for h in range(MH):
                        for m in range(MT):
                            b = h * MT + m
                            ins = te.transpose(ps[:, 4 + b // 4, (b % 4) * P:(b % 4 + 1) * P],
                                               mprobs[:, k % 2, h, m * P:(m + 1) * P], ident[:])
                    ins.then_inc(mt_done, 1)

            out_proj("mo", TR_MLP, lambda st: pe.wait_ge(mo_lo, st + 1) if st < NT else None)

            pe.wait_ge(lo_done, 2 * (TR_MLP + 4))
            pe.wait_ge(ev["mo"], 4 * NT)

            def up_step(st, slot):
                f, half = st % 2, st // 2
                for k in range(KD):
                    ins = three(ps[:, st, :], wcols(wh, slot, k, f * P, P), wcols(wl, slot, k, f * P, P),
                                oph[:, k, half * 512:(half + 1) * 512], opl[:, k, half * 512:(half + 1) * 512],
                                k == 0, k == KD - 1)
                ins.then_inc(up_done, 1)

            def down_step(n, par, slot, wait):
                i, ch = n // 2, n % 2
                pe.wait_ge(acc_done, wait)
                for f in range(2):
                    tok, col = slice(i * P, (i + 1) * P), slice(f * 1024 + ch * 512, f * 1024 + (ch + 1) * 512)
                    ins = three(ps[:, 4 + n % 4, :], uh[:, par, f, tok], ul[:, par, f, tok],
                                wh[:, slot, col], wl[:, slot, col], f == 0, f == 1)
                ins.then_inc(down_done, 1)

            unit_ready(N_UNITS)
            for st in range(4):
                if st == 2:
                    pe.wait_ge(lo_done, 2 * (TR_MLP + NT))
                up_step(st, 0)
                if st < 2:
                    norm_tile(TR_MLP, 2 * st + 4)
                    norm_tile(TR_MLP, 2 * st + 5)
            with pe.Fori(0, (NJ - 2) // 2) as jj:
                for r in range(2):
                    pe.wait_ge(w_lo, jj * 8 + 2 * (N_UNITS + 2 * r + 2))
                    for st in range(4):
                        pe.wait_ge(relu_done, jj * 8 + (4 * r + st + 1))
                        up_step(st, 1)
                    pe.wait_ge(w_lo, jj * 8 + 2 * (N_UNITS + 2 * r + 3))
                    pe.wait_ge(ul_done, jj * 8 + (4 * r + 4))
                    for n in range(16):
                        down_step(n, r, 0, jj * 32 + (16 * r + n + 1))
            unit_ready(N_UNITS + 2 * NJ - 3)
            for st in range(4):
                pe.wait_ge(relu_done, 4 * (NJ - 2) + st + 1)
                up_step(st, 1)
            for j, slot in ((NJ - 2, 0), (NJ - 1, 1)):
                unit_ready(N_UNITS + NJ + j)
                pe.wait_ge(ul_done, 4 * (j + 1))
                for n in range(16):
                    down_step(n, j % 2, slot, 16 * j + n + 1)


_INS = ["x", "mem", "positions", "norm_mix_pre", "norm_mix_post", "norm_mem_q", "norm_mem_kv", "norm_mem_post",
        "norm_mlp_pre", "norm_mlp_post", "w_in", "conv_w", "conv_b", "dt_bias", "a_log", "d_skip", "ssd_norm_w",
        "lambda_q1", "lambda_k1", "lambda_q2", "lambda_k2", "subln_w", "w_out", "w_mq", "w_mk", "w_mv", "w_mo",
        "w_up", "w_down"]


def kernel(**inputs):
    import numpy as _np
    import concourse.bacc as _bacc
    from concourse import mybir as _mybir
    from concourse.bass_utils import run_bass_kernel_spmd as _run

    nc = _bacc.Bacc("TRN2", target_bir_lowering=False, num_devices=1, dynamic_dma_scratch_size=1024)
    arrays, tensors = {}, {}
    for name in _INS:
        a = _np.ascontiguousarray(inputs[name])
        arrays[f"in_{name}_dram"] = a
        tensors[name] = nc.dram_tensor(f"in_{name}_dram", a.shape, _mybir.dt.from_np(a.dtype),
                                       kind="ExternalInput").ap()
    out = nc.dram_tensor("out_0_dram", (1, T, D), _mybir.dt.float32, kind="ExternalOutput").ap()
    build(nc, tensors, out)
    r = _run(nc, [arrays], core_ids=[0])
    return r.results[0]["out_0_dram"]
```

```python
import math
from contextlib import ExitStack

import concourse.bass as bass
import numpy as np
from concourse import mybir

F32 = mybir.dt.float32
F32R = mybir.dt.float32r
BF16 = mybir.dt.bfloat16
I32 = mybir.dt.int32
ALU = mybir.AluOpType
ACT = mybir.ActivationFunctionType
AX = mybir.AxisListType

P = 128
T = 1024
D = 1024
NT = T // P
KD = D // P
MEM = 256
MT = MEM // P
D_SSD = 512
XBC = 1024
SSD_H = 8
DH = 4
MH = 4
FF = 4096
EPS = 1e-6
LAMBDA_INIT = 0.8 - 0.6 * math.exp(-0.3 * 0)
THETA = 10000.0
HALF_DIM = 32
NEG = -1e30

UC = 256
UE = KD * UC
COL_Z, COL_XBC, COL_DT = 0, D_SSD, D_SSD + XBC
COL_Q = COL_DT + SSD_H
COL_K, COL_V = COL_Q + 512, COL_Q + 1024

TWO_PI_A = 6.28125
TWO_PI_B = 0.0019350051879882812
TWO_PI_C = 3.0199159795074593e-07
ROUND = 1.5 * 2.0 ** 23
PI_SAFE = 3.1415925

PROJ = [("xbc", 4, 4), ("dt", 2, 0), ("v", 8, 2), ("q", 8, 2), ("k", 8, 2), ("z", 8, 2),
        ("mk", 2, 4), ("mv", 2, 4), ("wo", 8, 4), ("mq", 4, 4), ("mo", 8, 4)]


def proj_tables():
    first, unit, steps, u = {}, {}, [], 0
    for name, per, n in PROJ:
        first[name], unit[name] = len(steps), u
        steps += [(name, s) for s in range(per * max(n, 1))]
        u += n
    return first, unit, steps, u


STEP0, UNIT0, STEPS, N_UNITS = proj_tables()
PER_UNIT = {name: per for name, per, _ in PROJ}

XBC_ORDER = [(0, 0), (1, 0), (0, 1), (1, 1)] + [(m, half) for m in range(2, KD) for half in range(2)]
MQ_ORDER = [(2 * u + f, half) for u in range(KD // 2) for half in range(2) for f in range(2)]
XBC_CONV = {2: 0, 3: 1, **{2 * m + 1: m for m in range(2, KD)}}

OUT_ORDER = ([(u, i) for u in range(2) for i in range(NT)] + [(2, 0), (2, 1), (2, 2)]
             + [x for i in range(NT - 3) for x in ((3, i), (2, i + 3))] + [(3, i) for i in range(NT - 3, NT)])
OUT_COMPLETE = [OUT_ORDER.index((3, i)) for i in range(NT)]
OUT_UNIT_END = [max(n for n, x in enumerate(OUT_ORDER) if x[0] == u) + 1 for u in range(4)]
OUT_SPLIT = {0: 2, 4: 3, 8: 4, 12: 5, 16: 6, 17: 7, OUT_UNIT_END[2]: 8, OUT_UNIT_END[2] + 1: 9}
OUT_TR = {OUT_COMPLETE[i + 2] + (i == 4): i for i in range(5)}

Y_DONE = 57

SSD_FIRST = {5 + 5 * c: c for c in range(NT)}
SSD_MID = {n + 1: c for n, c in SSD_FIRST.items()}
SSD_LAST = {n + 3: c for n, c in SSD_FIRST.items()}

TR_IN, TR_MEM, TR_MIX, TR_Q, TR_MLP = 0, 8, 10, 18, 26


def tr_bank(n):
    return 2 * (n - TR_MEM) if TR_MEM <= n < TR_MIX else 4 + 2 * (n % 2)


def cross_bank(n):
    return 2 * (n % 2) if n else 6


ATT_STEPS = ([x for a, b in ((4, 0), (5, 1)) for h in range(DH) for x in ((a, h), (b, h))]
             + [(i, h) for i in (2, 3, 6, 7) for h in range(DH)])
MIX_TILES = sorted(range(NT), key=lambda i: ATT_STEPS.index((i, DH - 1)))
O_COMPLETE = {ATT_STEPS.index((i, DH - 1)): i for i in MIX_TILES}
O_STEP = {i: n for n, i in O_COMPLETE.items()}

POWS = ([("in", i) for i in range(NT)] + [("y", i) for i in range(NT)] + [("mem", i) for i in range(MT)]
        + [("o", i) for i in MIX_TILES])
SQUARES = [x for x in POWS if x[0] != "o"]
for _a, _b in (("wo", "q"), ("mo", "mlp")):
    for _t in range(NT + 2):
        POWS += [(_b, _t - 2)] * (_t >= 2) + [(_a, _t)] * (_t < NT)
        SQUARES += [(_a, _t)] * (_t < NT) + [(_b, _t - 1)] * (1 <= _t <= NT)
POWS += [("down", i) for i in range(NT)]
SQUARES += [("down", i) for i in range(NT)]
SQ = {what: n for n, what in enumerate(SQUARES)}
POW = {what: n for n, what in enumerate(POWS)}
COL = {}
for _what in POWS:
    COL[_what] = sum(DH if x[0] == "o" else 1 for x in COL)
N_COLS = len(POWS) + NT * (DH - 1)


def build(nc, t, out):
    ctx = ExitStack()
    with ctx:
        base = (nc.sbuf_base + 63) // 64 * 64
        place = {}
        size = {"OPH": 32768, "OPL": 32768, "WH": 16384, "WL": 16384, "RAW": 8192, "X": 32768,
                "Q": 16384, "K": 16384, "V": 16384, "TMP": 16384, "GA": 4096, "GB": 4096, "MISC": 8192}
        for region, n in size.items():
            place[region] = base
            base += n
        rest = [base]

        def at(name, region, offset, shape, dt=F32):
            return nc.alloc_sbuf_tensor_at(name, shape, dt, offset=place[region] + offset)

        def small(name, shape, dt=F32):
            n = 4 if dt in (F32, F32R, I32) else 2
            for s in shape[1:]:
                n *= s
            r = nc.alloc_sbuf_tensor_at(name, shape, dt, offset=rest[0])
            rest[0] += (n + 31) // 32 * 32
            return r

        def sem(name):
            return ctx.enter_context(nc.semaphore(name))

        oph = at("oph", "OPH", 0, [P, KD, T], F32R)
        opl = at("opl", "OPL", 0, [P, KD, T], F32R)
        wh = at("wh", "WH", 0, [P, 2, UE], F32R)
        wl = at("wl", "WL", 0, [P, 2, UE], F32R)
        raw = at("raw", "RAW", 0, [P, 2, UE // 2])
        mix = at("mix", "X", 0, [P, KD, T])
        resid = at("resid", "X", 0, [P, NT, D])
        x_in = at("x_in", "V", 0, [P, 4, D])
        h_in = at("h_in", "K", 8192, [P, 2, D])
        xpre = at("xpre", "Q", 0, [P, 2, T + 4])
        rope_t = at("rope_t", "K", 0, [P, 4, NT, HALF_DIM])
        xdt = at("xdt", "TMP", 7168, [P, 512])
        xdt_end = at("xdt_end", "TMP", 9216, [P, 512])
        x_skip = at("x_skip", "TMP", 11264, [P, 512])
        b_cb = at("b_cb", "TMP", 13312, [P, 4, P])
        decay = at("decay", "GA", 0, [P, SSD_H, P])
        cb_decay = at("cb_decay", "GB", 0, [P, SSD_H, P])
        conv_rows = at("conv_rows", "TMP", 13312, [P, P])
        pos_i = at("pos_i", "TMP", 13824, [P, P], I32)
        pos_rows = at("pos_rows", "TMP", 14336, [P, P])
        state = at("state", "TMP", 0, [P, 512])
        y_off = at("y_off", "TMP", 2048, [P, 512])
        roped = at("roped", "TMP", 4096, [P, 2, UC])
        rope_b = at("rope_b", "TMP", 6144, [P, UC])
        silu_z = at("silu_z", "TMP", 7168, [P, 2, UC])
        junk = at("junk", "TMP", 9216, [P, D])
        qt = at("qt", "Q", 0, [P, DH, T])
        kt = at("kt", "K", 0, [P, DH, T])
        vt = at("vt", "V", 0, [P, NT, 512])
        probs = at("probs", "OPH", 0, [P, 2, 2, T])
        probs_t = at("probs_t", "OPH", 16384, [P, 2, NT, P])
        memh = at("memh", "TMP", 0, [P, KD, MEM], F32R)
        meml = at("meml", "MISC", 0, [P, KD, MEM], F32R)
        m_in = at("m_in", "OPL", 0, [P, 2, D])
        h_mem = at("h_mem", "OPL", 8192, [P, 2, D])
        m_junk = at("m_junk", "OPL", 16384, [P, D])
        kmt = at("kmt", "V", 0, [P, KD, MEM])
        vm = at("vm", "V", 8192, [P, MT, D])
        kmh = at("kmh", "GA", 0, [P, KD, MEM], F32R)
        kml = at("kml", "V", 0, [P, KD, MEM], F32R)
        qch = at("qch", "MISC", 0, [P, KD, P], F32R)
        qcl = at("qcl", "MISC", 4096, [P, KD, P], F32R)
        proj_out = at("proj_out", "Q", 0, [P, NT, D])
        qct = at("qct", "Q", 0, [P, KD, T])
        h_tok = at("h_tok", "TMP", 0, [P, 2, D])
        mprobs = at("mprobs", "TMP", 0, [P, 2, MH, MEM])
        mprobs_t = at("mprobs_t", "TMP", 8192, [P, 2, MH * MT, P])
        uh = at("uh", "V", 0, [P, 2, 2, T], F32R)
        ul = at("ul", "TMP", 0, [P, 2, 2, T], F32R)
        relu_u = at("relu_u", "MISC", 0, [P, 2, 512])
        sq_u = at("sq_u", "MISC", 4096, [P, 2, 512])
        junk2 = at("junk2", "MISC", 0, [P, D])
        cos_t = at("cos_t", "MISC", 0, [P, NT, HALF_DIM])
        sin_t = at("sin_t", "MISC", 1024, [P, NT, HALF_DIM])
        nsin_t = at("nsin_t", "MISC", 2048, [P, NT, HALF_DIM])
        dts = [at(f"dts{n}", "MISC", 3072 + 256 * n, [P, NT, SSD_H]) for n in range(9)]
        ncum = dts[3]
        ssd_w = at("ssd_w", "MISC", 5376, [P, 512])
        gain_a = at("gain_a", "GA", 0, [P, D])
        gain_b = at("gain_b", "GB", 0, [P, D])

        ident = small("ident", [P, P])
        tri = small("tri", [P, P])
        ones = small("ones", [P, P])
        ident_b = small("ident_b", [P, P], BF16)
        mask_q = small("mask_q", [P, P], BF16)
        mask_s = small("mask_s", [P, 4, P], BF16)
        inv = small("inv", [P, HALF_DIM])
        conv_wb = small("conv_wb", [P, 5, KD])
        wdt = at("wdt", "MISC", 7424, [P, KD, SSD_H])
        wdt_h = at("wdt_h", "K", 4096, [P, KD * SSD_H + P], F32R)
        wdt_l = at("wdt_l", "K", 5120, [P, KD * SSD_H + P], F32R)
        dt_rows = at("dt_rows", "K", 8192, [P, T])
        heads8 = small("heads8", [P, 3, SSD_H])
        lam4 = small("lam4", [P, 4, 64])
        lam = small("lam", [P, 8])
        sub_w = small("sub_w", [P, P])
        stat = small("stat", [P, N_COLS])
        rms = small("rms", [P, N_COLS])
        mhalf = small("mhalf", [P, 4])
        half_pi = small("half_pi", [P, 1])
        nmax = small("nmax", [P, 2, 2])
        sums = small("sums", [P, 4, 2])
        recs = small("recs", [P, 4, 2])
        ratio = small("ratio", [P, 2])
        mmax = small("mmax", [P, 2, MH])
        msum = small("msum", [P, 2, MH])
        mrec = small("mrec", [P, 2, MH])
        assert rest[0] <= nc.sbuf_usable_end, (rest[0], nc.sbuf_usable_end)
        ps = ctx.enter_context(nc.psum_tensor("ps", [P, 8, 512], F32))

        x_loaded = [sem(f"x_loaded{n}") for n in range(4)]
        rows_loaded, wdt_loaded, small_loaded = sem("rows_loaded"), sem("wdt_loaded"), sem("small_loaded")
        pos_ready, rows_tr = sem("pos_ready"), sem("rows_tr")
        gain_a_loaded, gain_b_loaded = sem("gain_a_loaded"), sem("gain_b_loaded")
        raw_loaded = [sem(f"raw_loaded{n}") for n in range(2)]
        w_hi, w_lo = sem("w_hi"), sem("w_lo")
        pool_c = sem("pool_c")
        consts_ready = sem("consts_ready")
        sq_done, ms_ready, rms_ready = sem("sq_done"), sem("ms_ready"), sem("rms_ready")
        h_ready = sem("h_ready")
        tr_done, hi_done, lo_done = sem("tr_done"), sem("hi_done"), sem("lo_done")
        pj_done = sem("pj_done")
        ev = {name: sem(f"ev_{name}") for name, _, _ in PROJ}
        dv = sem("dv")
        av = sem("av")
        rope_r, rope_sin = sem("rope_r"), sem("rope_sin")
        conv_done, silu_done = sem("conv_done"), sem("silu_done")
        wdt_hi, wdt_lo = sem("wdt_hi"), sem("wdt_lo")
        dt_tr = sem("dt_tr")
        dt_v, dt_s = sem("dt_v"), sem("dt_s")
        da_ready, cum_done = sem("da_ready"), sem("cum_done")
        ssd_a, ssd_b = sem("ssd_a"), sem("ssd_b")
        ssd_x, ssd_bcb, ssd_exp, ssd_m = (sem(n) for n in ("ssd_x", "ssd_bcb", "ssd_exp", "ssd_m"))
        ssd_h, ssd_y = sem("ssd_h"), sem("ssd_y")
        rope_done, rt_done, rt_ev = sem("rope_done"), sem("rt_done"), sem("rt_ev")
        gate_done, lam_s = sem("gate_done"), sem("lam_s")
        s_done = [sem(f"s_done{c}") for c in range(2)]
        mx_done = [sem(f"mx_done{c}") for c in range(2)]
        ex_done = [sem(f"ex_done{c}") for c in range(2)]
        comb_done, pt_done, pt_ev, pv_done, o_ev = (sem(n) for n in ("comb_done", "pt_done", "pt_ev", "pv_done", "o_ev"))
        resid_loaded = sem("resid_loaded")
        scaled = sem("scaled")
        resid_p, resid_v = sem("resid_p"), sem("resid_v")
        km_hi, km_lo, qc_hi, qc_lo = sem("km_hi"), sem("km_lo"), sem("qc_hi"), sem("qc_lo")
        ms_done, mmx_done, mex_done, mn_done = sem("ms_done"), sem("mmx_done"), sem("mex_done"), sem("mn_done")
        mt_done, mt_ev, mo_done, mo_hi, mo_lo = (sem(n) for n in ("mt_done", "mt_ev", "mo_done", "mo_hi", "mo_lo"))
        up_done, relu_done, sqv_done, sqh_done, ul_done = (
            sem(n) for n in ("up_done", "relu_done", "sqv_done", "sqh_done", "ul_done"))
        down_done, acc_done = sem("down_done"), sem("acc_done")
        stored = sem("stored")

        w_in = t["w_in"][0]
        cols = {"xbc": (w_in, COL_XBC), "v": (w_in, COL_V), "q": (w_in, COL_Q), "k": (w_in, COL_K),
                "z": (w_in, COL_Z), "mk": (t["w_mk"][0], 0), "mv": (t["w_mv"][0], 0),
                "wo": (t["w_out"][0], 0), "mq": (t["w_mq"][0], 0), "mo": (t["w_mo"][0], 0)}
        w_up, w_down = t["w_up"][0], t["w_down"][0]
        HALVES0 = 2 * N_UNITS
        NJ = FF // UC
        N_SMALL = 16 * 7

        def pow_cols(what, w=1):
            return stat[:, COL[what]:COL[what] + w], rms[:, COL[what]:COL[what] + w]

        def unit_source(name, u, half):
            w, c0 = cols[name]
            return w[half * 512:(half + 1) * 512, c0 + u * UC:c0 + (u + 1) * UC].rearrange("(k p) c -> p k c", p=P)

        def bank_free(eng, g):
            if g >= 3:
                name, s = STEPS[g - 3]
                eng.wait_ge(ev[name], s + 1)

        def split_at(name, s):
            if name in ("wo", "mo"):
                return [2 * UNIT0[name] + OUT_SPLIT[s]] if s in OUT_SPLIT else []
            per = PER_UNIT[name]
            u = UNIT0[name] + s // per
            r = s % per
            halves = []
            for half, when in ((0, 0), (1, per // 2)):
                if r == when:
                    halves.append(2 * (u + 1) + half)
            return [q for q in halves if u >= 1 and q < HALVES0 + 4]

        def unit_end(u):
            if u >= N_UNITS:
                m = u - N_UNITS
                if m == 0 or (m % 2 and m < 2 * NJ - 1):
                    return up_done, 4 * ((m + 1) // 2 + 1)
                return down_done, 16 * ((m - 2) // 2 + 1)
            name = [x for x, _, n in PROJ if n and UNIT0[x] <= u][-1]
            if name in ("wo", "mo"):
                return pj_done, STEP0[name] + OUT_UNIT_END[u - UNIT0[name]]
            return pj_done, STEP0[name] + (u - UNIT0[name] + 1) * PER_UNIT[name]

        BRANCH = {"wo": 0, "mo": 1, "down": 2}
        POOL_TILES = 6

        def resid_ready(eng, name, i):
            if i < POOL_TILES:
                eng.wait_ge(resid_p, POOL_TILES * BRANCH[name] + i + 1)
            else:
                eng.wait_ge(resid_v, (NT - POOL_TILES) * BRANCH[name] + i - POOL_TILES + 1)

        block = ctx.enter_context(nc.Block())

        @block.sync
        def _(sp):
            def load_half(q, src):
                if q >= 2:
                    sp.wait_ge(w_lo, q - 1)
                sp.dma_start(raw[:, q % 2, :], src).then_inc(raw_loaded[q % 2], 16)

            def x_tile(i):
                if i >= 4:
                    sp.wait_ge(h_ready, i - 3)
                sp.dma_start(x_in[:, i % 4, :], t["x"][0][i * P:(i + 1) * P, :]).then_inc(x_loaded[i % 4], 16)

            def small_inputs():
                rows = lambda a: a.partition_broadcast(P)
                sp.dma_start(wdt[:], w_in[:, COL_DT:COL_DT + SSD_H].rearrange("(k p) c -> p k c", p=P),
                             allow_slow_non_contiguous=True).then_inc(wdt_loaded, 16)
                for n, name in enumerate(("dt_bias", "a_log", "d_skip")):
                    sp.dma_start(heads8[:, n, :], rows(t[name][0:1, :])).then_inc(small_loaded, 16)
                for n, name in enumerate(("lambda_q1", "lambda_q2", "lambda_k1", "lambda_k2")):
                    sp.dma_start(lam4[:, n, :], rows(t[name][0:1, :])).then_inc(small_loaded, 16)
                sp.dma_start(ssd_w[:], rows(t["ssd_norm_w"][0:1, :])).then_inc(gain_a_loaded, 16)
                sp.dma_start(sub_w[:], rows(t["subln_w"][0:1, :])).then_inc(gain_a_loaded, 16)

            for i in range(4):
                x_tile(i)
            q = 0
            for name, _, units in PROJ:
                for u in range(units):
                    for half in range(2):
                        if q == 2:
                            for i in range(4, NT):
                                x_tile(i)
                        if q == 4:
                            small_inputs()
                        src = unit_source(name, u, half)
                        load_half(q, src)
                        q += 1
            for half in range(2):
                load_half(q, w_up[half * 512:(half + 1) * 512, 0:UC].rearrange("(k p) c -> p k c", p=P))
                q += 1
            with sp.Fori(0, NJ - 1) as j:
                for half in range(2):
                    sp.wait_ge(w_lo, j * 4 + (HALVES0 + 2 + half - 1))
                    sp.dma_start(raw[:, half, :], w_up[half * 512:(half + 1) * 512, bass.ts(j + 1, UC)]
                                 .rearrange("(k p) c -> p k c", p=P)).then_inc(raw_loaded[half], 16)
                for half in range(2):
                    sp.wait_ge(w_lo, j * 4 + (HALVES0 + 4 + half - 1))
                    sp.dma_start(raw[:, half, :], w_down[bass.ts(j * 2 + half, P), :]).then_inc(raw_loaded[half], 16)
            q += 4 * (NJ - 1)
            for half in range(2):
                load_half(q, w_down[(2 * (NJ - 1) + half) * P:(2 * (NJ - 1) + half + 1) * P, :])
                q += 1
            for i in range(NT):
                resid_ready(sp, "down", i)
                sp.dma_start(out[0][i * P:(i + 1) * P, :], resid[:, i, :]).then_inc(stored, 16)
            sp.wait_ge(stored, 16 * NT)

        @block.gpsimd
        def _(pool):
            g = nc.gpsimd
            g.memset(ident[:], 0.0).then_inc(pool_c, 1)
            g.memset(mhalf[:], -0.5).then_inc(pool_c, 1)
            pool.wait_ge(pool_c, 2)
            g.affine_select(out=ident[:], in_=ident[:], compare_op=ALU.not_equal, fill=1.0, base=0,
                            pattern=[[-1, P]], channel_multiplier=1).then_inc(consts_ready, 1)

            def constants():
                g.memset(ident_b[:], 0.0).then_inc(pool_c, 1)
                g.memset(tri[:], 1.0).then_inc(pool_c, 1)
                g.memset(mask_q[:], 0.0).then_inc(pool_c, 1)
                g.memset(mask_s[:], 0.0).then_inc(pool_c, 1)
                g.memset(ones[:], 1.0).then_inc(consts_ready, 1)
                pool.wait_ge(pool_c, 6)
                g.affine_select(out=ident_b[:], in_=ident_b[:], compare_op=ALU.not_equal, fill=1.0, base=0,
                                pattern=[[-1, P]], channel_multiplier=1).then_inc(consts_ready, 1)
                g.affine_select(out=tri[:], in_=tri[:], compare_op=ALU.is_ge, fill=0.0, base=0,
                                pattern=[[1, P]], channel_multiplier=-1).then_inc(consts_ready, 1)
                g.affine_select(out=mask_q[:], in_=mask_q[:], compare_op=ALU.is_ge, fill=NEG, base=0,
                                pattern=[[-1, P]], channel_multiplier=1).then_inc(consts_ready, 1)
                g.affine_select(out=mask_s[:], in_=mask_s[:], compare_op=ALU.is_ge, fill=NEG, base=0,
                                pattern=[[0, 4], [1, P]], channel_multiplier=-1).then_inc(consts_ready, 1)
                for i in range(HALF_DIM):
                    g.memset(inv[:, i:i + 1], float(np.float32(THETA) ** np.float32(-i / HALF_DIM))).then_inc(consts_ready, 1)
                g.memset(half_pi[:], math.pi / 2).then_inc(consts_ready, 1)
                for b in range(2):
                    g.memset(xpre[:, b, 0:3], 0.0).then_inc(consts_ready, 1)

            def pow_step(what):
                w = 4 if what[0] == "o" else 1
                pool.wait_ge(ms_ready, POW[what] + 1)
                src, dst = pow_cols(what, w)
                g.tensor_tensor(dst, src, mhalf[:, 0:w], ALU.pow).then_inc(rms_ready, 1)

            for what in POWS[:4]:
                pow_step(what)
            constants()
            def add_resid(name, i):
                pool.wait_ge(scaled, NT * BRANCH[name] + i + 1)
                pool.wait_ge(resid_loaded, 16 * NT)
                g.tensor_tensor(resid[:, i, :], resid[:, i, :], proj_out[:, i, :], ALU.add).then_inc(resid_p, 1)

            for what in POWS[4:]:
                kind, i = what
                if what == ("down", 0):
                    resid_ready(pool, "mo", POOL_TILES - 1)
                    resid_ready(pool, "mo", NT - 1)
                    g.memset(proj_out[:], 0.0).then_inc(acc_done, 4)
                if kind in ("wo", "mo") and 1 <= i <= POOL_TILES:
                    add_resid(kind, i - 1)
                pow_step(what)
                if kind == "down" and 1 <= i <= POOL_TILES:
                    add_resid("down", i - 1)

        ALL_CONSTS = 6 + HALF_DIM + 3

        @block.scalar
        def _(act):
            s = nc.scalar
            n_av = [0]

            def after(ins):
                n_av[0] += 1
                ins.then_inc(av, 1)
                act.wait_ge(av, n_av[0])

            def slot_free(u):
                if u >= 2:
                    sem_of, n = unit_end(u - 2)
                    act.wait_ge(sem_of, n)

            def split_hi(q):
                act.wait_ge(raw_loaded[q % 2], 16 * (q // 2 + 1))
                slot_free(q // 2)
                s.activation(wh[:, (q // 2) % 2, (q % 2) * 1024:(q % 2 + 1) * 1024], raw[:, q % 2, :],
                             ACT.Copy).then_inc(w_hi, 1)

            def square(what, src, dst, scale=1.0):
                if SQ[what]:
                    act.wait_ge(sq_done, SQ[what])
                s.activation(dst, src, ACT.Square, scale=scale, accum_out=stat[:, COL[what]:COL[what] + 1]).then_inc(sq_done, 1)

            def tr_hi(n, dst):
                for b in range(2):
                    act.wait_ge(tr_done, 2 * n + b + 1)
                    s.activation(dst[:, 4 * b:4 * b + 4], ps[:, tr_bank(n) + b, :].rearrange("p (k c) -> p k c", k=4),
                                 ACT.Copy).then_inc(hi_done, 1)

            rows = lambda a: a.partition_broadcast(P)
            act.dma_start(gain_b[:], rows(t["norm_mix_pre"][0:1, :])).then_inc(gain_b_loaded, 16)
            act.dma_start(pos_i[0:NT, :], t["positions"][0].rearrange("(i p) -> i p", p=P)).then_inc(rows_loaded, 16)
            act.dma_start(conv_rows[0:4 * KD, :], t["conv_w"][0, :, 0].rearrange("w (m p) -> (w m) p", p=P)
                          ).then_inc(rows_loaded, 16)
            act.dma_start(conv_rows[4 * KD:5 * KD, :], t["conv_b"][0].rearrange("(m p) -> m p", p=P)
                          ).then_inc(rows_loaded, 16)

            def in_square(i):
                act.wait_ge(x_loaded[i % 4], 16 * (i // 4 + 1))
                square(("in", i), x_in[:, i % 4, :], junk[:])

            def in_hi(i):
                tr_hi(TR_IN + i, oph[:, :, i * P:(i + 1) * P])

            for i in range(4):
                in_square(i)
                if i >= 2:
                    in_hi(i - 2)
            in_hi(2)
            split_hi(0)
            in_hi(3)
            split_hi(1)
            for i in range(4, NT):
                in_square(i)
            for i in range(4, NT):
                in_hi(i)

            act.wait_ge(rope_r, 1)
            act.wait_ge(consts_ready, ALL_CONSTS)
            s.activation(sin_t[:], rope_t[:, 0], ACT.Sin).then_inc(rope_sin, 1)
            s.activation(nsin_t[:], rope_t[:, 0], ACT.Sin, scale=-1.0).then_inc(rope_sin, 1)
            after(s.activation(rope_t[:, 1], rope_t[:, 0], ACT.Abs))
            s.activation(cos_t[:], rope_t[:, 1], ACT.Sin, scale=-1.0, bias=half_pi[:]).then_inc(rope_sin, 1)

            def silu(m):
                act.wait_ge(conv_done, m + 1)
                s.activation(mix[:, m, :], mix[:, m, :], ACT.Silu).then_inc(silu_done, 1)

            for st in range(16):
                m, half = XBC_ORDER[st]
                g = STEP0["xbc"] + st
                act.wait_ge(pj_done, g + 1)
                if m >= 2:
                    act.wait_ge(conv_done, m - 1)
                s.activation(xpre[:, m % 2, 3 + half * 512:3 + (half + 1) * 512], ps[:, g % 3, :],
                             ACT.Copy).then_inc(ev["xbc"], 1)
                if st == 0:
                    split_hi(2)
                if st == 1:
                    split_hi(3)
                if st == 8:
                    act.wait_ge(wdt_loaded, 16)
                    s.activation(wdt_h[:, 0:KD * SSD_H], wdt[:].rearrange("p k c -> p (k c)"), ACT.Copy).then_inc(wdt_hi, 1)
                    s.activation(wdt_h[:, KD * SSD_H:], ones[:], ACT.Copy).then_inc(wdt_hi, 1)
                for q in split_at("xbc", st):
                    split_hi(q)
                if st >= 4 and st % 2:
                    silu(st // 2 - 2)

            for half in range(2):
                g = STEP0["dt"] + half
                act.wait_ge(pj_done, g + 1)
                s.activation(dt_rows[0:SSD_H, half * 512:(half + 1) * 512], ps[0:SSD_H, g % 3, :], ACT.Copy).then_inc(ev["dt"], 1)
            silu(6)
            silu(7)
            act.wait_ge(small_loaded, N_SMALL)
            act.wait_ge(dt_v, 1)
            after(s.activation(dts[1][:], dts[0][:], ACT.Abs))
            s.activation(dts[2][:], dts[1][:], ACT.Exp, scale=-1.0).then_inc(dt_s, 1)
            act.wait_ge(dt_v, 2)
            s.activation(dts[4][:], dts[3][:], ACT.Ln).then_inc(dt_s, 1)
            s.activation(heads8[:, 1, :], heads8[:, 1, :], ACT.Exp).then_inc(dt_s, 1)
            act.wait_ge(lam_s, 1)
            s.activation(lam[:, 2:4], lam[:, 0:2], ACT.Exp).then_inc(dt_s, 1)

            def decays():
                act.wait_ge(dt_v, 3)
                s.activation(dts[4][:], dts[5][:], ACT.Exp).then_inc(dt_s, 1)
                s.activation(dts[7][:], dts[6][:], ACT.Exp).then_inc(dt_s, 1)
                s.activation(dts[8][:], dts[2][:], ACT.Exp).then_inc(dt_s, 1)

            def ssd_act(c):
                act.wait_ge(ssd_a, c + 1)
                if c:
                    act.wait_ge(ssd_m, c)
                    act.wait_ge(ssd_b, c)
                s.activation(b_cb[:], ps[:, 5, :].rearrange("p (k c) -> p k c", k=4), ACT.Copy).then_inc(ssd_bcb, 1)
                both = ps[:, 6:8, :].rearrange("p b (h l) -> p (b h) l", h=4)
                for h in range(SSD_H):
                    ins = s.activation(decay[:, h, :], both[:, h, :], ACT.Exp, bias=ncum[:, c, h:h + 1])
                ins.then_inc(ssd_exp, 1)

            def rope_evac(st, name):
                dst, base_n = (qt, 0) if name == "q" else (kt, 16)
                u, i = st // NT, st % NT
                act.wait_ge(rt_done, base_n + st + 1)
                s.activation(dst[:, 2 * u:2 * u + 2, i * P:(i + 1) * P],
                             ps[:, 3, 0:UC].rearrange("p (k c) -> p k c", k=2), ACT.Copy,
                             scale=0.125 if name == "q" else 1.0).then_inc(rt_ev, 1)

            for n in range(Y_DONE + NT):
                name, st = STEPS[STEP0["v"] + n] if n < 64 else (None, 0)
                g = STEP0["v"] + n
                if name == "v":
                    u, i = st // NT, st % NT
                    act.wait_ge(pj_done, g + 1)
                    s.activation(vt[:, i, u * UC:(u + 1) * UC], ps[:, g % 3, 0:UC], ACT.Copy).then_inc(ev["v"], 1)
                if name == "z":
                    act.wait_ge(pj_done, g + 1)
                    if st >= 2:
                        act.wait_ge(gate_done, st - 1)
                    elif st == 0:
                        act.wait_ge(ssd_b, NT)
                    s.activation(silu_z[:, st % 2, :], ps[:, g % 3, 0:UC], ACT.Silu).then_inc(ev["z"], 1)
                if name:
                    for q in split_at(name, st):
                        split_hi(q)
                if n == 3:
                    decays()
                if n in SSD_FIRST:
                    ssd_act(SSD_FIRST[n])
                if 16 <= n - 2 < 48:
                    rope_evac((n - 18) % 16, "q" if n - 2 < 32 else "k")
                if n >= Y_DONE:
                    i = n - Y_DONE
                    act.wait_ge(gate_done, NT + i + 1)
                    square(("y", i), mix[:, 0:4, i * P:(i + 1) * P], junk[:, 0:512].rearrange("p (k c) -> p k c", k=4))

            steps = ATT_STEPS
            NS = len(steps)

            def mem_hi(i):
                tr_hi(TR_MEM + i, memh[:, :, i * P:(i + 1) * P])

            def attn_exp(n, c):
                keys = (steps[n][0] + 1) * P
                act.wait_ge(mx_done[c], n + 1)
                if n >= 2:
                    act.wait_ge(comb_done, n - 1) if c else act.wait_ge(pt_done, n - 1)
                src = ps[:, 2 * c:2 * c + 2, :].rearrange("p b k -> p (b k)")
                s.activation(probs[:, n % 2, c, 0:keys], src[:, 0:keys], ACT.Exp, bias=nmax[:, n % 2, c:c + 1],
                             accum_out=sums[:, n % 4, c:c + 1]).then_inc(ex_done[c], 1)

            act.wait_ge(pj_done, STEP0["z"] + 16)
            for i in range(MT):
                act.dma_start(m_in[:, i, :], t["mem"][0][i * P:(i + 1) * P, :]).then_inc(x_loaded[i], 16)
            act.wait_ge(ssd_b, NT)
            act.dma_start(gain_b[:], rows(t["norm_mem_kv"][0:1, :])).then_inc(gain_b_loaded, 16)
            act.dma_start(gain_a[:], rows(t["norm_mix_post"][0:1, :])).then_inc(gain_a_loaded, 16)
            for n in range(NS + 4):
                if n < NS:
                    attn_exp(n, 0)
                    attn_exp(n, 1)
                if n in (6, 7):
                    act.wait_ge(x_loaded[n - 6], 16 * 3)
                    square(("mem", n - 6), m_in[:, n - 6, :], m_junk[:])
                if n == NS + 1:
                    mem_hi(0)
                    mem_hi(1)
                if n >= 3 and n - 3 < NS:
                    k = n - 3
                    i, h = steps[k]
                    act.wait_ge(pv_done, k + 1)
                    o = ps[:, 6 + k % 2, 0:P]
                    s.activation(mix[:, 4 + h, i * P:(i + 1) * P], o, ACT.Copy, scale=recs[:, k % 4, 0:1])
                    if k >= 4:
                        act.wait_ge(o_ev, k - 3)
                    elif k == 0:
                        act.wait_ge(sq_done, 2 * NT)
                    s.activation(junk[:, (k % 4) * P:(k % 4 + 1) * P], o, ACT.Square, scale=recs[:, k % 4, 0:1],
                                 accum_out=stat[:, COL[("o", i)] + h:COL[("o", i)] + h + 1]).then_inc(o_ev, 1)
                if n >= 1 and n - 1 < NS:
                    k = n - 1
                    i = steps[k][0]
                    act.wait_ge(pt_done, k + 1)
                    if k >= 2:
                        act.wait_ge(pv_done, k - 1)
                    src = ps[:, 4:6, :].rearrange("p b k -> p (b k)")
                    s.activation(probs_t[:, k % 2, 0:i + 1, :].rearrange("p b k -> p (b k)"), src[:, 0:(i + 1) * P],
                                 ACT.Copy).then_inc(pt_ev, 1)

            act.wait_ge(h_ready, TR_MEM + MT)
            act.dma_start(gain_b[:], rows(t["norm_mem_q"][0:1, :])).then_inc(gain_b_loaded, 16)
            for n in range(16):
                name, st = STEPS[STEP0["mk"] + n]
                g = STEP0["mk"] + n
                for q in split_at(name, st):
                    split_hi(q)
                act.wait_ge(pj_done, g + 1)
                dst = kmt[:, st, :] if name == "mk" else vm[:, st % MT, (st // MT) * UC:(st // MT + 1) * UC]
                s.activation(dst, ps[:, g % 3, 0:UC], ACT.Copy).then_inc(ev[name], 1)
                if n % 2:
                    i = MIX_TILES[n // 2]
                    tr_hi(TR_MIX + n // 2, oph[:, :, i * P:(i + 1) * P])
            for i in range(NT):
                act.dma_start(resid[:, i, :], t["x"][0][i * P:(i + 1) * P, :]).then_inc(resid_loaded, 16)

            def out_proj(name, nxt, tr0):
                def norm_hi(i):
                    tr_hi(tr0 + i, oph[:, :, i * P:(i + 1) * P])

                st = 0
                for k in range(NT + 1):
                    if k >= 3:
                        norm_hi(k - 3)
                    while k < NT and st <= OUT_COMPLETE[k]:
                        u, i = OUT_ORDER[st]
                        g = STEP0[name] + st
                        act.wait_ge(pj_done, g + 1)
                        s.activation(proj_out[:, i, u * UC:(u + 1) * UC], ps[:, g % 3, 0:UC], ACT.Copy).then_inc(ev[name], 1)
                        for q in split_at(name, st):
                            split_hi(q)
                        st += 1
                    if k < NT:
                        act.wait_ge(ev[name], st)
                        square((name, k), proj_out[:, k, :], junk[:])
                    if 1 <= k <= NT:
                        resid_ready(act, name, k - 1)
                        square((nxt, k - 1), resid[:, k - 1, :], junk[:])
                norm_hi(6)
                norm_hi(7)

            out_proj("wo", "q", TR_Q)
            def query_hi(n):
                act.wait_ge(ev["mq"], 14 if n < NT // 2 else 16)
                if n:
                    act.wait_ge(ms_done, n)
                s.activation(qch[:], qct[:, :, n * P:(n + 1) * P], ACT.Copy).then_inc(qc_hi, 1)

            def cross_exp(n):
                act.wait_ge(mmx_done, n + 1)
                if n >= 2:
                    act.wait_ge(mt_done, n - 1)
                src = ps[:, cross_bank(n):cross_bank(n) + 2, :].rearrange("p b (h m) -> p (b h) m", h=2)
                for h in range(MH):
                    ins = s.activation(mprobs[:, n % 2, h, :], src[:, h, :], ACT.Exp, bias=mmax[:, n % 2, h:h + 1],
                                       accum_out=msum[:, n % 2, h:h + 1])
                ins.then_inc(mex_done, 1)

            for st in range(16):
                f, half = MQ_ORDER[st]
                g = STEP0["mq"] + st
                if st == 4:
                    act.wait_ge(h_ready, TR_Q + NT)
                    act.wait_ge(ev["mk"], 8)
                    s.activation(kmh[:], kmt[:], ACT.Copy).then_inc(km_hi, 1)
                if st == 14:
                    query_hi(0)
                if st == 15:
                    query_hi(1)
                    cross_exp(0)
                act.wait_ge(pj_done, g + 1)
                s.activation(qct[:, f, half * 512:(half + 1) * 512], ps[:, g % 3, :], ACT.Copy,
                             scale=0.0625).then_inc(ev["mq"], 1)
                for q in split_at("mq", st):
                    split_hi(q)

            for n in range(NT + 2):
                if 1 <= n < NT:
                    if n + 1 < NT:
                        query_hi(n + 1)
                    cross_exp(n)
                if n >= 2:
                    k = n - 2
                    act.wait_ge(mo_done, k + 1)
                    s.activation(oph[:, :, k * P:(k + 1) * P], ps[:, 6:8, :].rearrange("p b (h m) -> p (b h) m", h=4),
                                 ACT.Copy).then_inc(mo_hi, 1)
                if 1 <= n <= NT:
                    k = n - 1
                    act.wait_ge(mt_done, k + 1)
                    if k >= 2:
                        act.wait_ge(mo_done, k - 1)
                    s.activation(mprobs_t[:, k % 2], ps[:, 4:6, :].rearrange("p b (h m) -> p (b h) m", h=4),
                                 ACT.Copy).then_inc(mt_ev, 1)

            act.wait_ge(ms_done, NT)
            act.dma_start(gain_a[:], rows(t["norm_mem_post"][0:1, :])).then_inc(gain_a_loaded, 16)
            act.dma_start(gain_b[:], rows(t["norm_mlp_pre"][0:1, :])).then_inc(gain_b_loaded, 16)

            out_proj("mo", "mlp", TR_MLP)
            act.wait_ge(h_ready, TR_MLP + NT)
            act.dma_start(gain_a[:], rows(t["norm_mlp_post"][0:1, :])).then_inc(gain_a_loaded, 16)

            def relu_sq(done, sq_free, st, par):
                f, half = st % 2, st // 2
                act.wait_ge(up_done, done)
                if sq_free is not None:
                    act.wait_ge(sqv_done, sq_free)
                s.activation(relu_u[:, st % 2, :], ps[:, st, :], ACT.Relu).then_inc(relu_done, 1)
                act.wait_ge(relu_done, done)
                s.activation(uh[:, par, f, half * 512:(half + 1) * 512], relu_u[:, st % 2, :],
                             ACT.Square).then_inc(sqh_done, 1)

            for half in range(2):
                split_hi(2 * (N_UNITS + 1) + half)
            for st in range(4):
                relu_sq(st + 1, st - 1 if st >= 2 else None, st, 0)
            with act.Fori(0, (NJ - 2) // 2) as jj:
                for r in range(2):
                    act.wait_ge(up_done, jj * 8 + (4 * r + 5))
                    for half in range(2):
                        act.wait_ge(raw_loaded[half], jj * 64 + 16 * (N_UNITS + 2 * r + 3))
                        s.activation(wh[:, 0, half * 1024:(half + 1) * 1024], raw[:, half, :], ACT.Copy).then_inc(w_hi, 1)
                    for st in range(4):
                        relu_sq(jj * 8 + (4 * r + st + 5), jj * 8 + (4 * r + st + 3), st, (r + 1) % 2)
                    for half in range(2):
                        act.wait_ge(raw_loaded[half], jj * 64 + 16 * (N_UNITS + 2 * r + 4))
                        s.activation(wh[:, 1, half * 1024:(half + 1) * 1024], raw[:, half, :], ACT.Copy).then_inc(w_hi, 1)
            for half in range(2):
                split_hi(2 * (N_UNITS + 2 * NJ - 2) + half)
            for st in range(4):
                relu_sq(4 * (NJ - 1) + st + 1, 4 * (NJ - 1) + st - 1, st, 1)
            for half in range(2):
                split_hi(2 * (N_UNITS + 2 * NJ - 1) + half)
            act.wait_ge(sqv_done, 4 * NJ)
            for i in range(NT):
                act.wait_ge(acc_done, 4 + 16 * (NJ - 1) + 2 * i + 2)
                square(("down", i), proj_out[:, i, :], junk2[:])

        @block.vector
        def _(dve):
            v = nc.vector
            n_dv = [0]

            def after(ins):
                n_dv[0] += 1
                ins.then_inc(dv, 1)
                dve.wait_ge(dv, n_dv[0])

            def split_lo(q):
                dve.wait_ge(w_hi, q + 1)
                part = (slice(None), (q // 2) % 2, slice((q % 2) * 1024, (q % 2 + 1) * 1024))
                v.tensor_tensor(wl[part], raw[:, q % 2, :], wh[part].bitcast(F32), ALU.subtract).then_inc(w_lo, 1)

            def mean(what, n, w=1):
                c = stat[:, COL[what]:COL[what] + w]
                v.tensor_scalar(c, c, 1.0 / n, EPS, ALU.mult, ALU.add).then_inc(ms_ready, 1)

            def squares(what):
                dve.wait_ge(sq_done, SQ[what] + 1)

            def tr_lo(n, dst_h, dst_l):
                for b in range(2):
                    dve.wait_ge(hi_done, 2 * n + b + 1)
                    v.tensor_tensor(dst_l[:, 4 * b:4 * b + 4],
                                    ps[:, tr_bank(n) + b, :].rearrange("p (k c) -> p k c", k=4),
                                    dst_h[:, 4 * b:4 * b + 4].bitcast(F32), ALU.subtract).then_inc(lo_done, 1)

            def normalise(what, n, src, gain, dst):
                dve.wait_ge(rms_ready, POW[what] + 1)
                v.scalar_tensor_tensor(dst, src, rms[:, COL[what]:COL[what] + 1], gain, ALU.mult, ALU.mult).then_inc(h_ready, 1)

            def in_mean(i):
                squares(("in", i))
                mean(("in", i), D)

            def in_norm(i):
                if i >= 2:
                    dve.wait_ge(tr_done, 2 * (i - 1))
                if i == 0:
                    dve.wait_ge(gain_b_loaded, 16)
                normalise(("in", i), i, x_in[:, i % 4, :], gain_b[:], h_in[:, i % 2, :])

            def in_lo(i):
                tr_lo(i, oph[:, :, i * P:(i + 1) * P], opl[:, :, i * P:(i + 1) * P])

            for i in range(4):
                in_mean(i)
                if i >= 1:
                    in_norm(i - 1)
                if i == 1:
                    dve.wait_ge(rows_loaded, 48)
                    v.tensor_copy(pos_rows[0:NT, :], pos_i[0:NT, :]).then_inc(pos_ready, 1)
                if i >= 2:
                    in_lo(i - 2)
            in_norm(3)
            in_lo(2)
            split_lo(0)
            in_lo(3)
            split_lo(1)
            in_mean(4)
            in_mean(5)
            in_norm(4)
            in_norm(5)
            in_mean(6)
            in_mean(7)
            for i in range(4, NT):
                in_lo(i)
                if i < 6:
                    in_norm(i + 2)

            dve.wait_ge(consts_ready, ALL_CONSTS)
            ang, turns = rope_t[:, 0], rope_t[:, 2]
            dve.wait_ge(rows_tr, 1)
            v.tensor_copy(conv_wb[:], ps[:, 3, 0:5 * KD].rearrange("p (w m) -> p w m", w=5)).then_inc(rows_tr, 1)
            after(v.tensor_tensor(ang, ps[:, 3, 64:64 + NT].unsqueeze(2).to_broadcast([P, NT, HALF_DIM]),
                                  inv[:].unsqueeze(1).to_broadcast([P, NT, HALF_DIM]), ALU.mult))
            after(v.tensor_scalar(turns, ang, 1.0 / (2 * math.pi), None, ALU.mult))
            after(v.tensor_scalar(turns, turns, ROUND, None, ALU.add))
            after(v.tensor_scalar(turns, turns, -ROUND, None, ALU.add))
            for part in (TWO_PI_A, TWO_PI_B, TWO_PI_C):
                after(v.scalar_tensor_tensor(ang, turns, -part, ang, ALU.mult, ALU.add))
            v.tensor_scalar(ang, ang, PI_SAFE, -PI_SAFE, ALU.min, ALU.max).then_inc(rope_r, 1)

            dve.wait_ge(rows_tr, 2)

            def conv(m, st):
                dve.wait_ge(ev["xbc"], st + 1)
                x = xpre[:, m % 2, :]
                after(v.tensor_scalar(mix[:, m, :], x[:, 3:3 + T], conv_wb[:, 3, m:m + 1], conv_wb[:, 4, m:m + 1], ALU.mult, ALU.add))
                for w in (2, 1):
                    after(v.scalar_tensor_tensor(mix[:, m, :], x[:, w:w + T], conv_wb[:, w, m:m + 1], mix[:, m, :],
                                                 ALU.mult, ALU.add))
                v.scalar_tensor_tensor(mix[:, m, :], x[:, 0:T], conv_wb[:, 0, m:m + 1], mix[:, m, :],
                                       ALU.mult, ALU.add).then_inc(conv_done, 1)

            for st in range(16):
                if st == 0:
                    split_lo(2)
                if st == 1:
                    split_lo(3)
                for q in split_at("xbc", st):
                    split_lo(q)
                if st == 8:
                    dve.wait_ge(wdt_hi, 2)
                    v.tensor_tensor(wdt_l[:, 0:KD * SSD_H], wdt[:].rearrange("p k c -> p (k c)"),
                                    wdt_h[:, 0:KD * SSD_H].bitcast(F32), ALU.subtract).then_inc(wdt_lo, 1)
                    v.tensor_tensor(wdt_l[:, KD * SSD_H:], ones[:], wdt_h[:, KD * SSD_H:].bitcast(F32), ALU.subtract).then_inc(wdt_lo, 1)
                if st in XBC_CONV:
                    conv(XBC_CONV[st], st)

            dve.wait_ge(small_loaded, N_SMALL)
            after(v.tensor_tensor(lam4[:, 0:2, :], lam4[:, 0:2, :], lam4[:, 2:4, :], ALU.mult))
            v.tensor_reduce(lam[:, 0:2], lam4[:, 0:2, :], AX.X, ALU.add).then_inc(lam_s, 1)
            dve.wait_ge(gain_a_loaded, 32)
            v.tensor_scalar(sub_w[:], sub_w[:], 1.0 - LAMBDA_INIT, None, ALU.mult)

            dve.wait_ge(dt_tr, 1)
            after(v.tensor_tensor(dts[0][:], ps[:, 3, 0:64].rearrange("p (c h) -> p c h", h=SSD_H),
                                  heads8[:, 0, :].unsqueeze(1).to_broadcast([P, NT, SSD_H]), ALU.add))
            v.tensor_scalar(dts[3][:], dts[0][:], 0.0, None, ALU.max).then_inc(dt_v, 1)

            dve.wait_ge(dt_s, 1)
            after(v.tensor_scalar(dts[5][:], dts[3][:], 0.0, None, ALU.add))
            after(v.tensor_scalar(dts[3][:], dts[2][:], 1.0, None, ALU.add))
            v.tensor_scalar(dts[6][:], dts[3][:], -1.0, None, ALU.add).then_inc(dt_v, 1)
            dve.wait_ge(dt_v, 2)
            after(v.tensor_scalar(dts[7][:], dts[6][:], 1e-30, None, ALU.max))
            after(v.reciprocal(dts[7][:], dts[7][:]))
            after(v.tensor_tensor(dts[7][:], dts[7][:], dts[2][:], ALU.mult))
            dve.wait_ge(dt_s, 3)
            after(v.tensor_tensor(dts[7][:], dts[7][:], dts[4][:], ALU.mult))
            after(v.scalar_tensor_tensor(dts[8][:], dts[6][:], 0.0, dts[2][:], ALU.is_equal, ALU.mult))
            after(v.tensor_tensor(dts[7][:], dts[7][:], dts[8][:], ALU.add))
            after(v.tensor_tensor(dts[0][:], dts[7][:], dts[5][:], ALU.add))
            v.scalar_tensor_tensor(dts[1][:], dts[0][:], -1.0,
                                   heads8[:, 1, :].unsqueeze(1).to_broadcast([P, NT, SSD_H]),
                                   ALU.mult, ALU.mult).then_inc(da_ready, 1)
            dve.wait_ge(cum_done, 1)
            cum, end = dts[5], dts[6]
            v.tensor_copy(cum[:], ps[:, 4, 0:64].rearrange("p (c h) -> p c h", h=SSD_H)).then_inc(dv, 1)
            v.tensor_copy(end[:], ps[:, 4, 64:128].rearrange("p (c h) -> p c h", h=SSD_H)).then_inc(dv, 1)
            n_dv[0] += 2
            dve.wait_ge(dv, n_dv[0])
            after(v.tensor_scalar(ncum[:], cum[:], -1.0, None, ALU.mult))
            v.tensor_tensor(dts[2][:], end[:], cum[:], ALU.subtract).then_inc(dt_v, 1)
            dve.wait_ge(dt_s, 7)
            after(v.tensor_tensor(lam[:, 4:5], lam[:, 3:4], lam[:, 2:3], ALU.subtract))
            after(v.tensor_scalar(lam[:, 4:5], lam[:, 4:5], -LAMBDA_INIT, None, ALU.add))
            dt, e_cum, e_end, dt_end = dts[0], dts[4], dts[7], dts[2]
            after(v.tensor_tensor(dt_end[:], dt[:], dts[8][:], ALU.mult))

            def heads(a):
                return a.rearrange("p (h c) -> p h c", h=SSD_H)

            def spread(a, c):
                return a[:, c, :].unsqueeze(2).to_broadcast([P, SSD_H, 64])

            def ssd_first(c):
                dve.wait_ge(ssd_a, c + 1)
                if c:
                    dve.wait_ge(ssd_b, c)
                xs = heads(ps[:, 4, :])
                v.tensor_tensor(heads(xdt[:]), xs, spread(dt, c), ALU.mult).then_inc(ssd_x, 1)
                v.tensor_tensor(heads(xdt_end[:]), xs, spread(dt_end, c), ALU.mult).then_inc(ssd_x, 1)
                v.tensor_tensor(heads(x_skip[:]), xs, heads8[:, 2, :].unsqueeze(2).to_broadcast([P, SSD_H, 64]),
                                ALU.mult).then_inc(ssd_x, 1)

            def ssd_mid(c):
                dve.wait_ge(ssd_exp, c + 1)
                dve.wait_ge(ssd_bcb, c + 1)
                for gr in range(2):
                    ins = v.tensor_tensor(cb_decay[:, 4 * gr:4 * gr + 4, :], decay[:, 4 * gr:4 * gr + 4, :],
                                          b_cb[:, 2 + gr, :].unsqueeze(1).to_broadcast([P, 4, P]), ALU.mult)
                ins.then_inc(ssd_m, 1)

            def ssd_last(c):
                dve.wait_ge(ssd_b, c + 1)
                if c:
                    after(v.tensor_tensor(heads(y_off[:]), heads(ps[:, 7, :]), spread(e_cum, c), ALU.mult))
                    after(v.tensor_tensor(x_skip[:], x_skip[:], y_off[:], ALU.add))
                    after(v.tensor_tensor(heads(state[:]), heads(state[:]), spread(e_end, c), ALU.mult))
                    v.tensor_tensor(state[:], state[:], ps[:, 6, :], ALU.add).then_inc(ssd_h, 1)
                else:
                    v.tensor_copy(state[:], ps[:, 6, :]).then_inc(ssd_h, 1)
                dve.wait_ge(ssd_x, 3 * c + 3)
                v.tensor_tensor(mix[:, 0:4, c * P:(c + 1) * P], ps[:, 4, :].rearrange("p (k c) -> p k c", k=4),
                                x_skip[:].rearrange("p (k c) -> p k c", k=4), ALU.add).then_inc(ssd_y, 1)

            def rope(st, name, g):
                i = st % NT
                n = st + (16 if name == "k" else 0)
                dve.wait_ge(pj_done, g + 1)
                if n == 0:
                    dve.wait_ge(rope_sin, 3)
                if n >= 2:
                    dve.wait_ge(rt_done, n - 1)
                src = ps[:, g % 3, 0:UC].rearrange("p (a h c) -> p a h c", a=4, h=2)
                dst = roped[:, n % 2, :].rearrange("p (a h c) -> p a h c", a=4, h=2)
                tmp = rope_b[:].rearrange("p (a h c) -> p a h c", a=4, h=2)
                spread_t = lambda tab: tab[:, i, :].unsqueeze(1).to_broadcast([P, 4, HALF_DIM])
                for h in range(2):
                    v.tensor_tensor(dst[:, :, h, :], src[:, :, h, :], spread_t(cos_t), ALU.mult)
                if n:
                    dve.wait_ge(rope_done, n)
                v.tensor_tensor(tmp[:, :, 0, :], src[:, :, 1, :], spread_t(nsin_t), ALU.mult)
                v.tensor_tensor(tmp[:, :, 1, :], src[:, :, 0, :], spread_t(sin_t), ALU.mult).then_inc(ev[name], 1)
                dve.wait_ge(ev[name], st + 1)
                v.tensor_tensor(roped[:, n % 2, :], roped[:, n % 2, :], rope_b[:], ALU.add).then_inc(rope_done, 1)

            def y_mean(i):
                squares(("y", i))
                mean(("y", i), D_SSD)

            def y_norm(i):
                dve.wait_ge(rms_ready, POW[("y", i)] + 1)
                y = mix[:, 0:4, i * P:(i + 1) * P]
                v.scalar_tensor_tensor(y, y, rms[:, COL[("y", i)]:COL[("y", i)] + 1], ssd_w[:].rearrange("p (k c) -> p k c", k=4),
                                       ALU.mult, ALU.mult)

            for n in range(64):
                name, st = STEPS[STEP0["v"] + n]
                if name in ("q", "k"):
                    rope(st, name, STEP0["v"] + n)
                if name == "z":
                    u, i = st // NT, st % NT
                    dve.wait_ge(ev["z"], st + 1)
                    if st == 0:
                        dve.wait_ge(ssd_y, NT)
                    y = mix[:, 2 * u:2 * u + 2, i * P:(i + 1) * P]
                    v.tensor_tensor(y, y, silu_z[:, st % 2, :].rearrange("p (k c) -> p k c", k=2), ALU.mult).then_inc(gate_done, 1)
                for q in split_at(name, st):
                    split_lo(q)
                if n in SSD_FIRST:
                    ssd_first(SSD_FIRST[n])
                if n in SSD_MID:
                    ssd_mid(SSD_MID[n])
                if n in SSD_LAST:
                    ssd_last(SSD_LAST[n])
                if n >= Y_DONE + 2:
                    y_norm(n - Y_DONE - 2)
                if n >= Y_DONE + 1:
                    y_mean(n - Y_DONE - 1)

            steps = ATT_STEPS
            NS = len(steps)

            def attn_max(n, c):
                keys = (steps[n][0] + 1) * P
                dve.wait_ge(s_done[c], n + 1)
                if n >= 2:
                    dve.wait_ge(ex_done[c], n - 1)
                src = ps[:, 2 * c:2 * c + 2, :].rearrange("p b k -> p (b k)")
                v.tensor_reduce(nmax[:, n % 2, c:c + 1], src[:, 0:keys], AX.X, ALU.max, negate=True).then_inc(mx_done[c], 1)

            def attn_comb(n):
                keys = (steps[n][0] + 1) * P
                dve.wait_ge(ex_done[0], n + 1)
                dve.wait_ge(ex_done[1], n + 1)
                if n >= 4:
                    dve.wait_ge(o_ev, n - 3)
                after(v.reciprocal(recs[:, n % 4, :], sums[:, n % 4, :]))
                after(v.scalar_tensor_tensor(ratio[:, n % 2:n % 2 + 1], sums[:, n % 4, 0:1], recs[:, n % 4, 1:2],
                                             lam[:, 4:5], ALU.mult, ALU.mult))
                v.scalar_tensor_tensor(probs[:, n % 2, 0, 0:keys], probs[:, n % 2, 1, 0:keys], ratio[:, n % 2:n % 2 + 1],
                                       probs[:, n % 2, 0, 0:keys], ALU.mult, ALU.add).then_inc(comb_done, 1)

            def o_mean(i):
                dve.wait_ge(o_ev, O_STEP[i] + 1)
                mean(("o", i), P, DH)

            def o_norm(i):
                dve.wait_ge(rms_ready, POW[("o", i)] + 1)
                for h in range(DH):
                    o = mix[:, 4 + h, i * P:(i + 1) * P]
                    ins = v.scalar_tensor_tensor(o, o, rms[:, COL[("o", i)] + h:COL[("o", i)] + h + 1], sub_w[:], ALU.mult, ALU.mult)
                ins.then_inc(h_ready, 1)

            for n in range(NS + 7):
                if 1 <= n <= NS:
                    attn_comb(n - 1)
                if n < NS:
                    attn_max(n, 0)
                    attn_max(n, 1)
                if n < 3:
                    y_norm(5 + n)
                if n < 2:
                    y_mean(6 + n)
                if n == NS + 2:
                    for i in range(MT):
                        tr_lo(TR_MEM + i, memh[:, :, i * P:(i + 1) * P], meml[:, :, i * P:(i + 1) * P])
                if n == 8:
                    for i in range(MT):
                        squares(("mem", i))
                        mean(("mem", i), D)
                if n == 9:
                    dve.wait_ge(gain_b_loaded, 32)
                    for i in range(MT):
                        normalise(("mem", i), TR_MEM + i, m_in[:, i, :], gain_b[:], h_mem[:, i, :])
                if n - 7 in O_COMPLETE:
                    o_norm(O_COMPLETE[n - 7])
                if n - 6 in O_COMPLETE:
                    o_mean(O_COMPLETE[n - 6])
            for n in range(16):
                name, st = STEPS[STEP0["mk"] + n]
                for q in split_at(name, st):
                    split_lo(q)
                if n % 2:
                    i = MIX_TILES[n // 2]
                    tr_lo(TR_MIX + n // 2, oph[:, :, i * P:(i + 1) * P], opl[:, :, i * P:(i + 1) * P])

            def scale_branch(name, i):
                dve.wait_ge(rms_ready, POW[(name, i)] + 1)
                v.scalar_tensor_tensor(proj_out[:, i, :], proj_out[:, i, :], rms[:, COL[(name, i)]:COL[(name, i)] + 1],
                                       gain_a[:], ALU.mult, ALU.mult).then_inc(scaled, 1)

            def add_branch(name, i):
                if i >= POOL_TILES:
                    dve.wait_ge(scaled, NT * BRANCH[name] + i + 1)
                    v.tensor_tensor(resid[:, i, :], resid[:, i, :], proj_out[:, i, :], ALU.add).then_inc(resid_v, 1)

            def out_proj(name, nxt, tr0):
                def norm(i):
                    if i >= 2:
                        dve.wait_ge(tr_done, 2 * (tr0 + i - 1))
                    resid_ready(dve, name, i)
                    normalise((nxt, i), tr0 + i, resid[:, i, :], gain_b[:], h_tok[:, i % 2, :])

                def norm_lo(i):
                    tr_lo(tr0 + i, oph[:, :, i * P:(i + 1) * P], opl[:, :, i * P:(i + 1) * P])

                st = 0
                for k in range(NT + 2):
                    if k >= 2:
                        squares((nxt, k - 2))
                        mean((nxt, k - 2), D)
                    if k == 1:
                        dve.wait_ge(gain_a_loaded, 48 if name == "wo" else 64)
                        dve.wait_ge(gain_b_loaded, 48 if name == "wo" else 64)
                        dve.wait_ge(resid_loaded, 16 * NT)
                    if 1 <= k <= NT:
                        scale_branch(name, k - 1)
                        add_branch(name, k - 1)
                    if k >= 2:
                        norm(k - 2)
                    if k >= 3:
                        norm_lo(k - 3)
                    while k < NT and st <= OUT_COMPLETE[k]:
                        for q in split_at(name, st):
                            split_lo(q)
                        st += 1
                    if k < NT:
                        squares((name, k))
                        mean((name, k), D)
                norm_lo(7)

            out_proj("wo", "q", TR_Q)
            def query_lo(n):
                dve.wait_ge(qc_hi, n + 1)
                if n:
                    dve.wait_ge(ms_done, n)
                v.tensor_tensor(qcl[:], qct[:, :, n * P:(n + 1) * P], qch[:].bitcast(F32), ALU.subtract).then_inc(qc_lo, 1)

            for st in range(16):
                if st == 6:
                    dve.wait_ge(km_hi, 1)
                    v.tensor_tensor(kml[:], kmt[:], kmh[:].bitcast(F32), ALU.subtract).then_inc(km_lo, 1)
                if st == 14:
                    query_lo(0)
                for q in split_at("mq", st):
                    split_lo(q)

            for n in range(NT + 3):
                if n >= 3:
                    k = n - 3
                    dve.wait_ge(mo_hi, k + 1)
                    v.tensor_tensor(opl[:, :, k * P:(k + 1) * P], ps[:, 6:8, :].rearrange("p b (h m) -> p (b h) m", h=4),
                                    oph[:, :, k * P:(k + 1) * P].bitcast(F32), ALU.subtract).then_inc(mo_lo, 1)
                if 1 <= n <= NT:
                    k = n - 1
                    dve.wait_ge(mex_done, k + 1)
                    after(v.reciprocal(mrec[:, k % 2, :], msum[:, k % 2, :]))
                    v.tensor_tensor(mprobs[:, k % 2], mprobs[:, k % 2],
                                    mrec[:, k % 2, :].unsqueeze(2).to_broadcast([P, MH, MEM]), ALU.mult).then_inc(mn_done, 1)
                if n < NT:
                    dve.wait_ge(ms_done, n + 1)
                    if n >= 2:
                        dve.wait_ge(mex_done, n - 1)
                    src = ps[:, cross_bank(n):cross_bank(n) + 2, :].rearrange("p b (h m) -> p (b h) m", h=2)
                    v.tensor_reduce(mmax[:, n % 2, :], src, AX.X, ALU.max, negate=True).then_inc(mmx_done, 1)
                if n + 1 < NT:
                    query_lo(n + 1)

            out_proj("mo", "mlp", TR_MLP)

            for half in range(2):
                split_lo(2 * (N_UNITS + 1) + half)

            def square_lo(j4, par, st):
                f, half = st % 2, st // 2
                dve.wait_ge(relu_done, j4 + (st + 1))
                v.tensor_tensor(sq_u[:, st % 2, :], relu_u[:, st % 2, :], relu_u[:, st % 2, :], ALU.mult).then_inc(sqv_done, 1)
                dve.wait_ge(sqv_done, j4 + (st + 1))
                dve.wait_ge(sqh_done, j4 + (st + 1))
                part = (slice(None), par, f, slice(half * 512, (half + 1) * 512))
                v.tensor_tensor(ul[part], sq_u[:, st % 2, :], uh[part].bitcast(F32), ALU.subtract).then_inc(ul_done, 1)

            def add_down(j16, n):
                i, ch = n // 2, n % 2
                dve.wait_ge(down_done, j16 + (n + 1))
                a = proj_out[:, i, ch * 512:(ch + 1) * 512]
                v.tensor_tensor(a, a, ps[:, 4 + n % 4, :], ALU.add).then_inc(acc_done, 1)

            def split_lo_mlp(count, slot, half):
                dve.wait_ge(w_hi, count)
                part = (slice(None), slot, slice(half * 1024, (half + 1) * 1024))
                v.tensor_tensor(wl[part], raw[:, half, :], wh[part].bitcast(F32), ALU.subtract).then_inc(w_lo, 1)

            for st in range(4):
                square_lo(0, 0, st)
            dve.wait_ge(acc_done, 4)
            with dve.Fori(0, (NJ - 2) // 2) as jj:
                for r in range(2):
                    for half in range(2):
                        split_lo_mlp(jj * 8 + (2 * (N_UNITS + 2 * r + 2) + half + 1), 0, half)
                    for st in range(4):
                        square_lo(jj * 8 + 4 * (r + 1), (r + 1) % 2, st)
                    for n in range(4):
                        add_down(jj * 32 + 16 * r, n)
                    for half in range(2):
                        split_lo_mlp(jj * 8 + (2 * (N_UNITS + 2 * r + 3) + half + 1), 1, half)
                    for n in range(4, 16):
                        add_down(jj * 32 + 16 * r, n)
            split_lo(2 * (N_UNITS + 2 * NJ - 2))
            split_lo(2 * (N_UNITS + 2 * NJ - 2) + 1)
            for st in range(4):
                square_lo(4 * (NJ - 1), 1, st)
            for n in range(4):
                add_down(16 * (NJ - 2), n)
            split_lo(2 * (N_UNITS + 2 * NJ - 1))
            split_lo(2 * (N_UNITS + 2 * NJ - 1) + 1)
            for n in range(4, 16):
                add_down(16 * (NJ - 2), n)
            for n in range(16):
                add_down(16 * (NJ - 1), n)
                if n == 0:
                    dve.wait_ge(gain_a_loaded, 80)
                if n % 2 and n >= 3:
                    i = n // 2 - 1
                    squares(("down", i))
                    mean(("down", i), D)
                    if i >= 1:
                        scale_branch("down", i - 1)
            scale_branch("down", NT - 2)
            squares(("down", NT - 1))
            mean(("down", NT - 1), D)
            add_branch("down", NT - 2)
            scale_branch("down", NT - 1)
            add_branch("down", NT - 1)

        @block.tensor
        def _(pe):
            te = nc.tensor

            def three(o, lh, ll, rh, rl, first, last):
                te.matmul(o, lh, rh, start=first, stop=False)
                te.matmul(o, lh, rl, start=False, stop=False)
                return te.matmul(o, ll, rh, start=False, stop=last)

            def wcols(w, slot, k, c0=0, n=UC):
                return w[:, slot, k * UC + c0:k * UC + c0 + n]

            def unit_ready(u):
                pe.wait_ge(w_lo, 2 * u + 2)

            def token_step(name, st, lh, ll, tile, unit=None):
                g, u = STEP0[name] + st, UNIT0[name] + (st // PER_UNIT[name] if unit is None else unit)
                bank_free(pe, g)
                unit_ready(u)
                for k in range(KD):
                    ins = three(ps[:, g % 3, 0:UC], lh[:, k, tile * P:(tile + 1) * P], ll[:, k, tile * P:(tile + 1) * P],
                                wcols(wh, u % 2, k), wcols(wl, u % 2, k), k == 0, k == KD - 1)
                ins.then_inc(pj_done, 1)

            def feature_step(name, st, rh, rl, f, c0, n):
                per = PER_UNIT[name]
                g, u = STEP0[name] + st, UNIT0[name] + st // per
                bank_free(pe, g)
                unit_ready(u)
                for k in range(KD):
                    ins = three(ps[:, g % 3, 0:n], wcols(wh, u % 2, k, f * P, P), wcols(wl, u % 2, k, f * P, P),
                                rh[:, k, c0:c0 + n], rl[:, k, c0:c0 + n], k == 0, k == KD - 1)
                ins.then_inc(pj_done, 1)

            def transpose_tile(n, src):
                if n >= 2:
                    pe.wait_ge(lo_done, 2 * (n - 1))
                pe.wait_ge(h_ready, n + 1)
                for b in range(2):
                    for k in range(4):
                        ins = te.transpose(ps[:, tr_bank(n) + b, k * P:(k + 1) * P], src(4 * b + k), ident[:])
                    ins.then_inc(tr_done, 1)

            pe.wait_ge(consts_ready, 1)

            def in_tile(i):
                transpose_tile(TR_IN + i, lambda k: h_in[:, i % 2, k * P:(k + 1) * P])

            in_tile(0)
            in_tile(1)
            pe.wait_ge(rows_loaded, 48)
            pe.wait_ge(pos_ready, 1)
            te.transpose(ps[:, 3, 0:5 * KD], conv_rows[0:5 * KD, :], ident[0:5 * KD, 0:5 * KD])
            te.transpose(ps[:, 3, 64:64 + NT], pos_rows[0:NT, :], ident[0:NT, 0:NT]).then_inc(rows_tr, 1)
            in_tile(2)
            in_tile(3)
            for st in range(16):
                f, half = XBC_ORDER[st]
                if st in (0, 2):
                    pe.wait_ge(lo_done, 4 * st + 8)
                feature_step("xbc", st, oph, opl, f % 2, half * 512, 512)
                if st < 2:
                    in_tile(2 * st + 4)
                    in_tile(2 * st + 5)

            pe.wait_ge(wdt_lo, 2)
            for half in range(2):
                g = STEP0["dt"] + half
                bank_free(pe, g)
                for k in range(KD):
                    tok = slice(half * 512, (half + 1) * 512)
                    cols8 = slice(k * SSD_H, k * SSD_H + P)
                    ins = three(ps[:, g % 3, :], wdt_h[:, cols8], wdt_l[:, cols8], oph[:, k, tok], opl[:, k, tok],
                                k == 0, k == KD - 1)
                ins.then_inc(pj_done, 1)

            def dt_transpose():
                pe.wait_ge(ev["dt"], 2)
                for i in range(NT):
                    ins = te.transpose(ps[:, 3, i * SSD_H:(i + 1) * SSD_H], dt_rows[0:SSD_H, i * P:(i + 1) * P],
                                       ident[0:SSD_H, 0:SSD_H])
                ins.then_inc(dt_tr, 1)

            da = dts[1]

            def sums_of_da():
                pe.wait_ge(consts_ready, ALL_CONSTS)
                pe.wait_ge(da_ready, 1)
                da_all = da[:].rearrange("p c h -> p (c h)")
                te.matmul(ps[:, 4, 0:64], tri[:], da_all, start=True, stop=True)
                te.matmul(ps[:, 4, 64:128], ones[:], da_all, start=True, stop=True).then_inc(cum_done, 1)

            def ssd_products(c):
                tok = slice(c * P, (c + 1) * P)
                pe.wait_ge(silu_done, KD)
                pe.wait_ge(dt_v, 3)
                if c:
                    pe.wait_ge(ssd_y, c)
                    pe.wait_ge(ssd_h, c)
                    pe.wait_ge(ssd_bcb, c)
                for k in range(4):
                    te.transpose(ps[:, 4, k * P:(k + 1) * P], mix[:, k, tok], ident[:])
                for gr in range(2):
                    te.transpose(ps[:, 5, gr * P:(gr + 1) * P], mix[:, 4 + gr, tok], ident[:])
                for gr in range(2):
                    te.matmul(ps[:, 5, (2 + gr) * P:(3 + gr) * P], mix[:, 4 + gr, tok], mix[:, 6 + gr, tok],
                              start=True, stop=True)
                for b in range(2):
                    te.matmul(ps[:, 6 + b, :], ident_b[:], mask_s[:].rearrange("p a l -> p (a l)"), start=True, stop=False)
                    for h in range(4):
                        hh = 4 * b + h
                        ins = te.matmul(ps[:, 6 + b, h * P:(h + 1) * P], da[:, c, hh:hh + 1].to_broadcast([P, P]), tri[:],
                                        start=False, stop=h == 3)
                ins.then_inc(ssd_a, 1)

            def ssd_outputs(c):
                pe.wait_ge(ssd_m, c + 1)
                pe.wait_ge(ssd_x, 3 * c + 3)
                for h in range(SSD_H):
                    te.matmul(ps[:, 4, h * 64:(h + 1) * 64], cb_decay[:, h, :], xdt[:, h * 64:(h + 1) * 64],
                              start=True, stop=True)
                for gr in range(2):
                    ins = te.matmul(ps[:, 6, gr * 256:(gr + 1) * 256], b_cb[:, gr, :], xdt_end[:, gr * 256:(gr + 1) * 256],
                                    start=True, stop=True)
                if c:
                    pe.wait_ge(ssd_h, c)
                    for gr in range(2):
                        ins = te.matmul(ps[:, 7, gr * 256:(gr + 1) * 256], mix[:, 6 + gr, c * P:(c + 1) * P],
                                        state[:, gr * 256:(gr + 1) * 256], start=True, stop=True)
                ins.then_inc(ssd_b, 1)

            def rope_transpose(n):
                pe.wait_ge(rope_done, n + 1)
                if n:
                    pe.wait_ge(rt_ev, n)
                for b in range(2):
                    ins = te.transpose(ps[:, 3, b * P:(b + 1) * P], roped[:, n % 2, b * P:(b + 1) * P], ident[:])
                ins.then_inc(rt_done, 1)

            for n in range(66):
                if n < 64:
                    name, st = STEPS[STEP0["v"] + n]
                    token_step(name, st, oph, opl, st % NT)
                if n == 0:
                    dt_transpose()
                if n == 3:
                    sums_of_da()
                if n in SSD_FIRST:
                    ssd_products(SSD_FIRST[n])
                if n in SSD_LAST:
                    ssd_outputs(SSD_LAST[n])
                if 16 <= n - 2 < 48:
                    rope_transpose(n - 18)

            steps = ATT_STEPS
            NS = len(steps)
            pe.wait_ge(ev["z"], 16)
            pe.wait_ge(rt_ev, 32)
            pe.wait_ge(ev["v"], 16)

            def scores(n, c):
                i, h = steps[n]
                half = slice(64 * c, 64 * c + 64)
                if n:
                    pe.wait_ge(ex_done[c], n)
                for k0 in range(0, (i + 1) * P, 512):
                    kn = min(512, (i + 1) * P - k0)
                    diag = k0 + kn == (i + 1) * P
                    ins = te.matmul(ps[:, 2 * c + k0 // 512, 0:kn], qt[half, h, i * P:(i + 1) * P], kt[half, h, k0:k0 + kn],
                                    start=True, stop=not diag)
                    if diag:
                        ins = te.matmul(ps[:, 2 * c + k0 // 512, kn - P:kn], ident_b[:], mask_q[:], start=False, stop=True)
                ins.then_inc(s_done[c], 1)

            def mem_tile(i):
                pe.wait_ge(ex_done[0], NS)
                pe.wait_ge(ex_done[1], NS)
                transpose_tile(TR_MEM + i, lambda k: h_mem[:, i, k * P:(k + 1) * P])

            for n in range(NS + 3):
                if n < NS:
                    scores(n, 0)
                    scores(n, 1)
                if n == NS + 1:
                    mem_tile(1)
                if n >= 3:
                    k = n - 3
                    i, h = steps[k]
                    pe.wait_ge(pt_ev, k + 1)
                    if k >= 2:
                        pe.wait_ge(o_ev, k - 1)
                    for b in range(i + 1):
                        ins = te.matmul(ps[:, 6 + k % 2, 0:P], probs_t[:, k % 2, b, :], vt[:, b, h * P:(h + 1) * P],
                                        start=b == 0, stop=b == i)
                    ins.then_inc(pv_done, 1)
                if n == NS:
                    mem_tile(0)
                if 1 <= n <= NS:
                    k = n - 1
                    i = steps[k][0]
                    pe.wait_ge(comb_done, k + 1)
                    if k:
                        pe.wait_ge(pt_ev, k)
                    for b in range(i + 1):
                        ins = te.transpose(ps[:, 4 + b // 4, (b % 4) * P:(b % 4 + 1) * P],
                                           probs[:, k % 2, 0, b * P:(b + 1) * P], ident[:])
                    ins.then_inc(pt_done, 1)

            pe.wait_ge(pt_ev, NS)
            pe.wait_ge(o_ev, NS)
            pe.wait_ge(lo_done, 2 * (TR_MEM + MT))
            for n in range(16):
                name, st = STEPS[STEP0["mk"] + n]
                if name == "mk":
                    feature_step("mk", st, memh, meml, st % 2, 0, MEM)
                else:
                    token_step("mv", st, memh, meml, st % MT)
                if n % 2:
                    i = MIX_TILES[n // 2]
                    transpose_tile(TR_MIX + n // 2, lambda k: mix[:, k, i * P:(i + 1) * P])

            def norm_tile(tr0, i):
                transpose_tile(tr0 + i, lambda k: h_tok[:, i % 2, k * P:(k + 1) * P])

            def out_proj(name, tr0, ready, done=0):
                for st, (u, i) in enumerate(OUT_ORDER):
                    if st < done:
                        continue
                    ready(st)
                    token_step(name, st, oph, opl, i, u)
                    if st in OUT_TR:
                        norm_tile(tr0, OUT_TR[st])

            def cross_scores(n):
                pe.wait_ge(km_lo, 1)
                pe.wait_ge(qc_lo, n + 1)
                if n >= 2:
                    pe.wait_ge(mex_done, n - 1)
                for h in range(MH):
                    for d in (2 * h, 2 * h + 1):
                        ins = three(ps[:, cross_bank(n) + h // 2, (h % 2) * MEM:(h % 2 + 1) * MEM],
                                    qch[:, d, :], qcl[:, d, :], kmh[:, d, :], kml[:, d, :], d % 2 == 0, d % 2 == 1)
                ins.then_inc(ms_done, 1)

            out_proj("wo", TR_Q, lambda st: pe.wait_ge(lo_done, 2 * (TR_MIX + MIX_TILES.index(st) + 1)) if st < NT else None)
            for st in range(16):
                f, half = MQ_ORDER[st]
                if st == 15:
                    cross_scores(0)
                if st in (0, 2):
                    pe.wait_ge(lo_done, 2 * (TR_Q + 2 * st + 4))
                feature_step("mq", st, oph, opl, f % 2, half * 512, 512)
                if st == 0:
                    norm_tile(TR_Q, 5)
                if st == 1:
                    norm_tile(TR_Q, 6)
                    norm_tile(TR_Q, 7)

            pe.wait_ge(ev["mq"], 16)
            pe.wait_ge(ev["mv"], 8)

            def first_mo_step(st):
                pe.wait_ge(mo_lo, st + 1)
                token_step("mo", st, oph, opl, st, 0)

            for n in range(NT + 2):
                if 1 <= n < NT:
                    cross_scores(n)
                if n == NT + 1:
                    first_mo_step(1)
                if n >= 2:
                    k = n - 2
                    pe.wait_ge(mt_ev, k + 1)
                    if k:
                        pe.wait_ge(mo_lo, k)
                    for d in range(KD):
                        for m in range(MT):
                            ins = te.matmul(ps[:, 6 + d // 4, (d % 4) * P:(d % 4 + 1) * P], vm[:, m, d * P:(d + 1) * P],
                                            mprobs_t[:, k % 2, (d // 2) * MT + m, :], start=m == 0, stop=m == MT - 1)
                    ins.then_inc(mo_done, 1)
                if n == NT:
                    pe.wait_ge(mex_done, NT)
                    first_mo_step(0)
                if 1 <= n <= NT:
                    k = n - 1
                    pe.wait_ge(mn_done, k + 1)
                    if k:
                        pe.wait_ge(mt_ev, k)
                    for h in range(MH):
                        for m in range(MT):
                            b = h * MT + m
                            ins = te.transpose(ps[:, 4 + b // 4, (b % 4) * P:(b % 4 + 1) * P],
                                               mprobs[:, k % 2, h, m * P:(m + 1) * P], ident[:])
                    ins.then_inc(mt_done, 1)

            out_proj("mo", TR_MLP, lambda st: pe.wait_ge(mo_lo, st + 1) if st < NT else None, done=2)

            pe.wait_ge(lo_done, 2 * (TR_MLP + 4))
            pe.wait_ge(ev["mo"], 4 * NT)

            def up_step(st, slot):
                f, half = st % 2, st // 2
                for k in range(KD):
                    ins = three(ps[:, st, :], wcols(wh, slot, k, f * P, P), wcols(wl, slot, k, f * P, P),
                                oph[:, k, half * 512:(half + 1) * 512], opl[:, k, half * 512:(half + 1) * 512],
                                k == 0, k == KD - 1)
                ins.then_inc(up_done, 1)

            def down_step(n, par, slot, wait):
                i, ch = n // 2, n % 2
                pe.wait_ge(acc_done, wait)
                for f in range(2):
                    tok, col = slice(i * P, (i + 1) * P), slice(f * 1024 + ch * 512, f * 1024 + (ch + 1) * 512)
                    ins = three(ps[:, 4 + n % 4, :], uh[:, par, f, tok], ul[:, par, f, tok],
                                wh[:, slot, col], wl[:, slot, col], f == 0, f == 1)
                ins.then_inc(down_done, 1)

            unit_ready(N_UNITS)
            for st in range(4):
                if st == 2:
                    pe.wait_ge(lo_done, 2 * (TR_MLP + NT))
                up_step(st, 0)
                if st == 0:
                    norm_tile(TR_MLP, 5)
                if st == 1:
                    norm_tile(TR_MLP, 6)
                    norm_tile(TR_MLP, 7)
            with pe.Fori(0, (NJ - 2) // 2) as jj:
                for r in range(2):
                    pe.wait_ge(w_lo, jj * 8 + 2 * (N_UNITS + 2 * r + 2))
                    for st in range(4):
                        pe.wait_ge(relu_done, jj * 8 + (4 * r + st + 1))
                        up_step(st, 1)
                    pe.wait_ge(w_lo, jj * 8 + 2 * (N_UNITS + 2 * r + 3))
                    pe.wait_ge(ul_done, jj * 8 + (4 * r + 4))
                    for n in range(16):
                        down_step(n, r, 0, jj * 32 + (16 * r + n + 1))
            unit_ready(N_UNITS + 2 * NJ - 3)
            for st in range(4):
                pe.wait_ge(relu_done, 4 * (NJ - 2) + st + 1)
                up_step(st, 1)
            for j, slot in ((NJ - 2, 0), (NJ - 1, 1)):
                unit_ready(N_UNITS + NJ + j)
                pe.wait_ge(ul_done, 4 * (j + 1))
                for n in range(16):
                    down_step(n, j % 2, slot, 16 * j + n + 1)


_INS = ["x", "mem", "positions", "norm_mix_pre", "norm_mix_post", "norm_mem_q", "norm_mem_kv", "norm_mem_post",
        "norm_mlp_pre", "norm_mlp_post", "w_in", "conv_w", "conv_b", "dt_bias", "a_log", "d_skip", "ssd_norm_w",
        "lambda_q1", "lambda_k1", "lambda_q2", "lambda_k2", "subln_w", "w_out", "w_mq", "w_mk", "w_mv", "w_mo",
        "w_up", "w_down"]


def kernel(**inputs):
    import numpy as _np
    import concourse.bacc as _bacc
    from concourse import mybir as _mybir
    from concourse.bass_utils import run_bass_kernel_spmd as _run

    nc = _bacc.Bacc("TRN2", target_bir_lowering=False, num_devices=1, dynamic_dma_scratch_size=1024)
    arrays, tensors = {}, {}
    for name in _INS:
        a = _np.ascontiguousarray(inputs[name])
        arrays[f"in_{name}_dram"] = a
        tensors[name] = nc.dram_tensor(f"in_{name}_dram", a.shape, _mybir.dt.from_np(a.dtype),
                                       kind="ExternalInput").ap()
    out = nc.dram_tensor("out_0_dram", (1, T, D), _mybir.dt.float32, kind="ExternalOutput").ap()
    build(nc, tensors, out)
    r = _run(nc, [arrays], core_ids=[0])
    return r.results[0]["out_0_dram"]
```
